# Optimizing a Trainium2 kernel written in Bass

```python
import math
import jax, jax.numpy as jnp
from jax import lax
import numpy as np

D_MODEL = 1024
BATCH = 1
SEQ = 256
DEPTH = 2

N_MIXERS = 4
N_HEADS = 8
HEAD_DIM = D_MODEL // N_HEADS
ROPE_THETA = 10000.0
Q_BLOCK = 128
HG_CHUNK = 64
DA_HALF = HEAD_DIM // 2
NSA_GROUPS = 2
NSA_HPG = N_HEADS // NSA_GROUPS
CMP_BLOCK = 32
CMP_STRIDE = 16
SLC_BLOCK = 64
SLC_TOPK = 16
WINDOW = 512
NSA_Q_BLOCK = 64
D_FF = 2816
N_EXPERTS = 8
TOP_K = 2
D_FF_EXPERT = 3584
MOE_BLOCK = 128
LN_EPS = 1e-5
NEG = -1e30
FORCE = 1e9
DEEPNORM_ALPHA = (2 * DEPTH) ** 0.25
DEEPNORM_BETA = (8 * DEPTH) ** -0.25


def layer_norm(x, g, b):
    xf = x.astype(jnp.float32)
    mu = jnp.mean(xf, axis=-1, keepdims=True)
    xc = xf - mu
    var = jnp.mean(xc * xc, axis=-1, keepdims=True)
    return (xc * lax.rsqrt(var + LN_EPS) * g.astype(jnp.float32) + b.astype(jnp.float32)).astype(x.dtype)

def rms_norm(x, g):
    xf = x.astype(jnp.float32)
    return xf * lax.rsqrt(jnp.mean(xf * xf, axis=-1, keepdims=True) + LN_EPS) * g.astype(jnp.float32)

def rope(x, pos):
    d = x.shape[-1]
    half = d // 2
    inv = ROPE_THETA ** (-jnp.arange(half, dtype=jnp.float32) / half)
    ang = pos.astype(jnp.float32)[:, None] * inv[None, :]
    shp = (1, x.shape[1]) + (1,) * (x.ndim - 3) + (half,)
    cos = jnp.cos(ang).reshape(shp)
    sin = jnp.sin(ang).reshape(shp)
    xf = x.astype(jnp.float32)
    x1, x2 = xf[..., :half], xf[..., half:]
    return jnp.concatenate([x1 * cos - x2 * sin, x2 * cos + x1 * sin], axis=-1).astype(x.dtype)

def masked_softmax(s, mask):
    s = jnp.where(mask, s.astype(jnp.float32), NEG)
    p = jax.nn.softmax(s, axis=-1)
    return jnp.where(mask, p, 0.0)

def hgrn2_mixer(h, w_in, lb_logits, norm_g, w_out, layer):
    b, s, _ = h.shape
    nh, dk = N_HEADS, HEAD_DIM
    c = HG_CHUNK
    nc = s // c
    q, f, i, g = jnp.split(h @ w_in, 4, axis=-1)
    lb = jnp.cumsum(jax.nn.softmax(lb_logits.astype(jnp.float32), axis=0), axis=0)[layer]
    forget = lb + (1.0 - lb) * jax.nn.sigmoid(f.astype(jnp.float32))
    log_f = jnp.log(forget)
    k = 1.0 - forget
    q = jax.nn.silu(q.astype(jnp.float32))
    v = i.astype(jnp.float32)

    def to_chunks(t):
        return t.reshape(b, nc, c, nh, dk).transpose(1, 0, 3, 2, 4)

    tri = jnp.tril(jnp.ones((c, c), bool))[:, :, None]

    def step(state, inp):
        qc, kc, vc, lf = inp
        cum = jnp.cumsum(lf, axis=2)
        rel = jnp.where(tri, cum[:, :, :, None, :] - cum[:, :, None, :, :], -jnp.inf)
        scores = jnp.einsum('bhtd,bhsd,bhtsd->bhts', qc, kc, jnp.exp(rel))
        out = scores @ vc + jnp.einsum('bhtd,bhdv->bhtv', qc * jnp.exp(cum), state)
        last = cum[:, :, -1:, :]
        new_state = jnp.exp(last[:, :, 0, :, None]) * state + jnp.einsum('bhsd,bhsv->bhdv', kc * jnp.exp(last - cum), vc)
        return new_state, out

    state0 = jnp.zeros((b, nh, dk, dk), jnp.float32)
    _, o = lax.scan(step, state0, (to_chunks(q), to_chunks(k), to_chunks(v), to_chunks(log_f)))
    o = o.transpose(1, 0, 3, 2, 4).reshape(b, s, nh, dk)
    o = rms_norm(o, norm_g) * jax.nn.sigmoid(g.astype(jnp.float32)).reshape(b, s, nh, dk)
    return o.reshape(b, s, D_MODEL).astype(h.dtype) @ w_out

def diff_attention_mixer(h, w_in, lam, norm_g, w_out, pos, layer):
    b, s, _ = h.shape
    q, k, v = jnp.split(h @ w_in, 3, axis=-1)
    q = rope(q.reshape(b, s, N_HEADS, 2, DA_HALF), pos).transpose(0, 2, 3, 1, 4)
    k = rope(k.reshape(b, s, N_HEADS, 2, DA_HALF), pos).transpose(0, 2, 3, 1, 4)
    v = v.reshape(b, s, N_HEADS, HEAD_DIM).transpose(0, 2, 1, 3)
    lam_init = 0.8 - 0.6 * math.exp(-0.3 * layer)
    lf = lam.astype(jnp.float32)
    lmb = jnp.exp(jnp.sum(lf[0] * lf[1])) - jnp.exp(jnp.sum(lf[2] * lf[3])) + lam_init
    kpos = jnp.arange(s)
    scale = DA_HALF ** -0.5

    def block(bi):
        s0 = bi * Q_BLOCK
        qb = lax.dynamic_slice_in_dim(q, s0, Q_BLOCK, axis=3)
        sc = jnp.einsum('bhcqd,bhckd->bhcqk', qb, k).astype(jnp.float32) * scale
        mask = (s0 + jnp.arange(Q_BLOCK))[:, None] >= kpos[None, :]
        p = masked_softmax(sc, mask)
        attn = p[:, :, 0] - lmb * p[:, :, 1]
        return jnp.einsum('bhqk,bhkd->bqhd', attn.astype(v.dtype), v)

    o = lax.map(block, jnp.arange(s // Q_BLOCK))
    o = o.transpose(1, 0, 2, 3, 4).reshape(b, s, N_HEADS, HEAD_DIM)
    o = rms_norm(o, norm_g) * (1.0 - lam_init)
    return o.reshape(b, s, D_MODEL).astype(h.dtype) @ w_out

def nsa_mixer(h, w_in, cmp_pe, cmp_w1, cmp_w2, w_out, pos):
    b, s, _ = h.shape
    G, HG, dk = NSA_GROUPS, NSA_HPG, HEAD_DIM
    proj = h @ w_in
    q, kv, gates = jnp.split(proj, [D_MODEL, D_MODEL + 6 * G * dk], axis=-1)
    q = q.reshape(b, s, N_HEADS, dk)
    kv = kv.reshape(b, s, 6, G, dk)
    k_cmp, v_cmp, k_slc, v_slc, k_win, v_win = [kv[:, :, j] for j in range(6)]
    gates = jax.nn.sigmoid(gates.astype(jnp.float32)).reshape(b, s, N_HEADS, 3)
    q_rot = rope(q, pos)
    k_slc = rope(k_slc, pos)
    k_win = rope(k_win, pos)

    n_cmp = (s - CMP_BLOCK) // CMP_STRIDE + 1
    tok_idx = np.arange(n_cmp)[:, None] * CMP_STRIDE + np.arange(CMP_BLOCK)[None, :]

    def compress(t, j):
        blk = t[:, tok_idx] + cmp_pe[j][None, None, :, None, :]
        blk = blk.transpose(0, 3, 1, 2, 4).reshape(b, G, n_cmp, CMP_BLOCK * dk)
        return jax.nn.gelu(blk @ cmp_w1[j]) @ cmp_w2[j]

    kc = compress(k_cmp, 0)
    vc = compress(v_cmp, 1)
    cmp_end = jnp.asarray(np.arange(n_cmp) * CMP_STRIDE + CMP_BLOCK - 1)
    n_slc = s // SLC_BLOCK
    cs = np.arange(n_cmp) * CMP_STRIDE
    ss_ = np.arange(n_slc) * SLC_BLOCK
    ov = np.clip(np.minimum(cs[:, None] + CMP_BLOCK, ss_[None, :] + SLC_BLOCK) - np.maximum(cs[:, None], ss_[None, :]), 0, None) / CMP_BLOCK
    cmp_to_slc = jnp.asarray(ov, jnp.float32)
    n_sel = min(SLC_TOPK, n_slc)
    ks_blk = k_slc.transpose(0, 2, 1, 3).reshape(b, G, n_slc, SLC_BLOCK * dk)
    vs_blk = v_slc.transpose(0, 2, 1, 3).reshape(b, G, n_slc, SLC_BLOCK * dk)
    kw = jnp.pad(k_win.transpose(0, 2, 1, 3), ((0, 0), (0, 0), (WINDOW, 0), (0, 0)))
    vw = jnp.pad(v_win.transpose(0, 2, 1, 3), ((0, 0), (0, 0), (WINDOW, 0), (0, 0)))
    qg = q.reshape(b, s, G, HG, dk).transpose(0, 2, 3, 1, 4)
    qrg = q_rot.reshape(b, s, G, HG, dk).transpose(0, 2, 3, 1, 4)
    scale = dk ** -0.5
    blk_id = jnp.arange(n_slc)
    qb_n = NSA_Q_BLOCK

    def block(bi):
        s0 = bi * qb_n
        tq = s0 + jnp.arange(qb_n)
        qb = lax.dynamic_slice_in_dim(qg, s0, qb_n, axis=3)
        qrb = lax.dynamic_slice_in_dim(qrg, s0, qb_n, axis=3)
        sc = jnp.einsum('bgiqd,bgcd->bgiqc', qb, kc).astype(jnp.float32) * scale
        pc = masked_softmax(sc, cmp_end[None, :] <= tq[:, None])
        o_cmp = jnp.einsum('bgiqc,bgcd->bgiqd', pc.astype(vc.dtype), vc)
        imp = jnp.einsum('bgqc,cn->bgqn', pc.sum(axis=2), cmp_to_slc)
        cur = tq // SLC_BLOCK
        forced = (blk_id[None, :] == 0) | (blk_id[None, :] == cur[:, None]) | (blk_id[None, :] == cur[:, None] - 1)
        imp = jnp.where(forced, FORCE, imp)
        imp = jnp.where(blk_id[None, :] <= cur[:, None], imp, NEG)
        top_s, top_i = lax.top_k(imp, n_sel)
        sel_ok = top_s > 0.5 * NEG
        gidx = top_i.reshape(b, G, qb_n * n_sel, 1)
        kg = jnp.take_along_axis(ks_blk, gidx, axis=2).reshape(b, G, qb_n, n_sel * SLC_BLOCK, dk)
        vg = jnp.take_along_axis(vs_blk, gidx, axis=2).reshape(b, G, qb_n, n_sel * SLC_BLOCK, dk)
        tok = top_i[..., None] * SLC_BLOCK + jnp.arange(SLC_BLOCK)
        ms = (sel_ok[..., None] & (tok <= tq[None, None, :, None, None])).reshape(b, G, 1, qb_n, n_sel * SLC_BLOCK)
        sg = jnp.einsum('bgiqd,bgqmd->bgiqm', qrb, kg).astype(jnp.float32) * scale
        ps = masked_softmax(sg, ms)
        o_slc = jnp.einsum('bgiqm,bgqmd->bgiqd', ps.astype(vg.dtype), vg)
        kwb = lax.dynamic_slice_in_dim(kw, s0, qb_n + WINDOW, axis=2)
        vwb = lax.dynamic_slice_in_dim(vw, s0, qb_n + WINDOW, axis=2)
        kp = s0 - WINDOW + jnp.arange(qb_n + WINDOW)
        mw = (kp[None, :] <= tq[:, None]) & (kp[None, :] > tq[:, None] - WINDOW) & (kp[None, :] >= 0)
        sw = jnp.einsum('bgiqd,bgkd->bgiqk', qrb, kwb).astype(jnp.float32) * scale
        pw = masked_softmax(sw, mw)
        o_win = jnp.einsum('bgiqk,bgkd->bgiqd', pw.astype(vwb.dtype), vwb)
        o = jnp.stack([o_cmp, o_slc, o_win], axis=-2)
        return o.transpose(0, 3, 1, 2, 4, 5).reshape(b, qb_n, N_HEADS, 3, dk)

    o = lax.map(block, jnp.arange(s // qb_n))
    o = o.transpose(1, 0, 2, 3, 4, 5).reshape(b, s, N_HEADS, 3, dk)
    o = jnp.einsum('bshc,bshcd->bshd', gates.astype(o.dtype), o)
    return o.reshape(b, s, D_MODEL) @ w_out

def stick_breaking_mixer(h, w_in, w_out):
    b, s, _ = h.shape
    q, k, v = jnp.split(h @ w_in, 3, axis=-1)
    q = q.reshape(b, s, N_HEADS, HEAD_DIM).transpose(0, 2, 1, 3)
    k = k.reshape(b, s, N_HEADS, HEAD_DIM).transpose(0, 2, 1, 3)
    v = v.reshape(b, s, N_HEADS, HEAD_DIM).transpose(0, 2, 1, 3)
    kpos = jnp.arange(s)
    scale = HEAD_DIM ** -0.5

    def block(bi):
        s0 = bi * Q_BLOCK
        qb = lax.dynamic_slice_in_dim(q, s0, Q_BLOCK, axis=2)
        z = jnp.einsum('bhqd,bhkd->bhqk', qb, k).astype(jnp.float32) * scale
        tq = s0 + jnp.arange(Q_BLOCK)
        strict = kpos[None, :] < tq[:, None]
        log_keep = jnp.where(strict, jax.nn.log_sigmoid(-z), 0.0)
        after = lax.cumsum(log_keep, axis=3, reverse=True) - log_keep
        a = jnp.where(strict, jnp.exp(jax.nn.log_sigmoid(z) + after), 0.0)
        return jnp.einsum('bhqk,bhkd->bqhd', a.astype(v.dtype), v)

    o = lax.map(block, jnp.arange(s // Q_BLOCK))
    o = o.transpose(1, 0, 2, 3, 4).reshape(b, s, D_MODEL)
    return o @ w_out

def swiglu(h, w_gate, w_up, w_down):
    return (jax.nn.silu(h @ w_gate) * (h @ w_up)) @ w_down

def moe_swiglu(h, w_router, w_gate, w_up, w_down):
    b, s, d = h.shape
    t = b * s
    hf = h.reshape(t, d)
    logits = (hf @ w_router).astype(jnp.float32)
    top_val, top_idx = lax.top_k(logits, TOP_K)
    gates = jax.nn.softmax(top_val, axis=-1)
    n_assign = t * TOP_K
    flat_e = top_idx.reshape(n_assign)
    flat_tok = jnp.repeat(jnp.arange(t, dtype=jnp.int32), TOP_K)
    order = jnp.argsort(flat_e)
    sorted_e = flat_e[order]
    sorted_tok = flat_tok[order]
    counts = jnp.bincount(flat_e, length=N_EXPERTS)
    padded = (counts + MOE_BLOCK - 1) // MOE_BLOCK * MOE_BLOCK
    pad_end = jnp.cumsum(padded)
    pad_start = pad_end - padded
    grp_start = jnp.cumsum(counts) - counts
    dest = (pad_start[sorted_e] + jnp.arange(n_assign) - grp_start[sorted_e]).astype(jnp.int32)
    n_blocks = -(-n_assign // MOE_BLOCK) + N_EXPERTS
    n_slots = n_blocks * MOE_BLOCK
    slot_tok = jnp.zeros((n_slots,), jnp.int32).at[dest].set(sorted_tok)
    block_e = jnp.minimum(jnp.searchsorted(pad_end, jnp.arange(n_blocks) * MOE_BLOCK, side='right'), N_EXPERTS - 1)
    xs = hf[slot_tok].reshape(n_blocks, MOE_BLOCK, d)

    def expert_block(args):
        xb, e = args
        return (jax.nn.silu(xb @ w_gate[e]) * (xb @ w_up[e])) @ w_down[e]

    ys = lax.map(expert_block, (xs, block_e)).reshape(n_slots, d)
    slot_of_assign = jnp.zeros((n_assign,), jnp.int32).at[order].set(dest)
    y = ys[slot_of_assign].reshape(t, TOP_K, d)
    out = jnp.einsum('tk,tkd->td', gates.astype(y.dtype), y)
    return out.reshape(b, s, d)

def first_inputs(seed: int = 0) -> dict:
    key = jax.random.key(seed)
    ks = jax.random.split(key, 25)
    D = D_MODEL
    f32 = jnp.float32

    def nrm(k, shape, scale):
        return jax.random.normal(k, shape, f32) * scale

    nsa_in = D + 6 * NSA_GROUPS * HEAD_DIM + 3 * N_HEADS
    out_scale = DEEPNORM_BETA * D ** -0.5
    return {
        'x': nrm(ks[0], (BATCH, SEQ, D), 1.0),
        'hg_w_in': nrm(ks[1], (D, 4 * D), D ** -0.5),
        'hg_lb': nrm(ks[2], (DEPTH + 1, D), 0.1),
        'hg_norm_g': 1.0 + nrm(ks[3], (HEAD_DIM,), 0.01),
        'hg_w_out': nrm(ks[4], (D, D), out_scale),
        'da_w_in': nrm(ks[5], (D, 3 * D), D ** -0.5),
        'da_lam': nrm(ks[6], (4, DA_HALF), 0.1),
        'da_norm_g': 1.0 + nrm(ks[7], (HEAD_DIM,), 0.01),
        'da_w_out': nrm(ks[8], (D, D), out_scale),
        'nsa_w_in': nrm(ks[9], (D, nsa_in), D ** -0.5),
        'nsa_cmp_pe': nrm(ks[10], (2, CMP_BLOCK, HEAD_DIM), 0.02),
        'nsa_cmp_w1': nrm(ks[11], (2, CMP_BLOCK * HEAD_DIM, HEAD_DIM), (CMP_BLOCK * HEAD_DIM) ** -0.5),
        'nsa_cmp_w2': nrm(ks[12], (2, HEAD_DIM, HEAD_DIM), HEAD_DIM ** -0.5),
        'nsa_w_out': nrm(ks[13], (D, D), out_scale),
        'sb_w_in': nrm(ks[14], (D, 3 * D), D ** -0.5),
        'sb_w_out': nrm(ks[15], (D, D), out_scale),
        'ffn_w_gate': nrm(ks[16], (DEPTH // 2, D, D_FF), D ** -0.5),
        'ffn_w_up': nrm(ks[17], (DEPTH // 2, D, D_FF), D ** -0.5),
        'ffn_w_down': nrm(ks[18], (DEPTH // 2, D_FF, D), DEEPNORM_BETA * D_FF ** -0.5),
        'moe_w_router': nrm(ks[19], (DEPTH // 2, D, N_EXPERTS), D ** -0.5),
        'moe_w_gate': nrm(ks[20], (DEPTH // 2, N_EXPERTS, D, D_FF_EXPERT), D ** -0.5),
        'moe_w_up': nrm(ks[21], (DEPTH // 2, N_EXPERTS, D, D_FF_EXPERT), D ** -0.5),
        'moe_w_down': nrm(ks[22], (DEPTH // 2, N_EXPERTS, D_FF_EXPERT, D), DEEPNORM_BETA * D_FF_EXPERT ** -0.5),
        'ln_g': 1.0 + nrm(ks[23], (DEPTH, 2, D), 0.01),
        'ln_b': nrm(ks[24], (DEPTH, 2, D), 0.01),
    }

def first_block(x, hg_w_in, hg_lb, hg_norm_g, hg_w_out, da_w_in, da_lam, da_norm_g, da_w_out,
              nsa_w_in, nsa_cmp_pe, nsa_cmp_w1, nsa_cmp_w2, nsa_w_out, sb_w_in, sb_w_out,
              ffn_w_gate, ffn_w_up, ffn_w_down, moe_w_router, moe_w_gate, moe_w_up, moe_w_down,
              ln_g, ln_b):
    pos = jnp.arange(x.shape[1])
    h = x
    for layer in range(DEPTH):
        m = layer % N_MIXERS
        if m == 0:
            y = hgrn2_mixer(h, hg_w_in, hg_lb, hg_norm_g, hg_w_out, layer)
        elif m == 1:
            y = diff_attention_mixer(h, da_w_in, da_lam, da_norm_g, da_w_out, pos, layer)
        elif m == 2:
            y = nsa_mixer(h, nsa_w_in, nsa_cmp_pe, nsa_cmp_w1, nsa_cmp_w2, nsa_w_out, pos)
        else:
            y = stick_breaking_mixer(h, sb_w_in, sb_w_out)
        h = layer_norm(DEEPNORM_ALPHA * h + y.astype(h.dtype), ln_g[layer, 0], ln_b[layer, 0])
        j = layer // 2
        if layer % 2 == 0:
            y = swiglu(h, ffn_w_gate[j], ffn_w_up[j], ffn_w_down[j])
        else:
            y = moe_swiglu(h, moe_w_router[j], moe_w_gate[j], moe_w_up[j], moe_w_down[j])
        h = layer_norm(DEEPNORM_ALPHA * h + y.astype(h.dtype), ln_g[layer, 1], ln_b[layer, 1])
    return h


N_A_LAYERS = DEPTH // 2
N_B_LAYERS = DEPTH - N_A_LAYERS
CONV_WIDTH = 31
N_HEADS_2 = 16
HEAD_DIM_2 = D_MODEL // N_HEADS_2
D_FF_2 = 4 * D_MODEL
D_PLE = 256
EPS = 1e-6
NEG_BIG = -1e30


def rmsnorm(x, g):
    xf = x.astype(jnp.float32)
    y = xf * lax.rsqrt(jnp.mean(xf * xf, axis=-1, keepdims=True) + EPS)
    return (y * g.astype(jnp.float32)).astype(x.dtype)

def layernorm(x, g, b):
    xf = x.astype(jnp.float32)
    mu = jnp.mean(xf, axis=-1, keepdims=True)
    xc = xf - mu
    var = jnp.mean(xc * xc, axis=-1, keepdims=True)
    y = xc * lax.rsqrt(var + EPS)
    return (y * g.astype(jnp.float32) + b.astype(jnp.float32)).astype(x.dtype)

def conformer_conv(hn, w_pw1, b_pw1, w_dw, b_dw, ln_g, ln_b, w_pw2, b_pw2):
    u = hn @ w_pw1 + b_pw1
    a, g = jnp.split(u, 2, axis=-1)
    u = a * jax.nn.sigmoid(g)
    kern = w_dw[:, None, :].astype(u.dtype)
    u = lax.conv_general_dilated(
        u, kern, window_strides=(1,), padding=((CONV_WIDTH - 1, 0),),
        dimension_numbers=("NWC", "WIO", "NWC"),
        feature_group_count=D_MODEL) + b_dw
    u = layernorm(u, ln_g, ln_b)
    u = jax.nn.silu(u)
    return u @ w_pw2 + b_pw2

def shared_kv(h, kv_norm, w_kvf, b_f):
    B, S, _ = h.shape
    u = rmsnorm(h, kv_norm) @ w_kvf
    k = u[..., :D_MODEL].reshape(B, S, N_HEADS_2, HEAD_DIM_2)
    v = u[..., D_MODEL:2 * D_MODEL].reshape(B, S, N_HEADS_2, HEAD_DIM_2)
    f_logit = (u[..., 2 * D_MODEL:] + b_f).astype(jnp.float32)
    log_f = jax.nn.log_sigmoid(f_logit)
    c = jnp.cumsum(log_f, axis=1)
    return k, v, jnp.transpose(c, (0, 2, 1))

def fox_attention(hn, w_q, w_o, k, v, c_bhs):
    B, S, _ = hn.shape
    nb = S // Q_BLOCK
    q = (hn @ w_q).reshape(B, S, N_HEADS_2, HEAD_DIM_2) * (HEAD_DIM_2 ** -0.5)
    qb = jnp.transpose(q.reshape(B, nb, Q_BLOCK, N_HEADS_2, HEAD_DIM_2), (1, 0, 2, 3, 4))
    cb = jnp.transpose(c_bhs.reshape(B, N_HEADS_2, nb, Q_BLOCK), (2, 0, 1, 3))
    k_pos = jnp.arange(S)

    def one_block(args):
        q_blk, c_blk, i = args
        s = jnp.einsum("bqhd,bkhd->bhqk", q_blk, k,
                       preferred_element_type=jnp.float32)
        bias = c_blk[:, :, :, None] - c_bhs[:, :, None, :]
        q_pos = i * Q_BLOCK + jnp.arange(Q_BLOCK)
        causal = k_pos[None, :] <= q_pos[:, None]
        s = jnp.where(causal, s + bias, NEG_BIG)
        pr = jax.nn.softmax(s, axis=-1)
        return jnp.einsum("bhqk,bkhd->bqhd", pr.astype(v.dtype), v)

    o = lax.map(one_block, (qb, cb, jnp.arange(nb)))
    o = jnp.transpose(o, (1, 0, 2, 3, 4)).reshape(B, S, D_MODEL)
    return o @ w_o

def second_inputs(seed: int = 0) -> dict:
    key = jax.random.key(seed)
    ks = jax.random.split(key, 32)
    f32 = jnp.float32
    nrm = lambda k, shape, scale: (jax.random.normal(k, shape, f32) * scale)
    gain = lambda k, shape: 1.0 + 0.05 * jax.random.normal(k, shape, f32)
    D = D_MODEL
    x = jax.random.normal(ks[0], (BATCH, SEQ, D), f32)
    p = jax.random.normal(ks[1], (DEPTH, BATCH, SEQ, D_PLE), f32)
    mix_norm = gain(ks[2], (DEPTH, D))
    conv_w_pw1 = nrm(ks[3], (N_A_LAYERS, D, 2 * D), D ** -0.5)
    conv_b_pw1 = nrm(ks[4], (N_A_LAYERS, 2 * D), 0.02)
    conv_w_dw = nrm(ks[5], (N_A_LAYERS, CONV_WIDTH, D), CONV_WIDTH ** -0.5)
    conv_b_dw = nrm(ks[6], (N_A_LAYERS, D), 0.02)
    conv_ln_g = gain(ks[7], (N_A_LAYERS, D))
    conv_ln_b = nrm(ks[8], (N_A_LAYERS, D), 0.02)
    conv_w_pw2 = nrm(ks[9], (N_A_LAYERS, D, D), 0.5 * D ** -0.5)
    conv_b_pw2 = nrm(ks[10], (N_A_LAYERS, D), 0.02)
    kv_norm = gain(ks[11], (D,))
    w_kvf = jnp.concatenate([
        nrm(ks[12], (D, 2 * D), D ** -0.5),
        nrm(ks[13], (D, N_HEADS_2), 0.1 * D ** -0.5),
    ], axis=1)
    b_f = jax.random.uniform(ks[14], (N_HEADS_2,), f32, 1.0, 6.0)
    attn_w_q = nrm(ks[15], (N_B_LAYERS, D, D), D ** -0.5)
    attn_w_o = nrm(ks[16], (N_B_LAYERS, D, D), 0.5 * D ** -0.5)
    ffn_norm = gain(ks[17], (DEPTH, D))
    ffn_w1 = nrm(ks[18], (DEPTH, D, D_FF_2), D ** -0.5)
    ffn_w2 = nrm(ks[19], (DEPTH, D_FF_2, D), 0.5 * D_FF_2 ** -0.5)
    ple_norm = gain(ks[20], (DEPTH, D))
    ple_w_gate = nrm(ks[21], (DEPTH, D, D), D ** -0.5)
    ple_w_proj = nrm(ks[22], (DEPTH, D_PLE, D), 0.5 * D_PLE ** -0.5)
    final_norm = gain(ks[23], (D,))
    return {"x": x, "p": p, "mix_norm": mix_norm,
            "conv_w_pw1": conv_w_pw1, "conv_b_pw1": conv_b_pw1,
            "conv_w_dw": conv_w_dw, "conv_b_dw": conv_b_dw,
            "conv_ln_g": conv_ln_g, "conv_ln_b": conv_ln_b,
            "conv_w_pw2": conv_w_pw2, "conv_b_pw2": conv_b_pw2,
            "kv_norm": kv_norm, "w_kvf": w_kvf, "b_f": b_f,
            "attn_w_q": attn_w_q, "attn_w_o": attn_w_o,
            "ffn_norm": ffn_norm, "ffn_w1": ffn_w1, "ffn_w2": ffn_w2,
            "ple_norm": ple_norm, "ple_w_gate": ple_w_gate, "ple_w_proj": ple_w_proj,
            "final_norm": final_norm}

def second_block(x, p, mix_norm, conv_w_pw1, conv_b_pw1, conv_w_dw, conv_b_dw,
              conv_ln_g, conv_ln_b, conv_w_pw2, conv_b_pw2, kv_norm, w_kvf, b_f,
              attn_w_q, attn_w_o, ffn_norm, ffn_w1, ffn_w2, ple_norm, ple_w_gate,
              ple_w_proj, final_norm):
    h = x
    k = v = c_bhs = None
    for i in range(DEPTH):
        hn = rmsnorm(h, mix_norm[i])
        if i < N_A_LAYERS:
            h = h + conformer_conv(hn, conv_w_pw1[i], conv_b_pw1[i], conv_w_dw[i],
                                   conv_b_dw[i], conv_ln_g[i], conv_ln_b[i],
                                   conv_w_pw2[i], conv_b_pw2[i])
        else:
            j = i - N_A_LAYERS
            if j == 0:
                k, v, c_bhs = shared_kv(h, kv_norm, w_kvf, b_f)
            h = h + fox_attention(hn, attn_w_q[j], attn_w_o[j], k, v, c_bhs)
        hn = rmsnorm(h, ffn_norm[i])
        h = h + jnp.square(jax.nn.relu(hn @ ffn_w1[i])) @ ffn_w2[i]
        gate = jax.nn.sigmoid(rmsnorm(h, ple_norm[i]) @ ple_w_gate[i])
        h = h + gate * (p[i] @ ple_w_proj[i])
    return rmsnorm(h, final_norm)


def setup_inputs(seed=0):
    out = dict(first_inputs(seed))
    for name, value in second_inputs(seed + 1).items():
        if name != "x":
            out[name + "_2"] = value
    return out


def reference(
    x, hg_w_in, hg_lb, hg_norm_g, hg_w_out, da_w_in, da_lam, da_norm_g, da_w_out, nsa_w_in,
    nsa_cmp_pe, nsa_cmp_w1, nsa_cmp_w2, nsa_w_out, sb_w_in, sb_w_out, ffn_w_gate, ffn_w_up,
    ffn_w_down, moe_w_router, moe_w_gate, moe_w_up, moe_w_down, ln_g, ln_b, p_2, mix_norm_2,
    conv_w_pw1_2, conv_b_pw1_2, conv_w_dw_2, conv_b_dw_2, conv_ln_g_2, conv_ln_b_2,
    conv_w_pw2_2, conv_b_pw2_2, kv_norm_2, w_kvf_2, b_f_2, attn_w_q_2, attn_w_o_2, ffn_norm_2,
    ffn_w1_2, ffn_w2_2, ple_norm_2, ple_w_gate_2, ple_w_proj_2, final_norm_2,
):
    x = first_block(
        x, hg_w_in, hg_lb, hg_norm_g, hg_w_out, da_w_in, da_lam, da_norm_g, da_w_out, nsa_w_in,
        nsa_cmp_pe, nsa_cmp_w1, nsa_cmp_w2, nsa_w_out, sb_w_in, sb_w_out, ffn_w_gate, ffn_w_up,
        ffn_w_down, moe_w_router, moe_w_gate, moe_w_up, moe_w_down, ln_g, ln_b,
    )
    return second_block(
        x, p_2, mix_norm_2, conv_w_pw1_2, conv_b_pw1_2, conv_w_dw_2, conv_b_dw_2, conv_ln_g_2,
        conv_ln_b_2, conv_w_pw2_2, conv_b_pw2_2, kv_norm_2, w_kvf_2, b_f_2, attn_w_q_2,
        attn_w_o_2, ffn_norm_2, ffn_w1_2, ffn_w2_2, ple_norm_2, ple_w_gate_2, ple_w_proj_2,
        final_norm_2,
    )


_drawn_inputs = setup_inputs


def setup_inputs(seed=0):
    import zlib

    import numpy as np

    out = dict(_drawn_inputs(seed))
    spreads = {}
    factors = {'hg_lb': 8.0,
     'hg_norm_g': 8.0,
     'da_norm_g': 8.0,
     'mix_norm_2': 3.388,
     'conv_b_pw1_2': 8.0,
     'conv_b_dw_2': 4.07,
     'conv_ln_g_2': 3.149,
     'conv_ln_b_2': 8.0,
     'conv_b_pw2_2': 2.697,
     'kv_norm_2': 6.17,
     'ple_norm_2': 8.0}
    for name, (base, spread) in spreads.items():
        noise = np.random.default_rng([zlib.crc32(name.encode()), seed]).standard_normal(out[name].shape)
        drawn = base * np.exp(spread * noise) if base else spread * noise
        out[name] = __import__('jax').numpy.asarray(drawn.astype(out[name].dtype))
    for name, factor in factors.items():
        out[name] = (out[name] * factor).astype(out[name].dtype)
    return out
```

```python
import math
from contextlib import ExitStack

import numpy as np

import concourse.bass as bass
from concourse import mybir

P = 128
D = 1024
SEQ = 256
NB = SEQ // P
KT = D // P
NH = 8
DEPTH = 2
W = 512
HALF = W // 2
D_FF, D_FFE, D_FF2 = 2816, 3584, 4096
NE = 8
NH2, HD2 = 16, 64
D_PLE = 256
CONV = 31
LN_EPS, RMS_EPS = 1e-5, 1e-6
ALPHA = (2 * DEPTH) ** 0.25
LAM_INIT = 0.8 - 0.6 * math.exp(-0.3)
NEG = -1e30
RING = 3
RAW = 6
SPLITS = 3
CH = KT * W
MAX_EXTRA = SEQ * 2 // (P + 1)

F32 = mybir.dt.float32
F32R = mybir.dt.float32r
I32 = mybir.dt.int32
ALU = mybir.AluOpType
ACT = mybir.ActivationFunctionType
AX = mybir.AxisListType

C_ID, C_AID, C_CAUS = 0, P, 2 * P
C_COS = C_CAUS + 2 * P
C_SIN = C_COS + NB * 32
C_IOTA = C_SIN + NB * 32
C_KEY = C_IOTA + P
C_EVAL = C_KEY + NE
C_ONES = C_EVAL + NE
C_END = C_ONES + P
H_MASK, H_LEV, H_TRI, H_END = 0, 8 * P, 16 * P, 17 * P
LEVELS = [64, 32, 16, 8, 4, 2, 1]


def constant_table():
    c = np.zeros((P, C_END), np.float32)
    i = np.arange(P)
    c[:, C_ID:C_ID + P] = np.eye(P)
    c[:, C_AID:C_AID + P] = ALPHA * np.eye(P)
    u, t = i[:, None], i[None, :]
    lev = [(u > t)]
    mask = []
    for h in LEVELS:
        right = t % (2 * h) >= h
        mid = t // (2 * h) * (2 * h) + h
        lev.append(np.where(right, (u >= mid) & (u <= t), (u > t) & (u < mid)))
        mask.append((u // (2 * h) == t // (2 * h)) & right & (u % (2 * h) < h))
    lev.append(u <= t)
    mask.append(u == t)
    hg = np.concatenate(mask + lev, 1).astype(np.float32)
    c[:, C_CAUS + P:C_CAUS + 2 * P] = np.where(t <= u, 0.0, NEG)
    inv = (10000.0 ** (-np.arange(32, dtype=np.float32) / 32)).astype(np.float32)
    ang = (np.arange(SEQ, dtype=np.float32)[:, None] * inv[None, :]).astype(np.float32)
    for b in range(NB):
        c[:, C_COS + 32 * b:C_COS + 32 * b + 32] = np.cos(ang[b * P:b * P + P])
        c[:, C_SIN + 32 * b:C_SIN + 32 * b + 32] = np.sin(ang[b * P:b * P + P])
    c[:, C_IOTA:C_IOTA + P] = t
    c[:, C_KEY:C_KEY + NE] = NE - np.arange(NE)
    c[:, C_EVAL:C_EVAL + NE] = np.arange(NE)
    c[:, C_ONES:C_ONES + P] = 1.0
    return c, hg


def head_rows():
    return np.repeat(np.eye(NH2, dtype=np.float32)[:, :, None], P, 2)


class Plan:

    def __init__(self):
        self.steps = self.turns = self.chunk = 0
        self.ready = [0] * RING
        self.chunk_ready = {}
        self.chunk_use = {}
        self.uses = [0] * RING
        self.expert_start = None

    def new_chunks(self, n, loads, freed=True):
        first = self.chunk
        for c in range(first, first + n):
            s = c % RING
            self.ready[s] += loads[c - first]
            self.chunk_ready[c] = 16 * self.ready[s]
            self.chunk_use[c] = self.uses[s]
            self.uses[s] += freed
        self.chunk += n
        return first

    def take_turns(self, n):
        t = self.turns
        self.turns += n
        return t

    def take_steps(self, turned):
        g, t = self.steps, []
        for x in turned:
            t.append(self.turns if x else None)
            self.turns += bool(x)
        self.steps += len(turned)
        return g, t


def build(nc, t):
    ctx = ExitStack()
    with ctx:
        _program(nc, t, ctx)


def _program(nc, t, ctx):
    def sb(name, shape, dt=F32):
        return ctx.enter_context(nc.sbuf_tensor(name, shape, dt))

    def sem(name):
        return ctx.enter_context(nc.semaphore(name))

    acc = ctx.enter_context(nc.psum_tensor("acc", [P, 4, W], F32))
    up = ctx.enter_context(nc.psum_tensor("up", [P, 2, W], F32))
    tp = ctx.enter_context(nc.psum_tensor("tp", [P, 2, W], F32))

    raw = sb("raw", [P, RAW, CH // 2])
    ring = raw[:, 0:2 * RING, :].rearrange("p (c a) n -> p c (a n)", a=2)
    cst = sb("cst", [P, C_END])
    h = sb("h", [P, NB, D])
    xT = sb("xT", [P, KT, SEQ])
    x2 = sb("x2", [P, KT, SEQ])
    big = sb("big", [P, H_END])
    rows = big[:, 0:2 * D]
    stage = sb("stage", [P, 2, W])
    half = sb("half", [P, 2, W])
    wh = sb("wh", [P, SPLITS, CH // 2], F32R)
    wl = sb("wl", [P, SPLITS, CH // 2], F32R)
    xgh = sb("xgh", [P, KT, P], F32R)
    xgl = sb("xgl", [P, KT, P], F32R)
    hTh = sb("hTh", [P, 2, HALF], F32R)
    hTl = sb("hTl", [P, 2, HALF], F32R)
    hT = sb("hT", [P, 2, W])
    arena = sb("arena", [P, 5, 2 * D])
    cols = sb("cols", [P, 6, KT])
    rowcols = sb("rowcols", [P, 3, KT])
    wdw = sb("wdw", [P, KT, CONV])
    wr = sb("wr", [P, KT, NE])
    wf = sb("wf", [P, KT, NH2])
    bnd = sb("bnd", [P, 2, 6])
    mv = sb("mv", [P, NB, 2])
    sc = sb("sc", [P, NB, 8])
    ss = sb("ss", [P, NB, NH])
    rs = sb("rs", [P, NB, NH])
    lam = sb("lam", [P, 4 * 64 + 8])
    gn = sb("gn", [P, P])
    att = sb("att", [P, 2, 8])
    rt = sb("rt", [P, 16, NB, NE])
    ex = sb("ex", [P, 8, NE])
    slot = sb("slot", [P, NB, NE + MAX_EXTRA])
    gate = sb("gate", [P, NB, NE + MAX_EXTRA])
    extra = sb("extra", [P, 1 + MAX_EXTRA])
    extra_i = sb("extra_i", [P, 1 + MAX_EXTRA], I32)
    fx = sb("fx", [P, 8, NB, NH2])
    ncT = sb("ncT", [NH2, SEQ])
    bf = sb("bf", [P, NH2])

    ident = cst[:, C_ID:C_ID + P]
    aident = cst[:, C_AID:C_AID + P]
    ones = cst[:, C_ONES:C_ONES + P]
    tri = big[:, H_TRI:H_TRI + P]
    iota = cst[:, C_IOTA:C_IOTA + P]
    causal = cst[:, C_CAUS:C_CAUS + 2 * P]
    accb = acc[:, :, :].rearrange("p (b n) w -> p b (n w)", b=NB)

    lf, qT_, kT_, v_, o_ = (arena[:, i, :] for i in range(5))
    as_tm = lambda a: a.rearrange("p (b n) -> p b n", b=NB)
    as_cm = lambda a: a.rearrange("p (k n) -> p k n", k=KT)
    lf, v, o = as_tm(lf), as_tm(v_), as_tm(o_)
    qT, kT = as_cm(qT_), as_cm(kT_)
    flat = lambda a: a.rearrange("p a b -> p (a b)")
    hg_raw = flat(arena[:, 3:5, :])[:, 0:3 * D].rearrange("p (r n) -> p r n", r=3)
    x2f, xTf, hTf = flat(x2[:, :, :]), flat(xT[:, :, :]), flat(hT[:, :, :])
    lb, omlb = x2f[:, 0:D], x2f[:, D:2 * D]
    hgA = xTf.rearrange("p (i s n) -> p i s n", i=2, s=8)
    hgB = x2f.rearrange("p (i s n) -> p i s n", i=2, s=8)
    hgS = hTf.rearrange("p (s n) -> p s n", s=8)
    hgX = stage[:, 0, 0:P]
    at_s = arena[:, 0, 0:D].rearrange("p (i c n) -> p i c n", i=2, c=2)
    at_p = arena[:, 0, D:2 * D].rearrange("p (i c n) -> p i c n", i=2, c=2)
    headrow = x2f[0:NH2, :].rearrange("p (h q) -> p h q", h=NH2)
    y = as_tm(arena[:, 0, :])
    ye = arena[:, 1, D:2 * D]
    pick = arena[:, 2, 0:2 * P].rearrange("p (b n) -> p b n", b=NB)
    give = arena[:, 2, 2 * P:4 * P].rearrange("p (b n) -> p b n", b=NB)
    giveT = arena[:, 2, 4 * P:6 * P].rearrange("p (b n) -> p b n", b=NB)
    PADC = CONV - 1
    uT = flat(arena[:, 0:2, :])[:, 0:KT * (SEQ + PADC)].rearrange("p (k n) -> p k n", k=KT)
    cT = as_cm(arena[:, 2, :])
    ctm = as_tm(arena[:, 3, :])
    pe_tm = arena[:, 3, 0:2 * D_PLE].rearrange("p (b n) -> p b n", b=NB)
    pe_T = arena[:, 3, 2 * D_PLE:4 * D_PLE].rearrange("p (k n) -> p k n", k=2)

    def score_banks(n):
        return up if n % 2 == 0 else acc[:, 2:4, :]

    def ring_k(c, n=KT):
        return ring[:, c % RING, :].rearrange("p (k n) -> p k n", k=n)

    def ring_gu(c):
        return ring[:, c % RING, :].rearrange("p (k m n) -> p k m n", k=KT, m=2)

    pl = Plan()
    one = lambda n: [1] * n
    T_x = pl.take_turns(4)
    HG_CHUNKS = [2, 3, 0, 1, 4, 5, 6, 7]
    c_hg = pl.new_chunks(8, one(8))
    g_hg, t_hg = pl.take_steps([c < 4 for c in HG_CHUNKS for _ in range(NB)])
    T_hgo = pl.take_turns(4)
    c_hgo = pl.new_chunks(2, one(2))
    T_ff = pl.take_turns(4)
    FF_UNITS = D_FF // HALF
    c_ff = pl.new_chunks(17, [1 if i % 3 == 2 or i == 16 else 2 for i in range(17)])
    ff_gu = [c_ff + 3 * (u // 2) + u % 2 for u in range(FF_UNITS)]
    ff_d = [c_ff + 3 * (u // 2) + (2 if u // 2 < FF_UNITS // 2 else 1) for u in range(FF_UNITS)]
    g_ff, t_ff = pl.take_steps([1] * (FF_UNITS * NB))
    T_da = pl.take_turns(4)
    c_da = pl.new_chunks(6, one(6))
    g_da, t_da = pl.take_steps([c < 4 for c in range(6) for _ in range(NB)])
    T_dao = pl.take_turns(4)
    c_dao = pl.new_chunks(2, one(2))
    T_moe = pl.take_turns(4)
    pl.chunk += -pl.chunk % RING
    EU = D_FFE // HALF
    moe_use0 = list(pl.uses)
    G, DN = 0, 1
    HALVES = [(G, 0, 0), (G, 0, 1)]
    for u in range(1, EU):
        HALVES += [(G, u, 0), (G, u, 1), (DN, u - 1, 0)]
    HALVES.append((DN, EU - 1, 0))
    NHALF = len(HALVES)
    half_at = {x: m for m, x in enumerate(HALVES)}
    gate_half = lambda u, part: half_at[G, u, part]
    down_half = lambda u: half_at[DN, u, 0]
    assert NHALF % RAW == 0 and NHALF % SPLITS == 0
    half_loads = [2 if x[0] == G else 1 for x in HALVES]
    slot_loads = [sum(half_loads[r::RAW]) for r in range(RAW)]
    tells_used = lambda m: m < NHALF - 1 and not (HALVES[m][0] == G and HALVES[m][2] == 1)
    used_until = lambda m: sum(map(tells_used, range(m + 1)))
    NUSED = used_until(NHALF - 1)
    T_cv = pl.take_turns(4)
    c_pw1 = pl.new_chunks(4, [2] * 4)
    g_cv, t_cv = pl.take_steps([1] * 8)
    T_cback = pl.take_turns(4)
    T_cn = pl.take_turns(4)
    c_pw2 = pl.new_chunks(2, one(2))
    after = []
    for i in range(DEPTH):
        d = {}
        if i == 1:
            d["T_q"] = pl.take_turns(4)
            d["c_k"] = pl.new_chunks(4, one(4))
            d["g_kv"], d["t_kv"] = pl.take_steps([1] * 4 + [0] * 4)
            d["g_f"], _ = pl.take_steps([0] * 2)
            d["c_q"] = pl.new_chunks(2, one(2))
            d["g_q"], d["t_q"] = pl.take_steps([1] * 4)
            d["T_o"] = pl.take_turns(4)
            d["c_o"] = pl.new_chunks(2, one(2))
        d["T_f"] = pl.take_turns(4)
        d["c_f"] = pl.new_chunks(16, one(16))
        d["g_ff"], d["t_ff"] = pl.take_steps([1] * 16)
        d["T_p"] = pl.take_turns(1)
        d["T_g"] = pl.take_turns(4)
        d["c_p"] = pl.new_chunks(3, one(3))
        d["g_p"], _ = pl.take_steps([0] * 4)
        after.append(d)

    def half_ready(eng, m, i, x):
        eng.wait_ge(m["ready"][x % RAW], i * (16 * slot_loads[x % RAW]) + 16 * sum(half_loads[x % RAW:x + 1:RAW]))

    w_ready = [sem(f"w_ready{s}") for s in range(RING)]
    w_free = [sem(f"w_free{s}") for s in range(RING)]
    s_cst = sem("s_cst")
    s_x = sem("s_x")
    s_small = sem("s_small")
    s_gn = sem("s_gn")
    s_lb = sem("s_lb")
    s_rows = sem("s_rows")
    s_rows_free = sem("s_rows_free")
    s_pe = sem("s_pe")
    s_headrow = sem("s_headrow")
    s_up = sem("s_up")
    s_act = sem("s_act")
    s_st = sem("s_st")
    s_T = sem("s_T")
    s_Te = sem("s_Te")
    s_acc = sem("s_acc")
    s_norm = sem("s_norm")
    s_nA = sem("s_nA")
    s_nD = sem("s_nD")
    d_ch = sem("d_ch")
    a_ch = sem("a_ch")
    s_lbA, s_lbD = sem("s_lbA"), sem("s_lbD")
    hg_m, hg_e, hg_ab, hg_s, hg_sm, hg_o, hg_sq, hg_og = (
        sem(n) for n in ("hg_decay", "hg_exp", "hg_scaled", "hg_scores", "hg_masked", "hg_out", "hg_square", "hg_gated"))
    at_S, at_sm, at_e, at_w, at_T, at_Te, at_O, at_sq, at_og = (
        sem(n) for n in ("at_scores", "at_masked", "at_exp", "at_weights", "at_turned", "at_copied", "at_out",
                         "at_square", "at_kept"))
    s_hn = sem("s_hn")
    s_rl, s_rp, s_ra, s_rd = sem("router_logits"), sem("router_places"), sem("router_act"), sem("router_done")
    moe = [{n: sem(f"{p}{n}") for n in ("picked", "gath", "xg", "turned", "giveT", "up", "act", "st", "T", "Te",
                                        "hi", "lo", "used", "xgh", "Th", "down", "ye", "give", "added")} for p in ("m_", "x_")]
    for m, p_ in zip(moe, ("m_", "x_")):
        m["ready"] = [sem(f"{p_}ready{r}") for r in range(RAW)]
    cv_dw, cv_T, cv_n = sem("conv_done"), sem("conv_back"), sem("conv_normed")
    f_L, f_A, f_D, f_C, f_CT, f_ct = (sem(n) for n in ("f_logits", "f_act", "f_vec", "f_sum", "f_sumT", "f_sumT_sb"))
    s_xdone = sem("s_xdone")
    s_out = sem("s_out")

    block = ctx.enter_context(nc.Block())

    N_HGO, N_LN0, N_LN1, N_DAO, N_LN2, N_LN3 = (NB * i for i in range(6))
    N_RC = 6 * NB
    N_AFTER = []
    n = N_RC + NB
    N_CB = n
    n += NB
    for i in range(DEPTH):
        d = {}
        if i == 1:
            d["q"] = n
            n += NB
            d["o"] = n
            n += NB
        d["f"] = n
        n += NB
        d["g"] = n
        n += NB
        d["h"] = n
        n += NB
        N_AFTER.append(d)
    N_FIN = n
    A_HG, A_FF, A_DA = 0, NB, 2 * NB
    A_PW2 = 3 * NB
    A_F0, A_O1, A_F1 = 4 * NB, 5 * NB, 6 * NB

    @block.sync
    def _(sp):
        ld = lambda out, in_, s: sp.dma_start(out, in_).then_inc(s, 16)
        kp = lambda w: w.rearrange("(k p) n -> p k n", p=P)

        def wait_slot(c):
            if pl.chunk_use[c] > 0:
                sp.wait_ge(w_free[c % RING], pl.chunk_use[c])

        def cols_chunk(c, w, col):
            wait_slot(c)
            ld(ring_k(c), kp(w[:, col:col + W]), w_ready[c % RING])

        def pair_chunk(c, wa, wb, col):
            wait_slot(c)
            ld(ring_gu(c)[:, :, 0, :], kp(wa[:, col:col + HALF]), w_ready[c % RING])
            ld(ring_gu(c)[:, :, 1, :], kp(wb[:, col:col + HALF]), w_ready[c % RING])

        def rows_chunk(c, w, row, n):
            wait_slot(c)
            ld(ring_k(c, 4)[:, 0:n, :], kp(w[row:row + n * P, :]), w_ready[c % RING])

        ld(cst[:, :], t["consts"], s_cst)
        ld(big[:, :], t["hg_tables"], s_cst)
        ld(h[:, :, :], t["x"][0].rearrange("(b p) n -> p b n", p=P), s_x)
        for i, c in enumerate(HG_CHUNKS):
            cols_chunk(c_hg + i, t["hg_w_in"], c * W)
        for i in range(2):
            cols_chunk(c_hgo + i, t["hg_w_out"], i * W)
        for u in range(FF_UNITS):
            pair_chunk(ff_gu[u], t["ffn_w_gate"][0], t["ffn_w_up"][0], u * HALF)
            if u % 2 == 1:
                rows_chunk(ff_d[u], t["ffn_w_down"][0], (u - 1) * HALF, 4)
            elif u == FF_UNITS - 1:
                rows_chunk(ff_d[u], t["ffn_w_down"][0], u * HALF, 2)
        for i in range(6):
            cols_chunk(c_da + i, t["da_w_in"], i * W)
        for i in range(2):
            cols_chunk(c_dao + i, t["da_w_out"], i * W)

        def expert(m, e, i):
            gw, uw, dw = (t[n][0, bass.ds(e, 1), :, :].rearrange("a k n -> (a k) n")
                          for n in ("moe_w_gate", "moe_w_up", "moe_w_down"))
            for x, (kind, u, part) in enumerate(HALVES):
                sp.wait_ge(m["lo"], i * NHALF + (x + 1))
                dst, ready = raw[:, x % RAW, :], m["ready"][x % RAW]
                if kind == G:
                    dst = dst.rearrange("p (k m n) -> p k m n", k=KT // 2, m=2)
                    for j, w in enumerate((gw, uw)):
                        ld(dst[:, :, j, :], kp(w[part * (D // 2):(part + 1) * (D // 2), u * HALF:(u + 1) * HALF]), ready)
                else:
                    ld(dst.rearrange("p (k n) -> p k n", k=2), kp(dw[u * HALF:(u + 1) * HALF, :]), ready)

        for s in range(RING):
            sp.wait_ge(w_free[s], moe_use0[s])
        with sp.Fori(0, NE) as e:
            expert(moe[0], e, e)

        sp.wait_ge(s_rd, 1)
        sp.wait_ge(moe[0]["lo"], NE * NHALF + RAW)
        n_extra = sp.value_load(extra_i[0:1, 0:1], min_val=0, max_val=MAX_EXTRA)
        with sp.If(n_extra > 0):
            with sp.Fori(0, n_extra) as j:
                e = sp.value_load(extra_i[0:1, bass.ds(j + 1, 1)], min_val=0, max_val=NE - 1)
                expert(moe[1], e, j)
            sp.wait_ge(moe[1]["lo"], n_extra * NHALF + RAW)
            sp.sem_inc(s_xdone, 1)

        for i in range(4):
            pair_chunk(c_pw1 + i, t["conv_w_pw1_2"][0][:, 0:D], t["conv_w_pw1_2"][0][:, D:2 * D], i * HALF)
        for i in range(2):
            cols_chunk(c_pw2 + i, t["conv_w_pw2_2"][0], i * W)
        for i, d in enumerate(after):
            if i == 1:
                for c in range(4):
                    cols_chunk(d["c_k"] + c, t["w_kvf_2"], c * W)
                for c in range(2):
                    cols_chunk(d["c_q"] + c, t["attn_w_q_2"][0], c * W)
                for c in range(2):
                    cols_chunk(d["c_o"] + c, t["attn_w_o_2"][0], c * W)
            for u in range(8):
                cols_chunk(d["c_f"] + 2 * u, t["ffn_w1_2"][i], u * W)
                rows_chunk(d["c_f"] + 2 * u + 1, t["ffn_w2_2"][i], u * W, 4)
            wait_slot(d["c_p"])
            rows_chunk(d["c_p"], t["ple_w_proj_2"][i], 0, 2)
            for c in range(2):
                cols_chunk(d["c_p"] + 1 + c, t["ple_w_gate_2"][i], c * W)

        for b in range(NB):
            sp.wait_ge(s_norm, N_FIN + b + 1)
            ld(t["out"][0, b * P:(b + 1) * P, :], o[:, b, :], s_out)
        sp.wait_ge(s_out, 16 * NB)

    SMALL = 0

    @block.gpsimd
    def _(pool):
        nonlocal SMALL

        def small(out, in_):
            nonlocal SMALL
            pool.dma_start(out, in_).then_inc(s_small, 16)
            SMALL += 16

        bc = lambda row: row.partition_broadcast(P)
        pool.dma_start(hg_raw, t["hg_lb"].rearrange("r n -> (r n)").partition_broadcast(P)
                       .rearrange("p (r n) -> p r n", r=3)).then_inc(s_lb, 16)

        def load_rows(*srcs):
            for i, s in enumerate(srcs):
                pool.dma_start(rows[:, i * D:(i + 1) * D], bc(s)).then_inc(s_rows, 16)

        with nc.allow_non_contiguous_dma(reason="small parameters"):
            pool.dma_start(gn[:, :], bc(t["hg_norm_g"])).then_inc(s_gn, 16)
            small(lam[:, 0:256], bc(t["da_lam"].rearrange("a n -> (a n)")))
            small(wr[:, :, :], t["moe_w_router"][0].rearrange("(k p) n -> p k n", p=P))
            small(wf[:, :, :], t["w_kvf_2"][:, 2 * D:2 * D + NH2].rearrange("(k p) n -> p k n", p=P))
            small(bf[:, :], bc(t["b_f_2"]))
            for i, a in enumerate((t["mix_norm_2"][0], t["mix_norm_2"][1], t["kv_norm_2"],
                                   t["ffn_norm_2"][0], t["ffn_norm_2"][1], t["ple_norm_2"][0])):
                small(cols[:, i, :], a.rearrange("(k p) -> p k", p=P))
            for i, a in enumerate((t["conv_b_dw_2"][0], t["conv_ln_g_2"][0], t["conv_ln_b_2"][0])):
                small(rowcols[:, i, :], a.rearrange("(k p) -> p k", p=P))
            for k in range(KT):
                small(wdw[:, k, :], t["conv_w_dw_2"][0][:, k * P:(k + 1) * P].rearrange("j p -> p j"))
            pool.wait_ge(hg_o, NH * NB)
            load_rows(t["ln_g"][0, 0], t["ln_b"][0, 0])
            for i, s in enumerate(((t["ln_g"][0, 1], t["ln_b"][0, 1]), (t["ln_g"][1, 0], t["ln_b"][1, 0]),
                                   (t["ln_g"][1, 1], t["ln_b"][1, 1]),
                                   (t["conv_b_pw1_2"][0][0:D], t["conv_b_pw1_2"][0][D:2 * D]),
                                   (t["conv_b_pw2_2"][0], t["final_norm_2"]))):
                pool.wait_ge(s_rows_free, i + 1)
                load_rows(*s)
                if i == 0:
                    pool.dma_start(gn[:, :], bc(t["da_norm_g"])).then_inc(s_gn, 16)
            pool.wait_ge(s_T, T_cn + 4)
            pool.dma_start(pe_tm, t["p_2"][0, 0].rearrange("(b p) n -> p b n", p=P)).then_inc(s_pe, 16)
            pool.wait_ge(s_norm, N_AFTER[0]["h"] + NB)
            pool.dma_start(cols[:, 5, :], t["ple_norm_2"][1].rearrange("(k p) -> p k", p=P)).then_inc(s_pe, 16)
            pool.wait_ge(s_up, after[1]["g_f"] + NB)
            pool.dma_start(headrow, t["headrow"]).then_inc(s_headrow, 16)
            pool.wait_ge(s_T, after[1]["T_o"] + 4)
            pool.dma_start(pe_tm, t["p_2"][1, 0].rearrange("(b p) n -> p b n", p=P)).then_inc(s_pe, 16)

    @block.scalar
    def _(act):
        f = nc.scalar.activation
        chain = 0

        def link(ins):
            nonlocal chain
            chain += 1
            ins.then_inc(a_ch, 1)
            act.wait_ge(a_ch, chain)

        def copy_turn(t_, out, in_):
            act.wait_ge(s_T, t_ + 1)
            f(out, in_, ACT.Copy).then_inc(s_Te, 1)

        def to_channels(t0, dst=None):
            dst = xT if dst is None else dst
            for b in range(NB):
                for q in range(2):
                    tt = t0 + 2 * b + q
                    copy_turn(tt, dst[:, 4 * q:4 * q + 4, b * P:(b + 1) * P],
                              tp[:, tt % 2, :].rearrange("p (k n) -> p k n", k=4))

        def step_copy(tt, dst, chunk, b, nk=4):
            copy_turn(tt, dst[:, nk * chunk:nk * chunk + nk, b * P:(b + 1) * P],
                      tp[:, tt % 2, 0:nk * P].rearrange("p (k n) -> p k n", k=nk))

        acts = [0]

        def step_act(g, out, in_, func, **kw):
            act.wait_ge(s_up, g + 1)
            f(out, in_, func, **kw).then_inc(s_act, 1)
            acts[0] += 1

        nsq = [0]

        def norm_root(out, in_):
            nsq[0] += 1
            act.wait_ge(s_nD, nsq[0])
            f(out, in_, ACT.Sqrt).then_inc(s_nA, 1)

        def layer_norms():
            for b in range(NB):
                norm_root(sc[:, b, 1:2], sc[:, b, 0:1])

        sums = [0]

        def root_sums(b):
            f(half[:, :, :], h[:, b, :].rearrange("p (a n) -> p a n", a=2), ACT.Square,
              accum_out=sc[:, b, 2:3]).then_inc(a_ch, 1)

        def square_out(m):
            return half[:, (m // 4) % 2, (m % 4) * P:(m % 4 + 1) * P]

        act.wait_ge(s_lbD, 1)
        for r in range(3):
            ins = f(hg_raw[:, r, :], hg_raw[:, r, :], ACT.Exp)
        ins.then_inc(s_lbA, 1)
        to_channels(T_x)
        for i, c in enumerate(HG_CHUNKS):
            for b in range(NB):
                g = g_hg + NB * i + b
                if i > 0 or b > 0:
                    prev = t_hg[NB * i + b - 1]
                    if prev is not None:
                        pc = HG_CHUNKS[(NB * i + b - 1) // NB]
                        step_copy(prev, kT if pc >= 2 else qT, pc % 2, (b + 1) % NB)
                func = ACT.Sigmoid if c in (2, 3, 6, 7) else ACT.Silu if c < 2 else ACT.Copy
                step_act(g, half[:, g % 2, :], up[:, g % 2, :], func)
                if c in (2, 3):
                    act.wait_ge(s_lbD, 2 + (NB * i + b) + 1)
                    f(lf[:, b, (c - 2) * W:(c - 1) * W], half[:, g % 2, :], ACT.Ln).then_inc(s_lbA, 1)
        for n in range(NH * NB + 3):
            if n < NH * NB:
                act.wait_ge(hg_m, n + 1)
                f(acc[:, 0:2, :], acc[:, 0:2, :], ACT.Exp).then_inc(hg_e, 1)
            if 2 <= n < NH * NB + 2:
                m = n - 2
                j, b = m // NB, m % NB
                act.wait_ge(hg_o, m + 1)
                f(square_out(m), up[:, m % 2, 0:P], ACT.Square, accum_out=ss[:, b, j:j + 1]).then_inc(hg_sq, 1)
        act.wait_ge(s_hn, 1)
        f(rs[:, :, :], rs[:, :, :], ACT.Sqrt).then_inc(s_hn, 1)
        to_channels(T_hgo)
        layer_norms()

        def mlp(g0, ts, gate, width):
            for s, tt in enumerate(ts):
                if s > 0:
                    copy_turn(ts[s - 1], hT[:, (s - 1) % 2, 0:width], tp[:, ts[s - 1] % 2, 0:width])
                g = g0 + s
                step_act(g, half[:, g % 2, 0:width], up[:, g % 2, 0:width], gate)
            copy_turn(ts[-1], hT[:, (len(ts) - 1) % 2, 0:width], tp[:, ts[-1] % 2, 0:width])

        to_channels(T_ff)
        mlp(g_ff, t_ff, ACT.Silu, HALF)
        layer_norms()

        act.wait_ge(s_lbD, 2 + 2 * NB + 1)
        f(lam[:, 256:258], lam[:, 256:258], ACT.Exp).then_inc(s_lbA, 1)
        to_channels(T_da)
        for s in range(8):
            step_copy(t_da[s], qT if s < 4 else kT, (s // NB) % 2, s % NB)

        def exps(n, b, base):
            w = P * (b + 1)
            act.wait_ge(at_sm, base + n + 1)
            for c in range(2):
                ins = f(at_p[:, n % 2, c, 0:w], at_s[:, n % 2, c, 0:w], ACT.Exp, bias=att[:, n % 2, c:c + 1],
                        accum_out=att[:, n % 2, 2 + c:3 + c])
            ins.then_inc(at_e, 1)

        NA = NH * NB
        for n in range(NA + 3):
            if n < NA:
                exps(n, n % NB, 0)
            if 1 <= n <= NA:
                m = n - 1
                w = P * (m % NB + 1)
                act.wait_ge(at_T, m + 1)
                f(hT[:, m % 2, 0:w], tp[:, m % 2, 0:w], ACT.Copy).then_inc(at_Te, 1)
            if 2 <= n < NA + 2:
                m = n - 2
                act.wait_ge(at_O, m + 1)
                f(square_out(m), acc[:, m % 2, 0:P], ACT.Square,
                  accum_out=ss[:, m % NB, m // NB:m // NB + 1]).then_inc(at_sq, 1)
        act.wait_ge(s_hn, 4)
        f(rs[:, :, :], rs[:, :, :], ACT.Sqrt).then_inc(s_hn, 1)
        to_channels(T_dao)
        layer_norms()

        to_channels(T_moe)
        act.wait_ge(s_ra, 1)
        f(rt[:, 7, :, 0:1], rt[:, 7, :, 0:1], ACT.Sigmoid).then_inc(s_rp, 1)

        def expert(m, i):
            def split(x):
                half_ready(act, m, i, x)
                if x >= SPLITS:
                    kind, u, _ = HALVES[x - SPLITS]
                    if tells_used(x - SPLITS):
                        act.wait_ge(m["used"], i * NUSED + used_until(x - SPLITS))
                    else:
                        act.wait_ge(m["up"], i * EU + (u + 1))
                f(wh[:, x % SPLITS, :], raw[:, x % RAW, :], ACT.Copy).then_inc(m["hi"], 1)

            split(0)
            split(1)
            for q in range(2):
                act.wait_ge(m["gath"], i * 2 + (q + 2))
                f(xgh[:, 4 * q:4 * q + 4, :], tp[:, q, :].rearrange("p (k n) -> p k n", k=4), ACT.Copy).then_inc(m["xgh"], 1)
            act.wait_ge(m["turned"], i + 2)
            f(giveT, acc[:, 2, 0:2 * P].rearrange("p (b n) -> p b n", b=NB), ACT.Copy).then_inc(m["giveT"], 1)
            split(2)
            for s in range(EU + 1):
                if s > 0:
                    act.wait_ge(m["T"], i * EU + s)
                    f(hTh[:, (s - 1) % 2, :], tp[:, (s - 1) % 2, 0:HALF], ACT.Copy).then_inc(m["Th"], 1)
                if 1 <= s < EU - 1:
                    split(gate_half(s + 1, 0))
                if s < EU:
                    act.wait_ge(m["up"], i * EU + (s + 1))
                    f(half[:, s % 2, 0:HALF], up[:, s % 2, 0:HALF], ACT.Silu).then_inc(m["act"], 1)
                if s < EU - 1:
                    split(gate_half(s + 1, 1))
                if s < EU:
                    split(down_half(s))
            act.wait_ge(m["down"], i + 1)
            f(ye.rearrange("p (a n) -> p a n", a=2), acc[:, 0:2, :], ACT.Copy).then_inc(m["ye"], 1)

        for m in moe:
            act.sem_inc(m["ye"], 1)
        with act.Fori(0, NE) as i:
            expert(moe[0], i)
        act.wait_ge(s_rd, 1)
        n_extra = act.value_load(extra_i[0:1, 0:1], min_val=0, max_val=MAX_EXTRA)
        with act.If(n_extra > 0):
            with act.Fori(0, n_extra) as j:
                expert(moe[1], j)
        layer_norms()

        nrms = [0]

        def rms(from_acc, a0=None):
            for b in range(NB):
                if from_acc:
                    act.wait_ge(s_acc, a0 + b + 1)
                    link(f(h[:, b, :], accb[:, b, :], ACT.Copy))
                else:
                    act.wait_ge(s_nD, nsq[0] + 1)
                    nsq[0] += 1
                f(half[:, :, :], h[:, b, :].rearrange("p (a n) -> p a n", a=2), ACT.Square,
                  accum_out=sc[:, b, 2:3]).then_inc(s_nA, 1)
                nsq[0] += 1
                act.wait_ge(s_nD, nsq[0])
                f(sc[:, b, 1:2], sc[:, b, 0:1], ACT.Sqrt).then_inc(s_nA, 1)

        rms(False)
        for s in range(8):
            if s > 0:
                step_copy(t_cv[s - 1], uT[:, :, PADC:], (s - 1) // NB, (s - 1) % NB, 2)
            g = g_cv + s
            act.wait_ge(cv_n, s + 1)
            f(half[:, g % 2, HALF:W], half[:, g % 2, HALF:W], ACT.Sigmoid).then_inc(s_act, 1)
        step_copy(t_cv[7], uT[:, :, PADC:], 3, 1, 2)
        for b in range(NB):
            for q in range(2):
                tt = T_cback + 2 * b + q
                copy_turn(tt, ctm[:, b, q * W:(q + 1) * W], tp[:, tt % 2, :])
        layer_norms()
        for b in range(NB):
            for q in range(2):
                tt = T_cn + 2 * b + q
                act.wait_ge(s_T, tt + 1)
                for k in range(4 * q, 4 * q + 4):
                    ins = f(xT[:, k, b * P:(b + 1) * P], tp[:, tt % 2, (k % 4) * P:(k % 4 + 1) * P], ACT.Silu,
                            scale=rowcols[:, 1, k:k + 1], bias=rowcols[:, 2, k:k + 1])
                ins.then_inc(s_Te, 1)

        for i, d in enumerate(after):
            if i == 1:
                rms(False)
                for s in range(4):
                    step_copy(d["t_kv"][s], kT, s // NB, s % NB)
                act.wait_ge(f_D, 1)
                link(f(fx[:, 1], fx[:, 0], ACT.Abs))
                link(f(fx[:, 1], fx[:, 1], ACT.Exp, scale=-1.0))
                f(fx[:, 2], fx[:, 1], ACT.Ln, bias=1.0).then_inc(f_A, 1)
                for s in range(4):
                    step_copy(d["t_q"][s], qT, s // NB, s % NB)
                act.wait_ge(f_CT, 1)
                f(ncT[:, :], tp[0:NH2, 0, 0:SEQ], ACT.Copy, scale=-1.0).then_inc(f_ct, 1)
                for n in range(NA + 2):
                    if n < NA:
                        exps(n, n % NB, NA)
                    if 1 <= n <= NA:
                        m = n - 1
                        w = 2 * P * (m % NB + 1)
                        act.wait_ge(at_T, NA + m + 1)
                        f(hT[:, m % 2, 0:w], tp[:, m % 2, 0:w], ACT.Copy).then_inc(at_Te, 1)
                to_channels(d["T_o"])
                rms(True, A_O1)
            else:
                rms(False)
            mlp(d["g_ff"], d["t_ff"], ACT.Relu, W)
            rms(True, A_F1 if i else A_F0)
            copy_turn(d["T_p"], pe_T, tp[:, d["T_p"] % 2, :].rearrange("p (k n) -> p k n", k=2))
            for s in range(4):
                g = d["g_p"] + s
                step_act(g, half[:, g % 2, :], up[:, g % 2, :], ACT.Sigmoid)
        rms(False)

    @block.vector
    def _(dve):
        V = nc.vector
        chain = 0

        def link(ins):
            nonlocal chain
            chain += 1
            ins.then_inc(d_ch, 1)
            dve.wait_ge(d_ch, chain)

        acts = [0]

        def wait_act():
            acts[0] += 1
            dve.wait_ge(s_act, acts[0])

        def stage_free(g, last_turn):
            if last_turn is not None:
                dve.wait_ge(s_T, last_turn + 1)

        nst = [0, 0]

        def stats(b, src):
            for q in range(2):
                ins = V.bn_stats(bnd[:, q, :], src[:, q * W:(q + 1) * W])
            link(ins)
            link(V.bn_aggr(mv[:, b, :], bnd[:, :, :]))
            return mv[:, b, 1:2]

        def root(b, var, scale, eps):
            V.tensor_scalar(sc[:, b, 0:1], var, scale, eps, ALU.mult, ALU.add).then_inc(s_nD, 1)
            nst[0] += 1
            nst[1] += 1
            dve.wait_ge(s_nA, nst[1])
            link(V.reciprocal(sc[:, b, 3:4], sc[:, b, 1:2]))
            return sc[:, b, 3:4]

        nrows = [0]

        def layer_norm(src, a0=None):
            nrows[0] += 32
            for b in range(NB):
                if a0 is not None:
                    dve.wait_ge(s_acc, a0 + b + 1)
                r = root(b, stats(b, src[:, b, :]), 1.0, LN_EPS)
                if b == 0:
                    dve.wait_ge(s_rows, nrows[0])
                link(V.scalar_tensor_tensor(h[:, b, :], src[:, b, :], mv[:, b, 0:1], rows[:, 0:D], ALU.subtract, ALU.mult))
                ins = V.scalar_tensor_tensor(h[:, b, :], h[:, b, :], r, rows[:, D:2 * D], ALU.mult, ALU.add)
                chain_ins(ins)
                dve.sem_inc(s_norm, 1)
            dve.sem_inc(s_rows_free, 1)

        chain_ins = link

        e3 = hg_raw
        dve.wait_ge(s_lb, 16)
        link(V.tensor_tensor(lb, e3[:, 0, :], e3[:, 1, :], ALU.max))
        link(V.tensor_tensor(lb, lb, e3[:, 2, :], ALU.max))
        for r in range(3):
            ins = V.tensor_tensor(e3[:, r, :], e3[:, r, :], lb, ALU.subtract)
        ins.then_inc(s_lbD, 1)
        dve.wait_ge(s_lbA, 1)
        link(V.tensor_tensor(lb, e3[:, 0, :], e3[:, 1, :], ALU.add))
        link(V.tensor_tensor(lb, lb, e3[:, 2, :], ALU.add))
        link(V.reciprocal(omlb, lb))
        link(V.tensor_tensor(lb, e3[:, 0, :], omlb, ALU.mult))
        link(V.tensor_scalar(omlb, lb, -1.0, 1.0, ALU.mult, ALU.add))
        dve.sem_inc(s_lbD, 1)
        dve.wait_ge(s_gn, 16)
        last_turn = [None, None]
        for i, c in enumerate(HG_CHUNKS):
            for b in range(NB):
                s = NB * i + b
                g = g_hg + s
                hf = half[:, g % 2, :]
                st = stage[:, g % 2, :]
                wait_act()
                stage_free(g, last_turn[g % 2])
                if c in (2, 3):
                    cc = slice((c - 2) * W, (c - 1) * W)
                    link(V.tensor_tensor(hf, hf, omlb[:, cc], ALU.mult))
                    link(V.tensor_tensor(hf, hf, lb[:, cc], ALU.add))
                    link(V.tensor_scalar(st, hf, -1.0, 1.0, ALU.mult, ALU.add))
                    link(V.tensor_scalar(hf, hf, 2.0 ** -63, None, ALU.max))
                    dve.sem_inc(s_lbD, 1)
                    dve.wait_ge(s_lbA, 2 + s)
                    dve.sem_inc(s_st, 1)
                elif c < 2:
                    V.tensor_copy(st, hf).then_inc(s_st, 1)
                elif c < 6:
                    V.tensor_copy(v[:, b, (c - 4) * W:(c - 3) * W], hf).then_inc(s_st, 1)
                else:
                    V.tensor_tensor(o[:, b, (c - 6) * W:(c - 5) * W].rearrange("p (j n) -> p j n", n=P),
                                    hf.rearrange("p (j n) -> p j n", n=P),
                                    gn[:, :].unsqueeze(1).broadcast_to([P, 4, P]), ALU.mult).then_inc(s_st, 1)
                last_turn[g % 2] = t_hg[s] if t_hg[s] is not None else last_turn[g % 2]
        for n in range(NH * NB + 3):
            if n < NH * NB:
                j, b = n // NB, n % NB
                dve.wait_ge(hg_e, n + 1)
                if n == 0:
                    dve.wait_ge(s_Te, T_hgo)
                if n >= 2:
                    dve.wait_ge(hg_o, n - 1)
                ev = accb[:, 0, :].rearrange("p (s n) -> p s n", s=8)
                for dst, src in ((hgA, qT), (hgB, kT)):
                    ins = V.tensor_tensor(dst[:, n % 2], ev,
                                          src[:, j, b * P:(b + 1) * P].unsqueeze(1).broadcast_to([P, 8, P]), ALU.mult)
                ins.then_inc(hg_ab, 1)
            if 1 <= n <= NH * NB:
                m = n - 1
                dve.wait_ge(hg_s, m + 1)
                if m >= 1:
                    dve.wait_ge(hg_o, m)
                ins = V.tensor_tensor(hgS, accb[:, 1, :].rearrange("p (s n) -> p s n", s=8),
                                      big[:, H_MASK:H_MASK + 8 * P].rearrange("p (s n) -> p s n", s=8), ALU.mult)
                if m % NB == 1:
                    ins = V.tensor_copy(hgX, tp[:, (m // NB) % 2, 0:P])
                ins.then_inc(hg_sm, 1)
            if 3 <= n:
                m = n - 3
                j, b = m // NB, m % NB
                dve.wait_ge(hg_sq, m + 1)
                oj = o[:, b, j * P:(j + 1) * P]
                V.tensor_tensor(oj, up[:, m % 2, 0:P], oj, ALU.mult).then_inc(hg_og, 1)

        def head_norms(k):
            link(V.tensor_scalar(rs[:, :, :], ss[:, :, :], 1.0 / P, LN_EPS, ALU.mult, ALU.add))
            dve.sem_inc(s_hn, 1)
            dve.wait_ge(s_hn, k + 2)
            link(V.reciprocal(rs[:, :, :], rs[:, :, :]))
            for b in range(NB):
                ob = o[:, b, :].rearrange("p (j n) -> p j n", n=P)
                V.tensor_tensor(ob, ob, rs[:, b, :].unsqueeze(2).broadcast_to([P, NH, P]), ALU.mult).then_inc(s_norm, 1)

        dve.wait_ge(hg_og, NH * NB)
        head_norms(0)
        dve.sem_inc(s_hn, 1)
        layer_norm(accb, A_HG)

        def mlp(g0, ts, width, off):
            for s, tt in enumerate(ts):
                g = g0 + s
                wait_act()
                if s >= 2:
                    dve.wait_ge(s_T, ts[s - 2] + 1)
                V.tensor_tensor(stage[:, g % 2, 0:width], half[:, g % 2, 0:width], up[:, g % 2, off:off + width],
                                ALU.mult).then_inc(s_st, 1)

        mlp(g_ff, t_ff, HALF, HALF)
        layer_norm(accb, A_FF)

        dve.wait_ge(s_small, SMALL)
        lr = lam[:, 0:256].rearrange("p (a n) -> p a n", a=4)
        link(V.tensor_tensor(lr[:, 0, :], lr[:, 0, :], lr[:, 1, :], ALU.mult))
        link(V.tensor_tensor(lr[:, 2, :], lr[:, 2, :], lr[:, 3, :], ALU.mult))
        link(V.tensor_reduce(lam[:, 256:257], lr[:, 0, :], AX.X, ALU.add))
        link(V.tensor_reduce(lam[:, 257:258], lr[:, 2, :], AX.X, ALU.add))
        dve.sem_inc(s_lbD, 1)
        dve.wait_ge(s_lbA, 1 + 2 * NB + 1)
        link(V.tensor_tensor(lam[:, 258:259], lam[:, 257:258], lam[:, 256:257], ALU.subtract))
        link(V.tensor_scalar(lam[:, 259:260], lam[:, 258:259], -LAM_INIT, None, ALU.add))
        nlam = lam[:, 259:260]
        dve.wait_ge(s_gn, 32)
        link(V.tensor_scalar(gn[:, :], gn[:, :], 1.0 - LAM_INIT, None, ALU.mult))
        tmp = flat(half[:, :, :]).rearrange("p (i u n) -> p i u n", i=4, u=8)
        for s in range(12):
            g, c, b = g_da + s, s // NB, s % NB
            dve.wait_ge(s_up, g + 1)
            src = up[:, g % 2, :]
            if c < 4:
                if s >= 2:
                    dve.wait_ge(s_T, t_da[s - 2] + 1)
                x = src.rearrange("p (u m n) -> p u m n", m=2, n=32)
                dst = stage[:, g % 2, :].rearrange("p (u m n) -> p u m n", m=2, n=32)
                cos, sin = (cst[:, k + 32 * b:k + 32 * b + 32].unsqueeze(1).broadcast_to([P, 8, 32]) for k in (C_COS, C_SIN))
                V.tensor_tensor(tmp[:, 0], x[:, :, 0, :], cos, ALU.mult)
                V.tensor_tensor(tmp[:, 1], x[:, :, 1, :], sin, ALU.mult)
                V.tensor_tensor(tmp[:, 2], x[:, :, 1, :], cos, ALU.mult)
                link(V.tensor_tensor(tmp[:, 3], x[:, :, 0, :], sin, ALU.mult))
                V.tensor_tensor(dst[:, :, 0, :], tmp[:, 0], tmp[:, 1], ALU.subtract)
                link(V.tensor_tensor(dst[:, :, 1, :], tmp[:, 2], tmp[:, 3], ALU.add))
                dve.sem_inc(s_st, 1)
            else:
                V.tensor_copy(v[:, b, (c - 4) * W:(c - 3) * W], src).then_inc(s_st, 1)

        NA = NH * NB

        def maxima(n, w):
            link(V.tensor_reduce(att[:, n % 2, 0:2], at_s[:, n % 2, :, 0:w], AX.X, ALU.max, negate=True))
            dve.sem_inc(at_sm, 1)

        for n in range(NA + 3):
            if n < NA:
                b = n % NB
                w = P * (b + 1)
                dve.wait_ge(at_S, n + 1)
                if n >= 2:
                    dve.wait_ge(at_e, n - 1)
                link(V.scalar_tensor_tensor(at_s[:, n % 2, :, 0:w],
                                            score_banks(n)[:, :, 0:w], 0.125,
                                            causal[:, SEQ - w:SEQ].unsqueeze(1).broadcast_to([P, 2, w]), ALU.mult, ALU.add))
                maxima(n, w)
            if 1 <= n <= NA:
                m = n - 1
                w = P * (m % NB + 1)
                dve.wait_ge(at_e, m + 1)
                if m >= 2:
                    dve.wait_ge(at_T, m - 1)
                a = att[:, m % 2, :]
                link(V.reciprocal(a[:, 4:6], a[:, 2:4]))
                link(V.tensor_scalar(a[:, 5:6], a[:, 5:6], nlam, None, ALU.mult))
                st = stage[:, m % 2, 0:w]
                link(V.tensor_scalar(st, at_p[:, m % 2, 0, 0:w], a[:, 4:5], None, ALU.mult))
                link(V.scalar_tensor_tensor(st, at_p[:, m % 2, 1, 0:w], a[:, 5:6], st, ALU.mult, ALU.add))
                dve.sem_inc(at_w, 1)
            if 3 <= n:
                m = n - 3
                j, b = m // NB, m % NB
                dve.wait_ge(at_sq, m + 1)
                V.tensor_tensor(o[:, b, j * P:(j + 1) * P], acc[:, m % 2, 0:P], gn[:, :], ALU.mult).then_inc(at_og, 1)
        dve.wait_ge(at_og, NA)
        head_norms(3)
        layer_norm(accb, A_DA)

        dve.wait_ge(s_rl, 1)
        L, one1, one2, w1, w2, tot, G = (rt[:, i] for i in range(7))
        d21 = rt[:, 7, :, 0:1]
        m1, m2, r1, r2 = (rt[:, 8 + i, :, 0:1] for i in range(4))
        key = cst[:, C_KEY:C_KEY + NE].unsqueeze(1).broadcast_to([P, NB, NE])
        wide = lambda a: a.broadcast_to([P, NB, NE])
        link(V.tensor_copy(L, up[:, 0, 0:NB * NE].rearrange("p (b n) -> p b n", b=NB)))
        for mx, r, oh, wk, src in ((m1, r1, one1, w1, L), (m2, r2, one2, w2, w1)):
            link(V.tensor_reduce(mx, src, AX.X, ALU.max))
            link(V.tensor_tensor(oh, src, wide(mx), ALU.is_equal))
            link(V.tensor_tensor(oh, oh, key, ALU.mult))
            link(V.tensor_reduce(r, oh, AX.X, ALU.max))
            link(V.tensor_tensor(oh, oh, wide(r), ALU.is_equal))
            if oh is one1:
                link(V.tensor_scalar(wk, oh, NEG, None, ALU.mult))
                link(V.tensor_tensor(wk, wk, src, ALU.add))
        link(V.tensor_tensor(d21, m1, m2, ALU.subtract))
        link(V.tensor_tensor(tot, one1, one2, ALU.add))
        dve.sem_inc(s_ra, 1)
        dve.wait_ge(s_rp, 1)
        link(V.tensor_tensor(G, one1, wide(d21), ALU.mult))
        link(V.tensor_scalar(d21, d21, -1.0, 1.0, ALU.mult, ALU.add))
        link(V.tensor_tensor(w1, one2, wide(d21), ALU.mult))
        link(V.tensor_tensor(gate[:, :, 0:NE], G, w1, ALU.add))
        dve.wait_ge(s_rl, 2)
        link(V.tensor_tensor(w2, tot, up[:, 1, 0:NB * NE].rearrange("p (b n) -> p b n", b=NB), ALU.mult))
        link(V.tensor_scalar(slot[:, :, 0:NE], w2, -1.0, None, ALU.add))
        over, rank = ex[:, 0, :], ex[:, 1, :]
        link(V.tensor_scalar(over, up[:, 1, NB * NE:(NB + 1) * NE], float(P), None, ALU.is_gt))
        link(V.tensor_copy(rank, over))
        for e in range(1, NE):
            link(V.tensor_tensor(rank[:, e:e + 1], rank[:, e - 1:e], over[:, e:e + 1], ALU.add))
        link(V.tensor_copy(extra[:, 0:1], rank[:, NE - 1:NE]))
        for j in range(MAX_EXTRA):
            oh, wk = ex[:, 2, :], rt[:, 12]
            ohw = oh.unsqueeze(1).broadcast_to([P, NB, NE])
            link(V.tensor_scalar(oh, rank, float(j + 1), None, ALU.is_equal))
            link(V.tensor_tensor(oh, oh, over, ALU.mult))
            link(V.tensor_tensor(ex[:, 3, :], oh, cst[:, C_EVAL:C_EVAL + NE], ALU.mult))
            link(V.tensor_reduce(extra[:, 1 + j:2 + j], ex[:, 3, :], AX.X, ALU.add))
            link(V.tensor_tensor(wk, w2, ohw, ALU.mult))
            link(V.tensor_reduce(slot[:, :, NE + j:NE + j + 1], wk, AX.X, ALU.add))
            link(V.tensor_scalar(slot[:, :, NE + j], slot[:, :, NE + j], -1.0 - P, None, ALU.add))
            link(V.tensor_tensor(wk, gate[:, :, 0:NE], ohw, ALU.mult))
            link(V.tensor_reduce(gate[:, :, NE + j:NE + j + 1], wk, AX.X, ALU.add))
        link(V.tensor_copy(extra_i[:, :], extra[:, :]))
        for b in range(NB):
            ins = V.tensor_scalar(y[:, b, :], h[:, b, :], ALPHA, None, ALU.mult)
        link(ins)
        dve.sem_inc(s_rd, 1)

        def expert(m, i, first):
            dve.wait_ge(m["gath"], i * 2 + 1)
            dve.wait_ge(m["turned"], i + 1)
            for b in range(NB):
                V.tensor_scalar(pick[:, b, :], iota, slot[:, b, bass.ds(i + first, 1)], None, ALU.is_equal)
            for b in range(NB):
                ins = V.tensor_scalar(give[:, b, :], iota, slot[:, b, bass.ds(i + first, 1)],
                                      gate[:, b, bass.ds(i + first, 1)], ALU.is_equal, ALU.mult)
            ins.then_inc(m["picked"], 1)

            def split(x):
                dve.wait_ge(m["hi"], i * NHALF + (x + 1))
                V.tensor_tensor(wl[:, x % SPLITS, :], raw[:, x % RAW, :],
                                wh[:, x % SPLITS, :].bitcast(F32), ALU.subtract).then_inc(m["lo"], 1)

            split(0)
            split(1)
            for q in range(2):
                dve.wait_ge(m["xgh"], i * 2 + (q + 1))
                V.tensor_tensor(xgl[:, 4 * q:4 * q + 4, :], tp[:, q, :].rearrange("p (k n) -> p k n", k=4),
                                xgh[:, 4 * q:4 * q + 4, :].bitcast(F32), ALU.subtract).then_inc(m["xg"], 1)
            split(2)
            for s in range(EU + 1):
                if s > 0:
                    dve.wait_ge(m["Th"], i * EU + s)
                    V.tensor_tensor(hTl[:, (s - 1) % 2, :], tp[:, (s - 1) % 2, 0:HALF],
                                    hTh[:, (s - 1) % 2, :].bitcast(F32), ALU.subtract).then_inc(m["Te"], 1)
                if 1 <= s < EU - 1:
                    split(gate_half(s + 1, 0))
                if s == EU:
                    break
                dve.wait_ge(m["act"], i * EU + (s + 1))
                if s >= 2:
                    dve.wait_ge(m["T"], i * EU + (s - 1))
                V.tensor_tensor(stage[:, s % 2, 0:HALF], half[:, s % 2, 0:HALF], up[:, s % 2, HALF:W],
                                ALU.mult).then_inc(m["st"], 1)
                if s < EU - 1:
                    split(gate_half(s + 1, 1))
                split(down_half(s))
            for n in range(4):
                dve.wait_ge(m["give"], i * 4 + (n + 1))
                dve.wait_ge(m["added"], i * 4 + 1)
                yb = y[:, n // 2, (n % 2) * W:(n % 2 + 1) * W]
                V.tensor_tensor(yb, yb, acc[:, 2 + n % 2, :], ALU.add).then_inc(m["added"], 1)

        for m in moe:
            dve.sem_inc(m["added"], 1)
            dve.sem_inc(m["Te"], 1)
            dve.sem_inc(m["lo"], RAW)
        with dve.Fori(0, NE) as i:
            expert(moe[0], i, 0)
        dve.wait_ge(moe[0]["added"], 4 * NE + 1)
        n_extra = dve.value_load(extra_i[0:1, 0:1], min_val=0, max_val=MAX_EXTRA)
        with dve.If(n_extra > 0):
            with dve.Fori(0, n_extra) as j:
                expert(moe[1], j, NE)
            dve.wait_ge(moe[1]["added"], n_extra * 4 + 1)
            dve.sem_inc(s_xdone, 1)
        layer_norm(y)

        def rms(dst, src_ready):
            for b in range(NB):
                if src_ready:
                    dve.sem_inc(s_nD, 1)
                    nst[0] += 1
                nst[1] += 1
                dve.wait_ge(s_nA, nst[1])
                r = root(b, sc[:, b, 2:3], 1.0 / D, RMS_EPS)
                V.tensor_scalar(dst[:, b, :], h[:, b, :], r, None, ALU.mult).then_inc(s_norm, 1)

        def to_channels(t0, *dsts):
            for b in range(NB):
                for q in range(2):
                    tt = t0 + 2 * b + q
                    dve.wait_ge(s_T, tt + 1)
                    if tt == t0:
                        dve.wait_ge(s_Te, tt)
                    src = tp[:, tt % 2, :].rearrange("p (k n) -> p k n", k=4)
                    for dst, gain in dsts:
                        ins = V.tensor_tensor(dst[:, 4 * q:4 * q + 4, b * P:(b + 1) * P], src,
                                              cols[:, gain, 4 * q:4 * q + 4].unsqueeze(2).broadcast_to([P, 4, P]), ALU.mult)
                    ins.then_inc(s_Te, 1)

        hn = o

        link(V.memset(uT[:, :, 0:PADC], 0.0))
        rms(hn, True)
        to_channels(T_cv, (xT, 0))
        nrows[0] += 32
        dve.wait_ge(s_rows, nrows[0])
        r2 = rows[:, :].rearrange("p (m n) -> p m n", m=2)
        for s in range(8):
            g, c, b = g_cv + s, s // NB, s % NB
            dve.wait_ge(s_up, g + 1)
            hf = half[:, g % 2, :]
            link(V.tensor_tensor(hf.rearrange("p (m n) -> p m n", m=2), up[:, g % 2, :].rearrange("p (m n) -> p m n", m=2),
                                 r2[:, :, c * HALF:(c + 1) * HALF], ALU.add))
            dve.sem_inc(cv_n, 1)
            wait_act()
            if s >= 2:
                dve.wait_ge(s_T, t_cv[s - 2] + 1)
            V.tensor_tensor(stage[:, g % 2, 0:HALF], hf[:, 0:HALF], hf[:, HALF:W], ALU.mult).then_inc(s_st, 1)
        dve.sem_inc(s_rows_free, 1)
        dve.wait_ge(s_Te, T_cback)
        for j in range(CONV):
            for k in range(KT):
                src = uT[:, k, j:j + SEQ]
                if j == 0:
                    ins = V.tensor_scalar(cT[:, k, :], src, wdw[:, k, 0:1], rowcols[:, 0, k:k + 1], ALU.mult, ALU.add)
                else:
                    ins = V.scalar_tensor_tensor(cT[:, k, :], src, wdw[:, k, j:j + 1], cT[:, k, :], ALU.mult, ALU.add)
            link(ins)
        dve.sem_inc(cv_dw, 1)
        for b in range(NB):
            dve.wait_ge(s_Te, T_cback + 2 * b + 2)
            r = root(b, stats(b, ctm[:, b, :]), 1.0, RMS_EPS)
            V.tensor_scalar(ctm[:, b, :], ctm[:, b, :], mv[:, b, 0:1], r, ALU.subtract, ALU.mult).then_inc(s_norm, 1)
        nrows[0] += 32
        dve.wait_ge(s_rows, nrows[0])
        for b in range(NB):
            dve.wait_ge(s_acc, A_PW2 + b + 1)
            ins = V.tensor_tensor(h[:, b, :], accb[:, b, :], rows[:, 0:D], ALU.add)
        link(ins)

        for i, d in enumerate(after):
            if i == 1:
                rms(hn, True)
                to_channels(d["T_q"], (xT, 1), (x2, 2))
                for s in range(8):
                    g, c, b = d["g_kv"] + s, s // NB, s % NB
                    dve.wait_ge(s_up, g + 1)
                    if c < 2:
                        if s >= 2:
                            dve.wait_ge(s_T, d["t_kv"][s - 2] + 1)
                        dst = stage[:, g % 2, :]
                    else:
                        dst = v[:, b, (c - 2) * W:(c - 1) * W]
                    V.tensor_copy(dst, up[:, g % 2, :]).then_inc(s_st, 1)
                for b in range(NB):
                    g = d["g_f"] + b
                    dve.wait_ge(s_up, g + 1)
                    V.tensor_tensor(fx[:, 0, b, :], up[:, g % 2, 0:NH2], bf[:, :], ALU.add).then_inc(s_st, 1)
                dve.wait_ge(s_st, d["g_f"] + NB)
                dve.sem_inc(f_D, 1)
                link(V.tensor_scalar(fx[:, 3], fx[:, 0], 0.0, None, ALU.min))
                dve.wait_ge(f_A, 1)
                link(V.tensor_tensor(fx[:, 4], fx[:, 3], fx[:, 2], ALU.subtract))
                dve.sem_inc(f_D, 1)
                for s in range(4):
                    g = d["g_q"] + s
                    dve.wait_ge(s_up, g + 1)
                    if s >= 2:
                        dve.wait_ge(s_T, d["t_q"][s - 2] + 1)
                    V.tensor_scalar(stage[:, g % 2, :], up[:, g % 2, :], HD2 ** -0.5, None, ALU.mult).then_inc(s_st, 1)
                dve.wait_ge(f_C, 1)
                cb = fx[:, 5]
                link(V.tensor_copy(cb, up[:, 0, 0:NB * NH2].rearrange("p (b n) -> p b n", b=NB)))
                dve.sem_inc(f_D, 1)
                for n in range(NA + 3):
                    if n < NA:
                        j, b = n // NB, n % NB
                        w = P * (b + 1)
                        dve.wait_ge(at_S, NA + n + 1)
                        if n >= 2:
                            dve.wait_ge(at_e, NA + n - 1)
                        for c in range(2):
                            ins = V.scalar_tensor_tensor(at_s[:, n % 2, c, 0:w], score_banks(n)[:, c, 0:w],
                                                         cb[:, b, 2 * j + c:2 * j + c + 1], causal[:, SEQ - w:SEQ],
                                                         ALU.add, ALU.add)
                        link(ins)
                        maxima(n, w)
                    if 3 <= n:
                        m = n - 3
                        j, b = m // NB, m % NB
                        dve.wait_ge(at_O, NA + m + 1)
                        a = fx[:, 6, 0, 2 * (m % 4):2 * (m % 4) + 2]
                        V.tensor_tensor(o[:, b, j * P:(j + 1) * P].rearrange("p (c n) -> p c n", c=2),
                                        acc[:, m % 2, 0:P].rearrange("p (c n) -> p c n", c=2),
                                        a.unsqueeze(2).broadcast_to([P, 2, HD2]), ALU.mult).then_inc(at_og, 1)
                    if 1 <= n <= NA:
                        m = n - 1
                        dve.wait_ge(at_e, NA + m + 1)
                        link(V.reciprocal(fx[:, 6, 0, 2 * (m % 4):2 * (m % 4) + 2], att[:, m % 2, 2:4]))
                        dve.sem_inc(at_w, 1)
                dve.wait_ge(at_og, 2 * NA)
                dve.sem_inc(s_norm, NB)
                rms(hn, False)
            else:
                rms(hn, True)
            to_channels(d["T_f"], (xT, 3 + i))
            mlp(d["g_ff"], d["t_ff"], W, 0)
            rms(hn, False)
            dve.wait_ge(s_pe, 16 if i == 0 else 48)
            to_channels(d["T_g"], (xT, 5))
            for s in range(4):
                g, c, b = d["g_p"] + s, s // NB, s % NB
                wait_act()
                link(V.tensor_tensor(stage[:, g % 2, :], half[:, g % 2, :], acc[:, g % 2, :], ALU.mult))
                hb = h[:, b, c * W:(c + 1) * W]
                link(V.tensor_tensor(hb, hb, stage[:, g % 2, :], ALU.add))
                dve.sem_inc(s_st, 1)
            dve.sem_inc(s_norm, NB)
        for b in range(NB):
            dve.sem_inc(s_nD, 1)
            nst[0] += 1
            nst[1] += 1
            dve.wait_ge(s_nA, nst[1])
            r = root(b, sc[:, b, 2:3], 1.0 / D, RMS_EPS)
            V.scalar_tensor_tensor(o[:, b, :], h[:, b, :], r, rows[:, D:2 * D], ALU.mult, ALU.mult).then_inc(s_norm, 1)

    @block.tensor
    def _(pe):
        mm = nc.tensor.matmul

        def chunk_ready(c):
            pe.wait_ge(w_ready[c % RING], pl.chunk_ready[c])

        def chunk_done(c, ins):
            ins.then_inc(w_free[c % RING], 1)

        def turn_bank(tt):
            if tt >= 2:
                pe.wait_ge(s_Te, tt - 1)

        def turn_rows(t0, src, ready):
            for b in range(NB):
                ready(b)
                for q in range(2):
                    tt = t0 + 2 * b + q
                    turn_bank(tt)
                    for k in range(4):
                        ins = nc.tensor.transpose(tp[:, tt % 2, k * P:(k + 1) * P],
                                                  src[:, b, (4 * q + k) * P:(4 * q + k + 1) * P], ident)
                    ins.then_inc(s_T, 1)

        def normed(n):
            return lambda b: pe.wait_ge(s_norm, n + b + 1)

        def products(out, lhs, b, rhs, ks, last):
            for k in ks:
                ins = mm(out, lhs[:, k, b * P:(b + 1) * P], rhs[:, k, :], start=(k == 0), stop=(k == last))
            return ins

        def turn_step(g, tt, nk):
            pe.wait_ge(s_st, g + 1)
            turn_bank(tt)
            for k in range(nk):
                ins = nc.tensor.transpose(tp[:, tt % 2, k * P:(k + 1) * P], stage[:, g % 2, k * P:(k + 1) * P], ident)
            ins.then_inc(s_T, 1)

        def xT_ready(b, t0):
            pe.wait_ge(s_Te, t0 + 2 * b + 2)

        def project(g0, ts, chunks, lhs, t0, nk, down=None):
            total = len(chunks) * NB
            for s in range(total + 1):
                g = g0 + s
                if s < total:
                    c, b = chunks[s // NB], s % NB
                    if s < NB and t0 is not None:
                        xT_ready(b, t0)
                    if b == 0:
                        chunk_ready(c)
                    if g >= 2:
                        pe.wait_ge(s_st, g - 1)
                    products(up[:, g % 2, :], lhs, b, ring_k(c), range(0, 4), 7)
                if s >= 1 and ts[s - 1] is not None:
                    turn_step(g - 1, ts[s - 1], nk)
                if s < total:
                    ins = products(up[:, g % 2, :], lhs, b, ring_k(c), range(4, 8), 7)
                    ins.then_inc(s_up, 1)
                    if b == NB - 1:
                        pe.wait_ge(s_up, g + 1)
                        pe.sem_inc(w_free[c % RING], 1)
                if down is not None and s >= 1:
                    down(s - 1)

        def residual(scale):
            for b in range(NB):
                for n in range(2):
                    mm(acc[:, 2 * b + n, :], scale, h[:, b, n * W:(n + 1) * W], start=True, stop=False)

        def out_product(c0, t0, scale):
            residual(scale)
            for b in range(NB):
                xT_ready(b, t0)
                for n in range(2):
                    chunk_ready(c0 + n)
                    for k in range(KT):
                        ins = mm(acc[:, 2 * b + n, :], xT[:, k, b * P:(b + 1) * P], ring_k(c0 + n)[:, k, :],
                                 start=False, stop=(k == KT - 1))
                    if b == NB - 1:
                        chunk_done(c0 + n, ins)
                    elif n == 1:
                        ins.then_inc(s_acc, 1)
            pe.wait_ge(w_free[(c0 + 1) % RING], pl.chunk_use[c0 + 1] + 1)
            pe.sem_inc(s_acc, 1)

        def mlp_down(ts, down_chunk, tiles, per, last_free):
            total = len(ts)

            def down(s):
                b, u = s % NB, s // NB
                c, row = down_chunk(u)
                pe.wait_ge(s_Te, ts[s] + 1)
                if b == 0:
                    chunk_ready(c)
                for n in range(2):
                    for k in range(per):
                        ins = mm(acc[:, 2 * b + n, :], hT[:, s % 2, k * P:(k + 1) * P],
                                 ring_k(c, 4)[:, row + k, n * W:(n + 1) * W], start=False,
                                 stop=(u == total // NB - 1 and k == per - 1))
                if u == total // NB - 1:
                    ins.then_inc(s_acc, 1)
                if b == NB - 1 and last_free(u):
                    if u == total // NB - 1:
                        pe.wait_ge(s_acc, accs[0] + NB)
                        pe.sem_inc(w_free[c % RING], 1)
                    else:
                        chunk_done(c, ins)
            return down

        accs = [0]

        pe.wait_ge(s_cst, 32)
        turn_rows(T_x, h, lambda b: pe.wait_ge(s_x, 16))
        project(g_hg, t_hg, [c_hg + i for i in range(8)], xT, T_x, 4)
        pe.wait_ge(s_lbA, 1 + 2 * NB)
        lev = big[:, H_LEV:H_END]
        for n in range(NH * NB + 2):
            if n < NH * NB:
                j, b = n // NB, n % NB
                if n >= 1:
                    pe.wait_ge(hg_ab, n)
                for q in range(2):
                    ins = mm(acc[:, q, :], lf[:, b, j * P:(j + 1) * P], lev[:, b * P + q * W:b * P + (q + 1) * W],
                             start=True, stop=True)
                ins.then_inc(hg_m, 1)
            if 1 <= n <= NH * NB:
                m = n - 1
                j, b = m // NB, m % NB
                first = 1 - b
                pe.wait_ge(hg_ab, m + 1)
                if m >= 1:
                    pe.wait_ge(hg_sm, m)
                A, B = hgA[:, m % 2], hgB[:, m % 2]
                if b == 1:
                    if m >= 4:
                        pe.wait_ge(hg_sm, m - 3)
                    mm(tp[:, j % 2, 0:P], hgB[:, 0, 0, :], A[:, 7, :], start=True, stop=True)
                for l in range(7):
                    mm(acc[:, 2 + l // 4, (l % 4) * P:(l % 4 + 1) * P], B[:, first + l, :], A[:, first + l, :],
                       start=True, stop=True)
                qk = slice(b * P, (b + 1) * P)
                mm(acc[:, 3, 3 * P:4 * P], kT[:, j, qk], qT[:, j, qk], start=True, stop=True).then_inc(hg_s, 1)
            if 2 <= n:
                m = n - 2
                j, b = m // NB, m % NB
                pe.wait_ge(hg_sm, m + 1)
                if m >= 2:
                    pe.wait_ge(hg_og, m - 1)
                if b == 1:
                    mm(up[:, m % 2, 0:P], hgX, v[:, 0, j * P:(j + 1) * P], start=True, stop=False)
                for l in range(8):
                    ins = mm(up[:, m % 2, 0:P], hgS[:, l, :], v[:, b, j * P:(j + 1) * P], start=(l == 0 and b == 0),
                             stop=(l == 7))
                ins.then_inc(hg_o, 1)
        turn_rows(T_hgo, o, normed(N_HGO))
        out_product(c_hgo, T_hgo, aident)
        accs[0] += NB

        def swiglu_chunk(u):
            return ff_d[u], 2 * (u % 2)

        turn_rows(T_ff, h, normed(N_LN0))
        residual(aident)
        project(g_ff, t_ff, ff_gu, xT, T_ff, 2,
                mlp_down(t_ff, swiglu_chunk, 2, 2, lambda u: u % 2 == 1 or u == FF_UNITS - 1))
        accs[0] += NB

        turn_rows(T_da, h, normed(N_LN1))
        project(g_da, t_da, [c_da + i for i in range(6)], xT, T_da, 4)
        NA = NH * NB

        def attention(base, scores, turns, outs):
            for n in range(NA + 2):
                if n < NA:
                    if n >= 2:
                        pe.wait_ge(at_sm, base + n - 1)
                    scores(n, n // NB, n % NB).then_inc(at_S, 1)
                if 1 <= n <= NA:
                    m = n - 1
                    pe.wait_ge(at_w, base + m + 1)
                    if m >= 2:
                        pe.wait_ge(at_Te, base + m - 1)
                    turns(m, m % NB).then_inc(at_T, 1)
                if 2 <= n:
                    m = n - 2
                    pe.wait_ge(at_Te, base + m + 1)
                    if m >= 2:
                        pe.wait_ge(at_og, base + m - 1)
                    outs(m, m // NB, m % NB).then_inc(at_O, 1)

        def da_scores(n, j, b):
            for c in range(2):
                r = slice(64 * c, 64 * c + 64)
                ins = mm(score_banks(n)[:, c, 0:P * (b + 1)], qT[r, j, b * P:(b + 1) * P], kT[r, j, 0:P * (b + 1)],
                         start=True, stop=True)
            return ins

        def da_turns(m, b):
            for kb in range(b + 1):
                ins = nc.tensor.transpose(tp[:, m % 2, kb * P:(kb + 1) * P], stage[:, m % 2, kb * P:(kb + 1) * P], ident)
            return ins

        def da_outs(m, j, b):
            for kb in range(b + 1):
                ins = mm(acc[:, m % 2, 0:P], hT[:, m % 2, kb * P:(kb + 1) * P], v[:, kb, j * P:(j + 1) * P],
                         start=(kb == 0), stop=(kb == b))
            return ins

        pe.wait_ge(s_Te, T_dao)
        pe.wait_ge(s_st, g_da + 12)
        attention(0, da_scores, da_turns, da_outs)
        turn_rows(T_dao, o, normed(N_DAO))
        out_product(c_dao, T_dao, aident)
        accs[0] += NB

        turn_rows(T_moe, h, normed(N_LN2))
        pe.wait_ge(s_small, SMALL)
        for b in range(NB):
            xT_ready(b, T_moe)
            for k in range(KT):
                ins = mm(up[:, 0, b * NE:(b + 1) * NE], xT[:, k, b * P:(b + 1) * P], wr[:, k, :],
                         start=(k == 0), stop=(k == KT - 1))
        ins.then_inc(s_rl, 1)
        pe.wait_ge(s_ra, 1)
        tot = rt[:, 5]
        mm(up[:, 1, 0:NE], tri, tot[:, 0, :], start=True, stop=True)
        mm(up[:, 1, NE:2 * NE], ones, tot[:, 0, :], start=True, stop=False)
        mm(up[:, 1, NE:2 * NE], tri, tot[:, 1, :], start=False, stop=True)
        mm(up[:, 1, 2 * NE:3 * NE], ones, tot[:, 0, :], start=True, stop=False)
        mm(up[:, 1, 2 * NE:3 * NE], ones, tot[:, 1, :], start=False, stop=True).then_inc(s_rl, 1)

        def split_product(out, x_hi, x_lo, w_hi, w_lo, start, stop):
            mm(out, x_hi, w_hi, start=start, stop=False)
            mm(out, x_hi, w_lo, start=False, stop=False)
            return mm(out, x_lo, w_hi, start=False, stop=stop)

        def expert(m, i):
            pe.wait_ge(m["picked"], i + 1)
            pe.wait_ge(m["Te"], i * EU + 1)
            for q in range(2):
                for k in range(4 * q, 4 * q + 4):
                    for b in range(NB):
                        ins = mm(tp[:, q, (k % 4) * P:(k % 4 + 1) * P], h[:, b, k * P:(k + 1) * P], pick[:, b, :],
                                 start=(b == 0), stop=(b == NB - 1))
                ins.then_inc(m["gath"], 1)
            pe.wait_ge(m["added"], i * 4 + 1)
            for b in range(NB):
                ins = nc.tensor.transpose(acc[:, 2, b * P:(b + 1) * P], give[:, b, :], ident)
            ins.then_inc(m["turned"], 1)
            def split_ready(x):
                pe.wait_ge(m["lo"], i * NHALF + (RAW + x + 1))

            def gate_up(s, part):
                x = gate_half(s, part)
                split_ready(x)
                w_hi, w_lo = (w[:, x % SPLITS, :].rearrange("p (k n) -> p k n", k=4) for w in (wh, wl))
                for k in range(4):
                    kk = 4 * part + k
                    ins = split_product(up[:, s % 2, :], xgh[:, kk, :], xgl[:, kk, :], w_hi[:, k, :], w_lo[:, k, :],
                                        kk == 0, kk == KT - 1)
                return ins

            for s in range(EU + 1):
                if s < EU:
                    if s >= 2:
                        pe.wait_ge(m["st"], i * EU + (s - 1))
                    if s == 0:
                        pe.wait_ge(m["xg"], i * 2 + 1)
                    gate_up(s, 0).then_inc(m["used"], 1)
                if s >= 1:
                    pe.wait_ge(m["st"], i * EU + s)
                    if s >= 3:
                        pe.wait_ge(m["Te"], i * EU + (s - 1))
                    for k in range(2):
                        ins = nc.tensor.transpose(tp[:, (s - 1) % 2, k * P:(k + 1) * P],
                                                  stage[:, (s - 1) % 2, k * P:(k + 1) * P], ident)
                    ins.then_inc(m["T"], 1)
                if s < EU:
                    if s == 0:
                        pe.wait_ge(m["xg"], i * 2 + 2)
                    gate_up(s, 1).then_inc(m["up"], 1)
                if s >= 1:
                    u = s - 1
                    x = down_half(u)
                    split_ready(x)
                    w_hi, w_lo = (w[:, x % SPLITS, :].rearrange("p (k n) -> p k n", k=2) for w in (wh, wl))
                    pe.wait_ge(m["Te"], i * EU + (s + 1))
                    if u == 0:
                        pe.wait_ge(m["ye"], i + 1)
                    for n in range(2):
                        for k in range(2):
                            t_, c_ = slice(k * P, (k + 1) * P), slice(n * W, (n + 1) * W)
                            ins = split_product(acc[:, n, :], hTh[:, u % 2, t_], hTl[:, u % 2, t_], w_hi[:, k, c_],
                                                w_lo[:, k, c_], u == 0 and k == 0, u == EU - 1 and k == 1)
                    ins.then_inc(m["down"] if u == EU - 1 else m["used"], 1)
            pe.wait_ge(m["ye"], i + 2)
            pe.wait_ge(m["giveT"], i + 1)
            for n in range(4):
                if n >= 2:
                    pe.wait_ge(m["added"], i * 4 + n)
                mm(acc[:, 2 + n % 2, :], giveT[:, n // 2, :], ye[:, (n % 2) * W:(n % 2 + 1) * W],
                   start=True, stop=True).then_inc(m["give"], 1)

        for m in moe:
            pe.sem_inc(m["gath"], 1)
            pe.sem_inc(m["turned"], 1)
        with pe.Fori(0, NE) as i:
            expert(moe[0], i)
        pe.wait_ge(s_rd, 1)
        n_extra = pe.value_load(extra_i[0:1, 0:1], min_val=0, max_val=MAX_EXTRA)
        with pe.If(n_extra > 0):
            with pe.Fori(0, n_extra) as j:
                expert(moe[1], j)

        turn_rows(T_cv, o, normed(N_RC))
        project(g_cv, t_cv, [c_pw1 + i for i in range(4)], xT, T_cv, 2)
        pe.wait_ge(cv_dw, 1)
        for b in range(NB):
            for q in range(2):
                tt = T_cback + 2 * b + q
                turn_bank(tt)
                for k in range(4):
                    ins = nc.tensor.transpose(tp[:, tt % 2, k * P:(k + 1) * P], cT[:, 4 * q + k, b * P:(b + 1) * P], ident)
                ins.then_inc(s_T, 1)
        turn_rows(T_cn, ctm, normed(N_CB))
        out_product(c_pw2, T_cn, ident)
        accs[0] += NB

        for i, d in enumerate(after):
            if i == 1:
                turn_rows(d["T_q"], o, normed(N_AFTER[i]["q"]))
                project(d["g_kv"], d["t_kv"], [d["c_k"] + c for c in range(4)], x2, d["T_q"], 4)
                for b in range(NB):
                    g = d["g_f"] + b
                    pe.wait_ge(s_st, g - 1)
                    for k in range(KT):
                        ins = mm(up[:, g % 2, 0:NH2], x2[:, k, b * P:(b + 1) * P], wf[:, k, :],
                                 start=(k == 0), stop=(k == KT - 1))
                    ins.then_inc(s_up, 1)
                project(d["g_q"], d["t_q"], [d["c_q"] + c for c in range(2)], xT, None, 4)
                pe.wait_ge(f_D, 2)
                pe.wait_ge(s_Te, d["T_o"])
                lg = fx[:, 4]
                mm(up[:, 0, 0:NH2], tri, lg[:, 0, :], start=True, stop=True)
                mm(up[:, 0, NH2:2 * NH2], ones, lg[:, 0, :], start=True, stop=False)
                mm(up[:, 0, NH2:2 * NH2], tri, lg[:, 1, :], start=False, stop=True).then_inc(f_C, 1)
                pe.wait_ge(f_D, 3)
                for b in range(NB):
                    ins = nc.tensor.transpose(tp[0:NH2, 0, b * P:(b + 1) * P], fx[:, 5, b, :], ident)
                ins.then_inc(f_CT, 1)
                pe.wait_ge(f_ct, 1)
                pe.wait_ge(s_headrow, 16)

                def fox_scores(n, j, b):
                    w = P * (b + 1)
                    for c in range(2):
                        r = slice(64 * c, 64 * c + 64)
                        out = score_banks(n)[:, c, 0:w]
                        mm(out, qT[r, j, b * P:(b + 1) * P], kT[r, j, 0:w], start=True, stop=False)
                        ins = mm(out, headrow[:, 2 * j + c, :], ncT[:, 0:w], start=False, stop=True)
                    return ins

                def fox_turns(m, b):
                    for c in range(2):
                        for kb in range(b + 1):
                            at = (c * (b + 1) + kb) * P
                            ins = nc.tensor.transpose(tp[:, m % 2, at:at + P], at_p[:, m % 2, c, kb * P:(kb + 1) * P], ident)
                    return ins

                def fox_outs(m, j, b):
                    for c in range(2):
                        for kb in range(b + 1):
                            at = (c * (b + 1) + kb) * P
                            ins = mm(acc[:, m % 2, c * HD2:(c + 1) * HD2], hT[:, m % 2, at:at + P],
                                     v[:, kb, (2 * j + c) * HD2:(2 * j + c + 1) * HD2], start=(kb == 0), stop=(kb == b))
                    return ins

                attention(NA, fox_scores, fox_turns, fox_outs)
                turn_rows(d["T_o"], o, normed(N_AFTER[i]["o"]))
                out_product(d["c_o"], d["T_o"], ident)
                accs[0] += NB
            turn_rows(d["T_f"], o, normed(N_AFTER[i]["f"]))
            residual(ident)
            project(d["g_ff"], d["t_ff"], [d["c_f"] + 2 * u for u in range(8)], xT, d["T_f"], 4,
                    mlp_down(d["t_ff"], lambda u: (d["c_f"] + 2 * u + 1, 0), 4, 4, lambda u: True))
            accs[0] += NB
            pe.wait_ge(s_pe, 16 if i == 0 else 48)
            turn_bank(d["T_p"])
            for k in range(2):
                for b in range(NB):
                    ins = nc.tensor.transpose(tp[:, d["T_p"] % 2, (2 * k + b) * P:(2 * k + b + 1) * P],
                                              pe_tm[:, b, k * P:(k + 1) * P], ident)
            ins.then_inc(s_T, 1)
            turn_rows(d["T_g"], o, normed(N_AFTER[i]["g"]))
            for s in range(4):
                g, c, b = d["g_p"] + s, s // NB, s % NB
                if s < NB:
                    xT_ready(b, d["T_g"])
                pe.wait_ge(s_st, g - 1)
                if s == 0:
                    chunk_ready(d["c_p"])
                for k in range(2):
                    ins = mm(acc[:, g % 2, :], pe_T[:, k, b * P:(b + 1) * P], ring_k(d["c_p"], 4)[:, k, c * W:(c + 1) * W],
                             start=(k == 0), stop=(k == 1))
                if s == 3:
                    chunk_done(d["c_p"], ins)
                if b == 0:
                    chunk_ready(d["c_p"] + 1 + c)
                products(up[:, g % 2, :], xT, b, ring_k(d["c_p"] + 1 + c), range(KT), 7).then_inc(s_up, 1)
                if b == NB - 1:
                    pe.wait_ge(s_up, g + 1)
                    pe.sem_inc(w_free[(d["c_p"] + 1 + c) % RING], 1)


USED = ["x", "hg_w_in", "hg_lb", "hg_norm_g", "hg_w_out", "da_w_in", "da_lam", "da_norm_g", "da_w_out",
        "ffn_w_gate", "ffn_w_up", "ffn_w_down", "moe_w_router", "moe_w_gate", "moe_w_up", "moe_w_down",
        "ln_g", "ln_b", "p_2", "mix_norm_2", "conv_w_pw1_2", "conv_b_pw1_2", "conv_w_dw_2", "conv_b_dw_2",
        "conv_ln_g_2", "conv_ln_b_2", "conv_w_pw2_2", "conv_b_pw2_2", "kv_norm_2", "w_kvf_2", "b_f_2",
        "attn_w_q_2", "attn_w_o_2", "ffn_norm_2", "ffn_w1_2", "ffn_w2_2", "ple_norm_2", "ple_w_gate_2",
        "ple_w_proj_2", "final_norm_2"]


def declare(nc, inputs):
    arrays, t = {}, {}
    consts, hg_tables = constant_table()
    given = {n: inputs[n] for n in USED} | {"consts": consts, "hg_tables": hg_tables, "headrow": head_rows()}
    for name, a in given.items():
        a = np.ascontiguousarray(a)
        arrays[f"in_{name}"] = a
        t[name] = nc.dram_tensor(f"in_{name}", a.shape, mybir.dt.from_np(a.dtype), kind="ExternalInput").ap()
    t["out"] = nc.dram_tensor("out", (1, SEQ, D), F32, kind="ExternalOutput").ap()
    build(nc, t)
    return arrays


def kernel(**inputs):
    import concourse.bacc as _bacc
    from concourse.bass_utils import run_bass_kernel_spmd as _run

    nc = _bacc.Bacc("TRN2", target_bir_lowering=False, num_devices=1)
    arrays = declare(nc, inputs)
    return _run(nc, [arrays], core_ids=[0]).results[0]["out"]
```

```python
import math
from contextlib import ExitStack

import numpy as np

import concourse.bass as bass
from concourse import mybir

P = 128
D = 1024
SEQ = 256
NB = SEQ // P
KT = D // P
NH = 8
DEPTH = 2
W = 512
HALF = W // 2
D_FF, D_FFE, D_FF2 = 2816, 3584, 4096
NE = 8
NH2, HD2 = 16, 64
D_PLE = 256
CONV = 31
LN_EPS, RMS_EPS = 1e-5, 1e-6
ALPHA = (2 * DEPTH) ** 0.25
LAM_INIT = 0.8 - 0.6 * math.exp(-0.3)
NEG = -1e30
RING = 3
RAW = 6
SPLITS = 3
CH = KT * W
MAX_EXTRA = SEQ * 2 // (P + 1)

F32 = mybir.dt.float32
F32R = mybir.dt.float32r
I32 = mybir.dt.int32
ALU = mybir.AluOpType
ACT = mybir.ActivationFunctionType
AX = mybir.AxisListType

C_ID, C_AID, C_CAUS = 0, P, 2 * P
C_COS = C_CAUS + 2 * P
C_SIN = C_COS + NB * 32
C_IOTA = C_SIN + NB * 32
C_KEY = C_IOTA + P
C_EVAL = C_KEY + NE
C_ONES = C_EVAL + NE
C_END = C_ONES + P
H_MASK, H_LEV, H_TRI, H_END = 0, 8 * P, 16 * P, 17 * P
LEVELS = [64, 32, 16, 8, 4, 2, 1]


def constant_table():
    c = np.zeros((P, C_END), np.float32)
    i = np.arange(P)
    c[:, C_ID:C_ID + P] = np.eye(P)
    c[:, C_AID:C_AID + P] = ALPHA * np.eye(P)
    u, t = i[:, None], i[None, :]
    lev = [(u > t)]
    mask = []
    for h in LEVELS:
        right = t % (2 * h) >= h
        mid = t // (2 * h) * (2 * h) + h
        lev.append(np.where(right, (u >= mid) & (u <= t), (u > t) & (u < mid)))
        mask.append((u // (2 * h) == t // (2 * h)) & right & (u % (2 * h) < h))
    lev.append(u <= t)
    mask.append(u == t)
    hg = np.concatenate(mask + lev, 1).astype(np.float32)
    c[:, C_CAUS + P:C_CAUS + 2 * P] = np.where(t <= u, 0.0, NEG)
    inv = (10000.0 ** (-np.arange(32, dtype=np.float32) / 32)).astype(np.float32)
    ang = (np.arange(SEQ, dtype=np.float32)[:, None] * inv[None, :]).astype(np.float32)
    for b in range(NB):
        c[:, C_COS + 32 * b:C_COS + 32 * b + 32] = np.cos(ang[b * P:b * P + P])
        c[:, C_SIN + 32 * b:C_SIN + 32 * b + 32] = np.sin(ang[b * P:b * P + P])
    c[:, C_IOTA:C_IOTA + P] = t
    c[:, C_KEY:C_KEY + NE] = NE - np.arange(NE)
    c[:, C_EVAL:C_EVAL + NE] = np.arange(NE)
    c[:, C_ONES:C_ONES + P] = 1.0
    return c, hg


def head_rows():
    return np.repeat(np.eye(NH2, dtype=np.float32)[:, :, None], P, 2)


class Plan:

    def __init__(self):
        self.steps = self.turns = self.chunk = 0
        self.ready = [0] * RING
        self.chunk_ready = {}
        self.last_half = {}
        self.halves = []
        self.told = []
        self.used = self.sums = 0

    def new_chunks(self, n, loads):
        first = self.chunk
        for c in range(first, first + n):
            self.ready[c % RING] += loads[c - first]
            self.chunk_ready[c] = 16 * self.ready[c % RING]
        self.chunk += n
        return first

    def use(self, chunk, part, told=None):
        if told is None:
            self.used += 1
            told = "used", self.used
        self.last_half[chunk] = len(self.halves)
        self.halves.append((chunk, part))
        self.told.append(told)

    def use_project(self, chunks, g0):
        for i, c in enumerate(chunks):
            self.use(c, 0)
            self.use(c, 1, ("up", g0 + NB * (i + 1)))

    def use_mlp(self, chunks, down, g0):
        self.sums += NB
        for u in range(len(chunks) + 1):
            if u < len(chunks):
                self.use(chunks[u], 0)
                self.use(chunks[u], 1, ("up", g0 + NB * (u + 1)))
            if u >= 1:
                for x in down[u - 1]:
                    last = u == len(chunks) and x is down[u - 1][-1]
                    self.use(*x, ("acc", self.sums) if last else None)

    def use_out(self, c0):
        self.sums += NB
        for x in range(4):
            self.use(c0 + x // 2, x % 2, ("acc", self.sums) if x == 3 else None)

    def take_turns(self, n):
        t = self.turns
        self.turns += n
        return t

    def take_steps(self, turned):
        g, t = self.steps, []
        for x in turned:
            t.append(self.turns if x else None)
            self.turns += bool(x)
        self.steps += len(turned)
        return g, t


def build(nc, t):
    ctx = ExitStack()
    with ctx:
        _program(nc, t, ctx)


def _program(nc, t, ctx):
    def sb(name, shape, dt=F32):
        return ctx.enter_context(nc.sbuf_tensor(name, shape, dt))

    def sem(name):
        return ctx.enter_context(nc.semaphore(name))

    acc = ctx.enter_context(nc.psum_tensor("acc", [P, 4, W], F32))
    up = ctx.enter_context(nc.psum_tensor("up", [P, 2, W], F32))
    tp = ctx.enter_context(nc.psum_tensor("tp", [P, 2, W], F32))

    raw = sb("raw", [P, RAW, CH // 2])
    ring = raw[:, 0:2 * RING, :].rearrange("p (c a) n -> p c (a n)", a=2)
    cst = sb("cst", [P, C_END])
    h = sb("h", [P, NB, D])
    xTh = sb("xTh", [P, KT, SEQ], F32R)
    xTl = sb("xTl", [P, KT, SEQ], F32R)
    big = sb("big", [P, H_END])
    rows = big[:, 0:2 * D]
    stage = sb("stage", [P, 2, W])
    half = sb("half", [P, 2, W])
    spare = sb("spare", [P, 2 * D])
    wh = sb("wh", [P, SPLITS, CH // 2], F32R)
    wl = sb("wl", [P, SPLITS, CH // 2], F32R)
    hTh = sb("hTh", [P, 2, W], F32R)
    hTl = sb("hTl", [P, 2, W], F32R)
    arena = sb("arena", [P, 5, 2 * D])
    cols = sb("cols", [P, 6, KT])
    rowcols = sb("rowcols", [P, 3, KT])
    wdw = sb("wdw", [P, KT, CONV])
    wr = sb("wr", [P, KT, NE])
    wf = sb("wf", [P, KT, NH2])
    bnd = sb("bnd", [P, 2, 6])
    mv = sb("mv", [P, NB, 2])
    sc = sb("sc", [P, NB, 8])
    ss = sb("ss", [P, NB, NH])
    rs = sb("rs", [P, NB, NH])
    lam = sb("lam", [P, 4 * 64 + 8])
    gn = sb("gn", [P, P])
    att = sb("att", [P, 2, 8])
    rt = sb("rt", [P, 16, NB, NE])
    ex = sb("ex", [P, 8, NE])
    slot = sb("slot", [P, NB, NE + MAX_EXTRA])
    gate = sb("gate", [P, NB, NE + MAX_EXTRA])
    extra = sb("extra", [P, 1 + MAX_EXTRA])
    extra_i = sb("extra_i", [P, 1 + MAX_EXTRA], I32)
    fx = sb("fx", [P, 8, NB, NH2])
    ncT = sb("ncT", [NH2, SEQ])
    bf = sb("bf", [P, NH2])

    ident = cst[:, C_ID:C_ID + P]
    aident = cst[:, C_AID:C_AID + P]
    ones = cst[:, C_ONES:C_ONES + P]
    tri = big[:, H_TRI:H_TRI + P]
    iota = cst[:, C_IOTA:C_IOTA + P]
    causal = cst[:, C_CAUS:C_CAUS + 2 * P]
    accb = acc[:, :, :].rearrange("p (b n) w -> p b (n w)", b=NB)

    lf, qT_, kT_, v_, o_ = (arena[:, i, :] for i in range(5))
    as_tm = lambda a: a.rearrange("p (b n) -> p b n", b=NB)
    as_cm = lambda a: a.rearrange("p (k n) -> p k n", k=KT)
    lf, v, o = as_tm(lf), as_tm(v_), as_tm(o_)
    qT, kT = as_cm(qT_), as_cm(kT_)
    flat = lambda a: a.rearrange("p a b -> p (a b)")
    hg_raw = flat(arena[:, 3:5, :])[:, 0:3 * D].rearrange("p (r n) -> p r n", r=3)
    lb, omlb = spare[:, 0:D], spare[:, D:2 * D]
    HG_SLOT = 7 % RING
    hgA, hgB = (ring[:, HG_SLOT, i * 2 * D:(i + 1) * 2 * D].rearrange("p (i s n) -> p i s n", i=2, s=8) for i in range(2))
    hgS = flat(half[:, :, :]).rearrange("p (s n) -> p s n", s=8)
    hgX = stage[:, 0, 0:P]
    at_s = arena[:, 0, 0:D].rearrange("p (i c n) -> p i c n", i=2, c=2)
    at_p = arena[:, 0, D:2 * D].rearrange("p (i c n) -> p i c n", i=2, c=2)
    headrow = spare[0:NH2, :].rearrange("p (h q) -> p h q", h=NH2)
    xgh, xgl = xTh[:, :, 0:P], xTl[:, :, 0:P]
    y = as_tm(arena[:, 0, :])
    ye = arena[:, 1, D:2 * D]
    pick = arena[:, 2, 0:2 * P].rearrange("p (b n) -> p b n", b=NB)
    give = arena[:, 2, 2 * P:4 * P].rearrange("p (b n) -> p b n", b=NB)
    giveT = arena[:, 2, 4 * P:6 * P].rearrange("p (b n) -> p b n", b=NB)
    PADC = CONV - 1
    uT = flat(arena[:, 0:2, :])[:, 0:KT * (SEQ + PADC)].rearrange("p (k n) -> p k n", k=KT)
    cT = as_cm(arena[:, 2, :])
    ctm = as_tm(arena[:, 3, :])
    CV_DVE, CV_PE = range(4), range(4, KT)
    DIAGS = 2 * D // P
    diag = arena[:, 3, :].rearrange("p (i n) -> p i n", i=DIAGS)
    EARLY = 6
    pe_tm = arena[:, 3, 0:2 * D_PLE].rearrange("p (b n) -> p b n", b=NB)
    pe_Th, pe_Tl = (a[:, 0, :].rearrange("p (k n) -> p k n", k=2) for a in (hTh, hTl))

    def score_banks(n):
        return up if n % 2 == 0 else acc[:, 2:4, :]

    def ring_k(c, n=KT):
        return ring[:, c % RING, :].rearrange("p (k n) -> p k n", k=n)

    def ring_gu(c):
        return ring[:, c % RING, :].rearrange("p (k m n) -> p k m n", k=KT, m=2)

    pl = Plan()
    one = lambda n: [1] * n
    T_x = pl.take_turns(4)
    HG_CHUNKS = list(range(8))
    c_hg = pl.new_chunks(8, one(8))
    g_hg, t_hg = pl.take_steps([c < 4 for c in HG_CHUNKS for _ in range(NB)])
    pl.use_project([c_hg + i for i in range(8)], g_hg)
    T_hgo = pl.take_turns(4)
    c_hgo = pl.new_chunks(2, one(2))
    pl.use_out(c_hgo)
    T_ff = pl.take_turns(4)
    FF_UNITS = D_FF // HALF
    c_ff = pl.new_chunks(17, [1 if i % 3 == 2 or i == 16 else 2 for i in range(17)])
    ff_gu = [c_ff + 3 * (u // 2) + u % 2 for u in range(FF_UNITS)]
    ff_d = [c_ff + 3 * (u // 2) + (2 if u // 2 < FF_UNITS // 2 else 1) for u in range(FF_UNITS)]
    g_ff, t_ff = pl.take_steps([1] * (FF_UNITS * NB))
    pl.use_mlp(ff_gu, [[(ff_d[u], u % 2)] for u in range(FF_UNITS)], g_ff)
    T_da = pl.take_turns(4)
    c_da = pl.new_chunks(6, one(6))
    g_da, t_da = pl.take_steps([c < 4 for c in range(6) for _ in range(NB)])
    pl.use_project([c_da + i for i in range(6)], g_da)
    T_dao = pl.take_turns(4)
    c_dao = pl.new_chunks(2, one(2))
    pl.use_out(c_dao)
    T_moe = pl.take_turns(4)
    pl.chunk += -pl.chunk % RING
    EU = D_FFE // HALF
    before_moe = len(pl.halves)
    assert before_moe % SPLITS == 0
    c_after = pl.chunk
    G, DN = 0, 1
    HALVES = [(G, 0, 0), (G, 0, 1)]
    for u in range(1, EU):
        HALVES += [(G, u, 0), (G, u, 1), (DN, u - 1, 0)]
    HALVES.append((DN, EU - 1, 0))
    NHALF = len(HALVES)
    half_at = {x: m for m, x in enumerate(HALVES)}
    gate_half = lambda u, part: half_at[G, u, part]
    down_half = lambda u: half_at[DN, u, 0]
    assert NHALF % RAW == 0 and NHALF % SPLITS == 0
    half_loads = [2 if x[0] == G else 1 for x in HALVES]
    slot_loads = [sum(half_loads[r::RAW]) for r in range(RAW)]
    tells_used = lambda m: m < NHALF - 1 and not (HALVES[m][0] == G and HALVES[m][2] == 1)
    used_until = lambda m: sum(map(tells_used, range(m + 1)))
    NUSED = used_until(NHALF - 1)
    T_cv = pl.take_turns(4)
    c_pw1 = pl.new_chunks(4, [2] * 4)
    g_cv, t_cv = pl.take_steps([1] * 8)
    pl.use_project([c_pw1 + i for i in range(4)], g_cv)
    T_cback = pl.take_turns(4)
    T_cn = pl.take_turns(4)
    c_pw2 = pl.new_chunks(2, one(2))
    pl.use_out(c_pw2)
    after = []
    for i in range(DEPTH):
        d = {}
        if i == 1:
            d["T_q"] = pl.take_turns(4)
            d["c_k"] = pl.new_chunks(4, one(4))
            d["g_kv"], d["t_kv"] = pl.take_steps([1] * 4 + [0] * 4)
            d["g_f"], _ = pl.take_steps([0] * 2)
            pl.use_project([d["c_k"] + c for c in range(4)], d["g_kv"])
            d["T_q2"] = pl.take_turns(4)
            d["c_q"] = pl.new_chunks(2, one(2))
            d["g_q"], d["t_q"] = pl.take_steps([1] * 4)
            pl.use_project([d["c_q"] + c for c in range(2)], d["g_q"])
            d["T_o"] = pl.take_turns(4)
            d["c_o"] = pl.new_chunks(2, one(2))
            pl.use_out(d["c_o"])
        d["T_f"] = pl.take_turns(4)
        d["c_f"] = pl.new_chunks(16, one(16))
        d["g_ff"], d["t_ff"] = pl.take_steps([1] * 16)
        pl.use_mlp([d["c_f"] + 2 * u for u in range(8)],
                   [[(d["c_f"] + 2 * u + 1, x) for x in range(2)] for u in range(8)], d["g_ff"])
        d["T_p"] = pl.take_turns(1)
        d["T_g"] = pl.take_turns(4)
        d["c_p"] = pl.new_chunks(3, one(3))
        d["g_p"], _ = pl.take_steps([0] * 4)
        pl.use(d["c_p"], 0)
        pl.use_project([d["c_p"] + 1, d["c_p"] + 2], d["g_p"])
        after.append(d)

    def half_ready(eng, m, i, x):
        eng.wait_ge(m["ready"][x % RAW], i * (16 * slot_loads[x % RAW]) + 16 * sum(half_loads[x % RAW:x + 1:RAW]))

    w_ready = [sem(f"w_ready{s}") for s in range(RING)]
    s_hi = sem("s_hi")
    s_lo = sem("s_lo")
    s_used = sem("s_used")
    s_Th = sem("s_Th")
    s_cst = sem("s_cst")
    s_lbV = sem("s_lbV")
    s_big = sem("s_big")
    s_x = sem("s_x")
    s_small = sem("s_small")
    s_gn = sem("s_gn")
    s_lb = sem("s_lb")
    s_rows = sem("s_rows")
    s_rows_free = sem("s_rows_free")
    s_pe = sem("s_pe")
    s_headrow = sem("s_headrow")
    s_up = sem("s_up")
    s_act = sem("s_act")
    s_st = sem("s_st")
    s_T = sem("s_T")
    s_Te = sem("s_Te")
    s_acc = sem("s_acc")
    s_norm = sem("s_norm")
    s_nA = sem("s_nA")
    s_nD = sem("s_nD")
    d_ch = sem("d_ch")
    a_ch = sem("a_ch")
    s_lbA, s_lbD = sem("s_lbA"), sem("s_lbD")
    hg_m, hg_e, hg_ab, hg_s, hg_sm, hg_o, hg_sq, hg_og = (
        sem(n) for n in ("hg_decay", "hg_exp", "hg_scaled", "hg_scores", "hg_masked", "hg_out", "hg_square", "hg_gated"))
    at_S, at_sm, at_e, at_w, at_T, at_Te, at_O, at_sq, at_og = (
        sem(n) for n in ("at_scores", "at_masked", "at_exp", "at_weights", "at_turned", "at_copied", "at_out",
                         "at_square", "at_kept"))
    s_hn = sem("s_hn")
    s_rl, s_rp, s_ra, s_rd = sem("router_logits"), sem("router_places"), sem("router_act"), sem("router_done")
    moe = [{n: sem(f"{p}{n}") for n in ("picked", "gath", "xg", "turned", "giveT", "up", "act", "st", "T", "Te",
                                        "hi", "lo", "used", "xgh", "Th", "down", "ye", "give", "added")} for p in ("m_", "x_")]
    for m, p_ in zip(moe, ("m_", "x_")):
        m["ready"] = [sem(f"{p_}ready{r}") for r in range(RAW)]
    cv_dw, cv_n = sem("conv_done"), sem("conv_normed")
    cv_diag, cv_tap, cv_sum = sem("conv_diagonals"), sem("conv_taps"), sem("conv_sums")
    f_L, f_A, f_D, f_C, f_CT, f_ct = (sem(n) for n in ("f_logits", "f_act", "f_vec", "f_sum", "f_sumT", "f_sumT_sb"))
    s_xdone = sem("s_xdone")
    s_out = sem("s_out")

    told_by = {"used": s_used, "up": s_up, "acc": s_acc}

    def raw_half(q):
        c, part = pl.halves[q]
        return ring[:, c % RING, part * (CH // 2):(part + 1) * (CH // 2)]

    block = ctx.enter_context(nc.Block())

    N_HGO, N_LN0, N_LN1, N_DAO, N_LN2, N_LN3 = (NB * i for i in range(6))
    N_RC = 6 * NB
    N_AFTER = []
    n = N_RC + NB
    N_CB = n
    n += NB
    for i in range(DEPTH):
        d = {}
        if i == 1:
            d["q"] = n
            n += NB
            d["o"] = n
            n += NB
        d["f"] = n
        n += NB
        d["g"] = n
        n += NB
        d["h"] = n
        n += NB
        N_AFTER.append(d)
    N_FIN = n
    A_HG, A_FF, A_DA = 0, NB, 2 * NB
    A_PW2 = 3 * NB
    A_F0, A_O1, A_F1 = 4 * NB, 5 * NB, 6 * NB

    @block.sync
    def _(sp):
        ld = lambda out, in_, s: sp.dma_start(out, in_).then_inc(s, 16)
        kp = lambda w: w.rearrange("(k p) n -> p k n", p=P)

        def wait_slot(c):
            if RING <= c < c_after or c >= c_after + RING:
                sp.wait_ge(s_lo, pl.last_half[c - RING] + 1)

        def cols_chunk(c, w, col):
            wait_slot(c)
            ld(ring_k(c), kp(w[:, col:col + W]), w_ready[c % RING])

        def pair_chunk(c, wa, wb, col):
            wait_slot(c)
            ld(ring_gu(c)[:, :, 0, :], kp(wa[:, col:col + HALF]), w_ready[c % RING])
            ld(ring_gu(c)[:, :, 1, :], kp(wb[:, col:col + HALF]), w_ready[c % RING])

        def rows_chunk(c, w, row, n):
            wait_slot(c)
            ld(ring_k(c, 4)[:, 0:n, :], kp(w[row:row + n * P, :]), w_ready[c % RING])

        ld(h[:, :, :], t["x"][0].rearrange("(b p) n -> p b n", p=P), s_x)
        ld(cst[:, :], t["consts"], s_cst)
        for i, c in enumerate(HG_CHUNKS):
            cols_chunk(c_hg + i, t["hg_w_in"], c * W)
            if i == 2:
                ld(big[:, :], t["hg_tables"], s_big)
        for i in range(2):
            cols_chunk(c_hgo + i, t["hg_w_out"], i * W)
        sp.wait_ge(hg_o, NH * NB)
        for u in range(FF_UNITS):
            pair_chunk(ff_gu[u], t["ffn_w_gate"][0], t["ffn_w_up"][0], u * HALF)
            if u % 2 == 1:
                rows_chunk(ff_d[u], t["ffn_w_down"][0], (u - 1) * HALF, 4)
            elif u == FF_UNITS - 1:
                rows_chunk(ff_d[u], t["ffn_w_down"][0], u * HALF, 2)
        for i in range(6):
            cols_chunk(c_da + i, t["da_w_in"], i * W)
        for i in range(2):
            cols_chunk(c_dao + i, t["da_w_out"], i * W)

        def expert(m, e, i):
            gw, uw, dw = (t[n][0, bass.ds(e, 1), :, :].rearrange("a k n -> (a k) n")
                          for n in ("moe_w_gate", "moe_w_up", "moe_w_down"))
            for x, (kind, u, part) in enumerate(HALVES):
                sp.wait_ge(m["lo"], i * NHALF + (x + 1))
                dst, ready = raw[:, x % RAW, :], m["ready"][x % RAW]
                if kind == G:
                    dst = dst.rearrange("p (k m n) -> p k m n", k=KT // 2, m=2)
                    for j, w in enumerate((gw, uw)):
                        ld(dst[:, :, j, :], kp(w[part * (D // 2):(part + 1) * (D // 2), u * HALF:(u + 1) * HALF]), ready)
                else:
                    ld(dst.rearrange("p (k n) -> p k n", k=2), kp(dw[u * HALF:(u + 1) * HALF, :]), ready)

        sp.wait_ge(s_lo, before_moe)
        with sp.Fori(0, NE) as e:
            expert(moe[0], e, e)

        sp.wait_ge(s_rd, 1)
        sp.wait_ge(moe[0]["lo"], NE * NHALF + RAW)
        n_extra = sp.value_load(extra_i[0:1, 0:1], min_val=0, max_val=MAX_EXTRA)
        with sp.If(n_extra > 0):
            with sp.Fori(0, n_extra) as j:
                e = sp.value_load(extra_i[0:1, bass.ds(j + 1, 1)], min_val=0, max_val=NE - 1)
                expert(moe[1], e, j)
            sp.wait_ge(moe[1]["lo"], n_extra * NHALF + RAW)
            sp.sem_inc(s_xdone, 1)

        for i in range(4):
            pair_chunk(c_pw1 + i, t["conv_w_pw1_2"][0][:, 0:D], t["conv_w_pw1_2"][0][:, D:2 * D], i * HALF)
        for i in range(2):
            cols_chunk(c_pw2 + i, t["conv_w_pw2_2"][0], i * W)
        for i, d in enumerate(after):
            if i == 1:
                for c in range(4):
                    cols_chunk(d["c_k"] + c, t["w_kvf_2"], c * W)
                for c in range(2):
                    cols_chunk(d["c_q"] + c, t["attn_w_q_2"][0], c * W)
                for c in range(2):
                    cols_chunk(d["c_o"] + c, t["attn_w_o_2"][0], c * W)
            for u in range(8):
                cols_chunk(d["c_f"] + 2 * u, t["ffn_w1_2"][i], u * W)
                rows_chunk(d["c_f"] + 2 * u + 1, t["ffn_w2_2"][i], u * W, 4)
            wait_slot(d["c_p"])
            rows_chunk(d["c_p"], t["ple_w_proj_2"][i], 0, 2)
            for c in range(2):
                cols_chunk(d["c_p"] + 1 + c, t["ple_w_gate_2"][i], c * W)

        for b in range(NB):
            sp.wait_ge(s_norm, N_FIN + b + 1)
            ld(t["out"][0, b * P:(b + 1) * P, :], o[:, b, :], s_out)
        sp.wait_ge(s_out, 16 * NB)

    SMALL = 0

    @block.gpsimd
    def _(pool):
        nonlocal SMALL

        def small(out, in_):
            nonlocal SMALL
            pool.dma_start(out, in_).then_inc(s_small, 16)
            SMALL += 16

        bc = lambda row: row.partition_broadcast(P)
        pool.dma_start(hg_raw, t["hg_lb"].rearrange("r n -> (r n)").partition_broadcast(P)
                       .rearrange("p (r n) -> p r n", r=3)).then_inc(s_lb, 16)

        def load_rows(*srcs):
            for i, s in enumerate(srcs):
                pool.dma_start(rows[:, i * D:(i + 1) * D], bc(s)).then_inc(s_rows, 16)

        with nc.allow_non_contiguous_dma(reason="small parameters"):
            pool.dma_start(gn[:, :], bc(t["hg_norm_g"])).then_inc(s_gn, 16)
            small(lam[:, 0:256], bc(t["da_lam"].rearrange("a n -> (a n)")))
            small(wr[:, :, :], t["moe_w_router"][0].rearrange("(k p) n -> p k n", p=P))
            small(wf[:, :, :], t["w_kvf_2"][:, 2 * D:2 * D + NH2].rearrange("(k p) n -> p k n", p=P))
            small(bf[:, :], bc(t["b_f_2"]))
            for i, a in enumerate((t["mix_norm_2"][0], t["mix_norm_2"][1], t["kv_norm_2"],
                                   t["ffn_norm_2"][0], t["ffn_norm_2"][1], t["ple_norm_2"][0])):
                small(cols[:, i, :], a.rearrange("(k p) -> p k", p=P))
            for i, a in enumerate((t["conv_b_dw_2"][0], t["conv_ln_g_2"][0], t["conv_ln_b_2"][0])):
                small(rowcols[:, i, :], a.rearrange("(k p) -> p k", p=P))
            for k in range(KT):
                small(wdw[:, k, :], t["conv_w_dw_2"][0][:, k * P:(k + 1) * P].rearrange("j p -> p j"))
            pool.wait_ge(hg_o, NH * NB)
            load_rows(t["ln_g"][0, 0], t["ln_b"][0, 0])
            for i, s in enumerate(((t["ln_g"][0, 1], t["ln_b"][0, 1]), (t["ln_g"][1, 0], t["ln_b"][1, 0]),
                                   (t["ln_g"][1, 1], t["ln_b"][1, 1]),
                                   (t["conv_b_pw1_2"][0][0:D], t["conv_b_pw1_2"][0][D:2 * D]),
                                   (t["conv_b_pw2_2"][0], t["final_norm_2"]))):
                pool.wait_ge(s_rows_free, i + 1)
                load_rows(*s)
                if i == 0:
                    pool.dma_start(gn[:, :], bc(t["da_norm_g"])).then_inc(s_gn, 16)
            pool.wait_ge(s_T, T_cn + 4)
            pool.dma_start(pe_tm, t["p_2"][0, 0].rearrange("(b p) n -> p b n", p=P)).then_inc(s_pe, 16)
            pool.wait_ge(s_norm, N_AFTER[0]["h"] + NB)
            pool.dma_start(cols[:, 5, :], t["ple_norm_2"][1].rearrange("(k p) -> p k", p=P)).then_inc(s_pe, 16)
            pool.wait_ge(s_up, after[1]["g_f"] + NB)
            pool.dma_start(headrow, t["headrow"]).then_inc(s_headrow, 16)
            pool.wait_ge(s_T, after[1]["T_o"] + 4)
            pool.dma_start(pe_tm, t["p_2"][1, 0].rearrange("(b p) n -> p b n", p=P)).then_inc(s_pe, 16)

    @block.scalar
    def _(act):
        f = nc.scalar.activation
        chain = 0

        def link(ins):
            nonlocal chain
            chain += 1
            ins.then_inc(a_ch, 1)
            act.wait_ge(a_ch, chain)

        def copy_turn(t_, out, in_):
            act.wait_ge(s_T, t_ + 1)
            f(out, in_, ACT.Copy).then_inc(s_Te, 1)

        nsplit, last_split = 0, before_moe

        def split(n=1):
            nonlocal nsplit
            for _ in range(n):
                q = nsplit
                if q == last_split:
                    return
                c, part = pl.halves[q]
                act.wait_ge(w_ready[c % RING], pl.chunk_ready[c])
                if q >= SPLITS and not before_moe <= q < before_moe + SPLITS:
                    told, count = pl.told[q - SPLITS]
                    act.wait_ge(told_by[told], count)
                f(wh[:, q % SPLITS, :], raw_half(q), ACT.Copy).then_inc(s_hi, 1)
                nsplit += 1

        def turn_hi(tt, out, in_, **kw):
            act.wait_ge(s_T, tt + 1)
            f(out, in_, ACT.Copy, **kw).then_inc(s_Th, 1)

        def to_channels(t0, gain=None):
            for b in range(NB):
                for q in range(2):
                    tt = t0 + 2 * b + q
                    dst = xTh[:, 4 * q:4 * q + 4, b * P:(b + 1) * P]
                    src = tp[:, tt % 2, :].rearrange("p (k n) -> p k n", k=4)
                    if gain is None:
                        turn_hi(tt, dst, src)
                    else:
                        act.wait_ge(s_T, tt + 1)
                        for k in range(4):
                            ins = f(dst[:, k, :], src[:, k, :], ACT.Copy, scale=cols[:, gain, 4 * q + k:4 * q + k + 1])
                        ins.then_inc(s_Th, 1)

        def step_copy(tt, dst, chunk, b, nk=4):
            copy_turn(tt, dst[:, nk * chunk:nk * chunk + nk, b * P:(b + 1) * P],
                      tp[:, tt % 2, 0:nk * P].rearrange("p (k n) -> p k n", k=nk))

        acts = [0]

        def step_act(g, out, in_, func, **kw):
            act.wait_ge(s_up, g + 1)
            f(out, in_, func, **kw).then_inc(s_act, 1)
            acts[0] += 1

        nsq = [0]

        def norm_root(out, in_):
            nsq[0] += 1
            act.wait_ge(s_nD, nsq[0])
            f(out, in_, ACT.Sqrt).then_inc(s_nA, 1)

        def layer_norms():
            for b in range(NB):
                norm_root(sc[:, b, 1:2], sc[:, b, 0:1])

        sums = [0]

        def root_sums(b):
            f(half[:, :, :], h[:, b, :].rearrange("p (a n) -> p a n", a=2), ACT.Square,
              accum_out=sc[:, b, 2:3]).then_inc(a_ch, 1)

        to_channels(T_x)
        split(2)
        act.wait_ge(s_lbD, 1)
        for r in range(3):
            ins = f(hg_raw[:, r, :], hg_raw[:, r, :], ACT.Exp)
        ins.then_inc(s_lbA, 1)
        split(SPLITS - 2)
        for i, c in enumerate(HG_CHUNKS):
            split()
            if i > 0 and HG_CHUNKS[i - 1] < 4:
                for b in range(NB):
                    pc = HG_CHUNKS[i - 1]
                    step_copy(t_hg[NB * (i - 1) + b], kT if pc >= 2 else qT, pc % 2, b)
            for b in range(NB):
                g = g_hg + NB * i + b
                func = ACT.Sigmoid if c in (2, 3, 6, 7) else ACT.Silu if c < 2 else ACT.Copy
                step_act(g, half[:, g % 2, :], up[:, g % 2, :], func)
                if c in (2, 3):
                    act.wait_ge(s_lbD, 2 + (NB * (c - 2) + b) + 1)
                    f(lf[:, b, (c - 2) * W:(c - 1) * W], half[:, g % 2, :], ACT.Ln).then_inc(s_lbA, 1)
            split()
        for n in range(NH * NB + 3):
            if n < NH * NB:
                act.wait_ge(hg_m, n + 1)
                f(acc[:, 0:2, :], acc[:, 0:2, :], ACT.Exp).then_inc(hg_e, 1)
            if 2 <= n < NH * NB + 2:
                m = n - 2
                j, b = m // NB, m % NB
                act.wait_ge(hg_o, m + 1)
                f(up[:, m % 2, P:2 * P], up[:, m % 2, 0:P], ACT.Square, accum_out=ss[:, b, j:j + 1]).then_inc(hg_sq, 1)
        act.wait_ge(s_hn, 1)
        f(rs[:, :, :], rs[:, :, :], ACT.Sqrt).then_inc(s_hn, 1)
        to_channels(T_hgo)
        split(2)
        layer_norms()

        def mlp(g0, ts, gate, width, down_halves):
            for u in range(len(ts) // NB):
                split()
                for b in range(NB):
                    step_act(g0 + NB * u + b, half[:, b, 0:width], up[:, b, 0:width], gate)
                split()
                if u >= 1:
                    split(down_halves)
                for b in range(NB):
                    tt = ts[NB * u + b]
                    turn_hi(tt, hTh[:, b, 0:width], tp[:, tt % 2, 0:width])

        to_channels(T_ff)
        split(2)
        mlp(g_ff, t_ff, ACT.Silu, HALF, 1)
        layer_norms()

        act.wait_ge(s_lbD, 2 + 2 * NB + 1)
        f(lam[:, 256:258], lam[:, 256:258], ACT.Exp).then_inc(s_lbA, 1)
        to_channels(T_da)
        split(1)
        for c in range(6):
            split()
            if 1 <= c <= 4:
                for b in range(NB):
                    step_copy(t_da[NB * (c - 1) + b], qT if c <= 2 else kT, (c - 1) % 2, b)
            split()

        def exps(n, b, base):
            w = P * (b + 1)
            act.wait_ge(at_sm, base + n + 1)
            for c in range(2):
                ins = f(at_p[:, n % 2, c, 0:w], at_s[:, n % 2, c, 0:w], ACT.Exp, bias=att[:, n % 2, c:c + 1],
                        accum_out=att[:, n % 2, 2 + c:3 + c])
            ins.then_inc(at_e, 1)

        NA = NH * NB
        for n in range(NA + 3):
            if n < NA:
                exps(n, n % NB, 0)
            if 1 <= n <= NA:
                m = n - 1
                w = P * (m % NB + 1)
                act.wait_ge(at_T, m + 1)
                f(half[:, m % 2, 0:w], tp[:, m % 2, 0:w], ACT.Copy).then_inc(at_Te, 1)
            if 2 <= n < NA + 2:
                m = n - 2
                act.wait_ge(at_O, m + 1)
                f(acc[:, m % 2, P:2 * P], acc[:, m % 2, 0:P], ACT.Square,
                  accum_out=ss[:, m % NB, m // NB:m // NB + 1]).then_inc(at_sq, 1)
        act.wait_ge(s_hn, 4)
        f(rs[:, :, :], rs[:, :, :], ACT.Sqrt).then_inc(s_hn, 1)
        to_channels(T_dao)
        split(2)
        layer_norms()

        to_channels(T_moe)
        act.wait_ge(s_ra, 1)
        f(rt[:, 7, :, 0:1], rt[:, 7, :, 0:1], ACT.Sigmoid).then_inc(s_rp, 1)

        def expert(m, i):
            def split_half(x):
                half_ready(act, m, i, x)
                if x >= SPLITS:
                    kind, u, _ = HALVES[x - SPLITS]
                    if tells_used(x - SPLITS):
                        act.wait_ge(m["used"], i * NUSED + used_until(x - SPLITS))
                    else:
                        act.wait_ge(m["up"], i * EU + (u + 1))
                f(wh[:, x % SPLITS, :], raw[:, x % RAW, :], ACT.Copy).then_inc(m["hi"], 1)

            split_half(0)
            split_half(1)
            for q in range(2):
                act.wait_ge(m["gath"], i * 2 + (q + 2))
                f(xgh[:, 4 * q:4 * q + 4, :], tp[:, q, :].rearrange("p (k n) -> p k n", k=4), ACT.Copy).then_inc(m["xgh"], 1)
            act.wait_ge(m["turned"], i + 2)
            f(giveT, acc[:, 2, 0:2 * P].rearrange("p (b n) -> p b n", b=NB), ACT.Copy).then_inc(m["giveT"], 1)
            split_half(2)
            for s in range(EU + 1):
                if s > 0:
                    act.wait_ge(m["T"], i * EU + s)
                    f(hTh[:, (s - 1) % 2, 0:HALF], tp[:, (s - 1) % 2, 0:HALF], ACT.Copy).then_inc(m["Th"], 1)
                if 1 <= s < EU - 1:
                    split_half(gate_half(s + 1, 0))
                if s < EU:
                    act.wait_ge(m["up"], i * EU + (s + 1))
                    f(half[:, s % 2, 0:HALF], up[:, s % 2, 0:HALF], ACT.Silu).then_inc(m["act"], 1)
                if s < EU - 1:
                    split_half(gate_half(s + 1, 1))
                if s < EU:
                    split_half(down_half(s))
            act.wait_ge(m["down"], i + 1)
            f(ye.rearrange("p (a n) -> p a n", a=2), acc[:, 0:2, :], ACT.Copy).then_inc(m["ye"], 1)

        for m in moe:
            act.sem_inc(m["ye"], 1)
        with act.Fori(0, NE) as i:
            expert(moe[0], i)
        act.wait_ge(s_rd, 1)
        n_extra = act.value_load(extra_i[0:1, 0:1], min_val=0, max_val=MAX_EXTRA)
        with act.If(n_extra > 0):
            with act.Fori(0, n_extra) as j:
                expert(moe[1], j)
        layer_norms()

        nrms = [0]

        def rms(from_acc, a0=None):
            for b in range(NB):
                if from_acc:
                    act.wait_ge(s_acc, a0 + b + 1)
                    link(f(h[:, b, :], accb[:, b, :], ACT.Copy))
                else:
                    act.wait_ge(s_nD, nsq[0] + 1)
                    nsq[0] += 1
                f(half[:, :, :], h[:, b, :].rearrange("p (a n) -> p a n", a=2), ACT.Square,
                  accum_out=sc[:, b, 2:3]).then_inc(s_nA, 1)
                nsq[0] += 1
                act.wait_ge(s_nD, nsq[0])
                f(sc[:, b, 1:2], sc[:, b, 0:1], ACT.Sqrt).then_inc(s_nA, 1)

        last_split = len(pl.halves)
        split(1)
        rms(False)
        to_channels(T_cv, 0)
        split(2)
        for c in range(4):
            split()
            if c > 0:
                for b in range(NB):
                    step_copy(t_cv[NB * (c - 1) + b], uT[:, :, PADC:], c - 1, b, 2)
            for b in range(NB):
                act.wait_ge(cv_n, NB * c + b + 1)
                f(half[:, b, HALF:W], half[:, b, HALF:W], ACT.Sigmoid).then_inc(s_act, 1)
            split()
        for b in range(NB):
            step_copy(t_cv[NB * 3 + b], uT[:, :, PADC:], 3, b, 2)

        def conv_sum(i):
            k = CV_PE[i]
            act.wait_ge(cv_tap, CONV * (i + 1))
            f(cT[:, k, :], up[:, k % 2, 0:SEQ], ACT.Identity, bias=rowcols[:, 0, k:k + 1]).then_inc(cv_sum, 1)

        for x in range(CONV * len(CV_PE)):
            if x >= DIAGS:
                act.wait_ge(cv_tap, x - DIAGS + 1)
            if x % CONV == DIAGS and x > CONV:
                conv_sum(x // CONV - 1)
            f(diag[:, x % DIAGS, :], ident, ACT.Copy, scale=wdw[:, CV_PE[x // CONV], x % CONV:x % CONV + 1]).then_inc(cv_diag, 1)
        conv_sum(len(CV_PE) - 1)
        for b in range(NB):
            for q in range(2):
                tt = T_cback + 2 * b + q
                copy_turn(tt, ctm[:, b, q * W:(q + 1) * W], tp[:, tt % 2, :])
        layer_norms()
        for b in range(NB):
            for q in range(2):
                tt = T_cn + 2 * b + q
                act.wait_ge(s_T, tt + 1)
                for k in range(4 * q, 4 * q + 4):
                    kk = slice((k % 4) * P, (k % 4 + 1) * P)
                    ins = f(stage[:, tt % 2, kk], tp[:, tt % 2, kk], ACT.Silu,
                            scale=rowcols[:, 1, k:k + 1], bias=rowcols[:, 2, k:k + 1])
                link(ins)
                f(xTh[:, 4 * q:4 * q + 4, b * P:(b + 1) * P], stage[:, tt % 2, :].rearrange("p (k n) -> p k n", k=4),
                  ACT.Copy).then_inc(s_Th, 1)
        split(2)

        for i, d in enumerate(after):
            if i == 1:
                rms(False)
                to_channels(d["T_q"], 2)
                for c in range(4):
                    split()
                    if 1 <= c <= 2:
                        for b in range(NB):
                            step_copy(d["t_kv"][NB * (c - 1) + b], kT, c - 1, b)
                    split()
                to_channels(d["T_q2"], 1)
                act.wait_ge(f_D, 1)
                link(f(fx[:, 1], fx[:, 0], ACT.Abs))
                link(f(fx[:, 1], fx[:, 1], ACT.Exp, scale=-1.0))
                f(fx[:, 2], fx[:, 1], ACT.Ln, bias=1.0).then_inc(f_A, 1)
                for c in range(2):
                    split()
                    if c == 1:
                        for b in range(NB):
                            step_copy(d["t_q"][b], qT, 0, b)
                    split()
                for b in range(NB):
                    step_copy(d["t_q"][NB + b], qT, 1, b)
                act.wait_ge(f_CT, 1)
                f(ncT[:, :], tp[0:NH2, 0, 0:SEQ], ACT.Copy, scale=-1.0).then_inc(f_ct, 1)
                for n in range(NA + 2):
                    if n < NA:
                        exps(n, n % NB, NA)
                    if 1 <= n <= NA:
                        m = n - 1
                        w = 2 * P * (m % NB + 1)
                        act.wait_ge(at_T, NA + m + 1)
                        f(half[:, m % 2, 0:w], tp[:, m % 2, 0:w], ACT.Copy).then_inc(at_Te, 1)
                to_channels(d["T_o"])
                split(2)
                rms(True, A_O1)
            else:
                rms(False)
            to_channels(d["T_f"], 3 + i)
            split(2)
            mlp(d["g_ff"], d["t_ff"], ACT.Relu, W, 2)
            rms(True, A_F1 if i else A_F0)
            turn_hi(d["T_p"], hTh[:, 0, :], tp[:, d["T_p"] % 2, :])
            act.wait_ge(s_pe, 16 if i == 0 else 48)
            to_channels(d["T_g"], 5)
            split(2)
            split()
            for c in range(2):
                split()
                for b in range(NB):
                    step_act(d["g_p"] + NB * c + b, half[:, b, :], up[:, b, :], ACT.Sigmoid)
                split()
        rms(False)

    @block.vector
    def _(dve):
        V = nc.vector
        chain = 0

        def link(ins):
            nonlocal chain
            chain += 1
            ins.then_inc(d_ch, 1)
            dve.wait_ge(d_ch, chain)

        acts = [0]

        def wait_act():
            acts[0] += 1
            dve.wait_ge(s_act, acts[0])

        def stage_free(g, last_turn):
            if last_turn is not None:
                dve.wait_ge(s_T, last_turn + 1)

        nst = [0, 0]

        def stats(b, src):
            for q in range(2):
                ins = V.bn_stats(bnd[:, q, :], src[:, q * W:(q + 1) * W])
            link(ins)
            link(V.bn_aggr(mv[:, b, :], bnd[:, :, :]))
            return mv[:, b, 1:2]

        def root(b, var, scale, eps):
            V.tensor_scalar(sc[:, b, 0:1], var, scale, eps, ALU.mult, ALU.add).then_inc(s_nD, 1)
            nst[0] += 1
            nst[1] += 1
            dve.wait_ge(s_nA, nst[1])
            link(V.reciprocal(sc[:, b, 3:4], sc[:, b, 1:2]))
            return sc[:, b, 3:4]

        nrows = [0]

        def layer_norm(src, a0=None):
            nrows[0] += 32
            for b in range(NB):
                if a0 is not None:
                    dve.wait_ge(s_acc, a0 + b + 1)
                r = root(b, stats(b, src[:, b, :]), 1.0, LN_EPS)
                if b == 0:
                    dve.wait_ge(s_rows, nrows[0])
                link(V.scalar_tensor_tensor(h[:, b, :], src[:, b, :], mv[:, b, 0:1], rows[:, 0:D], ALU.subtract, ALU.mult))
                ins = V.scalar_tensor_tensor(h[:, b, :], h[:, b, :], r, rows[:, D:2 * D], ALU.mult, ALU.add)
                chain_ins(ins)
                dve.sem_inc(s_norm, 1)
            dve.sem_inc(s_rows_free, 1)

        chain_ins = link
        nsplit, last_split = 0, before_moe

        def split(n=1):
            nonlocal nsplit
            for _ in range(n):
                q = nsplit
                if q == last_split:
                    return
                dve.wait_ge(s_hi, q + 1)
                V.tensor_tensor(wl[:, q % SPLITS, :], raw_half(q), wh[:, q % SPLITS, :].bitcast(F32),
                                ALU.subtract).then_inc(s_lo, 1)
                nsplit += 1

        turned = 0

        def wait_turn():
            nonlocal turned
            turned += 1
            dve.wait_ge(s_Th, turned)

        def turn_lo(out, hi, in_):
            wait_turn()
            V.tensor_tensor(out, in_, hi.bitcast(F32), ALU.subtract).then_inc(s_Te, 1)

        def to_channels(t0, gain=None, src=None):
            for b in range(NB):
                for q in range(2):
                    tt = t0 + 2 * b + q
                    at = slice(4 * q, 4 * q + 4), slice(b * P, (b + 1) * P)
                    lo, hi = xTl[:, at[0], at[1]], xTh[:, at[0], at[1]]
                    x = (tp if src is None else src)[:, tt % 2, :].rearrange("p (k n) -> p k n", k=4)
                    if gain is None:
                        turn_lo(lo, hi, x)
                    else:
                        wait_turn()
                        for k in range(4):
                            ins = V.scalar_tensor_tensor(lo[:, k, :], x[:, k, :], cols[:, gain, 4 * q + k:4 * q + k + 1],
                                                         hi[:, k, :].bitcast(F32), ALU.mult, ALU.subtract)
                        ins.then_inc(s_Te, 1)

        last_turn = [None, None]
        to_channels(T_x)
        split(2)
        e3 = hg_raw
        dve.wait_ge(s_lb, 16)
        link(V.tensor_tensor(lb, e3[:, 0, :], e3[:, 1, :], ALU.max))
        link(V.tensor_tensor(lb, lb, e3[:, 2, :], ALU.max))
        for r in range(3):
            ins = V.tensor_tensor(e3[:, r, :], e3[:, r, :], lb, ALU.subtract)
        ins.then_inc(s_lbD, 1)
        split(SPLITS - 2)
        for i, c in enumerate(HG_CHUNKS):
            split()
            if i == 0:
                dve.wait_ge(s_lbA, 1)
                link(V.tensor_tensor(lb, e3[:, 0, :], e3[:, 1, :], ALU.add))
                link(V.tensor_tensor(lb, lb, e3[:, 2, :], ALU.add))
            elif i == 1:
                V.reciprocal(omlb[:, W:D], lb[:, W:D]).then_inc(s_lbV, 1)
            for b in range(NB):
                s = NB * i + b
                g = g_hg + s
                hf = half[:, g % 2, :]
                st = stage[:, g % 2, :]
                wait_act()
                stage_free(g, last_turn[g % 2])
                if c in (2, 3):
                    cc = slice((c - 2) * W, (c - 1) * W)
                    link(V.tensor_tensor(hf, hf, omlb[:, cc], ALU.mult))
                    link(V.tensor_tensor(hf, hf, lb[:, cc], ALU.add))
                    link(V.tensor_scalar(st, hf, -1.0, 1.0, ALU.mult, ALU.add))
                    link(V.tensor_scalar(hf, hf, 2.0 ** -63, None, ALU.max))
                    dve.sem_inc(s_lbD, 1)
                    dve.wait_ge(s_lbA, 2 + NB * (c - 2) + b)
                    dve.sem_inc(s_st, 1)
                elif c < 2:
                    V.tensor_copy(st, hf).then_inc(s_st, 1)
                elif c < 6:
                    V.tensor_copy(v[:, b, (c - 4) * W:(c - 3) * W], hf).then_inc(s_st, 1)
                else:
                    V.tensor_tensor(o[:, b, (c - 6) * W:(c - 5) * W].rearrange("p (j n) -> p j n", n=P),
                                    hf.rearrange("p (j n) -> p j n", n=P),
                                    gn[:, :].unsqueeze(1).broadcast_to([P, 4, P]), ALU.mult).then_inc(s_st, 1)
                last_turn[g % 2] = t_hg[s] if t_hg[s] is not None else last_turn[g % 2]
            split()
            if i == 0:
                V.reciprocal(omlb[:, 0:W], lb[:, 0:W]).then_inc(s_lbV, 1)
            elif i == 1:
                dve.wait_ge(s_lbV, 2)
                link(V.tensor_tensor(lb, e3[:, 0, :], omlb, ALU.mult))
                link(V.tensor_scalar(omlb, lb, -1.0, 1.0, ALU.mult, ALU.add))
                dve.sem_inc(s_lbD, 1)
                dve.wait_ge(s_gn, 16)
        for n in range(NH * NB + 3):
            if n < NH * NB:
                j, b = n // NB, n % NB
                dve.wait_ge(hg_e, n + 1)
                if n == 0:
                    dve.wait_ge(s_Te, T_hgo)
                if n >= 2:
                    dve.wait_ge(hg_s, n - n % NB)
                ev = accb[:, 0, :].rearrange("p (s n) -> p s n", s=8)
                for dst, src in ((hgA, qT), (hgB, kT)):
                    ins = V.tensor_tensor(dst[:, n % 2], ev,
                                          src[:, j, b * P:(b + 1) * P].unsqueeze(1).broadcast_to([P, 8, P]), ALU.mult)
                ins.then_inc(hg_ab, 1)
            if 1 <= n <= NH * NB:
                m = n - 1
                dve.wait_ge(hg_s, m + 1)
                if m >= 1:
                    dve.wait_ge(hg_o, m)
                ins = V.tensor_tensor(hgS, accb[:, 1, :].rearrange("p (s n) -> p s n", s=8),
                                      big[:, H_MASK:H_MASK + 8 * P].rearrange("p (s n) -> p s n", s=8), ALU.mult)
                if m % NB == 1:
                    ins = V.tensor_copy(hgX, tp[:, (m // NB) % 2, 0:P])
                ins.then_inc(hg_sm, 1)
            if 3 <= n:
                m = n - 3
                j, b = m // NB, m % NB
                dve.wait_ge(hg_sq, m + 1)
                oj = o[:, b, j * P:(j + 1) * P]
                V.tensor_tensor(oj, up[:, m % 2, 0:P], oj, ALU.mult).then_inc(hg_og, 1)

        def head_norms(k):
            link(V.tensor_scalar(rs[:, :, :], ss[:, :, :], 1.0 / P, LN_EPS, ALU.mult, ALU.add))
            dve.sem_inc(s_hn, 1)
            dve.wait_ge(s_hn, k + 2)
            link(V.reciprocal(rs[:, :, :], rs[:, :, :]))
            for b in range(NB):
                ob = o[:, b, :].rearrange("p (j n) -> p j n", n=P)
                V.tensor_tensor(ob, ob, rs[:, b, :].unsqueeze(2).broadcast_to([P, NH, P]), ALU.mult).then_inc(s_norm, 1)

        dve.wait_ge(hg_og, NH * NB)
        head_norms(0)
        dve.sem_inc(s_hn, 1)
        to_channels(T_hgo)
        split(2)
        layer_norm(accb, A_HG)

        def mlp(g0, ts, width, off, down_halves):
            for u in range(len(ts) // NB):
                split()
                for b in range(NB):
                    s = NB * u + b
                    wait_act()
                    if u >= 1:
                        dve.wait_ge(s_T, ts[s - NB] + 1)
                    V.tensor_tensor(stage[:, b, 0:width], half[:, b, 0:width], up[:, b, off:off + width],
                                    ALU.mult).then_inc(s_st, 1)
                split()
                if u >= 1:
                    split(down_halves)
                for b in range(NB):
                    turn_lo(hTl[:, b, 0:width], hTh[:, b, 0:width], tp[:, ts[NB * u + b] % 2, 0:width])

        to_channels(T_ff)
        split(2)
        mlp(g_ff, t_ff, HALF, HALF, 1)
        layer_norm(accb, A_FF)

        dve.wait_ge(s_small, SMALL)
        lr = lam[:, 0:256].rearrange("p (a n) -> p a n", a=4)
        link(V.tensor_tensor(lr[:, 0, :], lr[:, 0, :], lr[:, 1, :], ALU.mult))
        link(V.tensor_tensor(lr[:, 2, :], lr[:, 2, :], lr[:, 3, :], ALU.mult))
        link(V.tensor_reduce(lam[:, 256:257], lr[:, 0, :], AX.X, ALU.add))
        link(V.tensor_reduce(lam[:, 257:258], lr[:, 2, :], AX.X, ALU.add))
        dve.sem_inc(s_lbD, 1)
        dve.wait_ge(s_lbA, 1 + 2 * NB + 1)
        link(V.tensor_tensor(lam[:, 258:259], lam[:, 257:258], lam[:, 256:257], ALU.subtract))
        link(V.tensor_scalar(lam[:, 259:260], lam[:, 258:259], -LAM_INIT, None, ALU.add))
        nlam = lam[:, 259:260]
        dve.wait_ge(s_gn, 32)
        link(V.tensor_scalar(gn[:, :], gn[:, :], 1.0 - LAM_INIT, None, ALU.mult))
        tmp = flat(half[:, :, :]).rearrange("p (i u n) -> p i u n", i=4, u=8)
        to_channels(T_da)
        split(1)
        for s in range(12):
            g, c, b = g_da + s, s // NB, s % NB
            if b == 0:
                split()
            dve.wait_ge(s_up, g + 1)
            src = up[:, g % 2, :]
            if c < 4:
                if s >= 2:
                    dve.wait_ge(s_T, t_da[s - 2] + 1)
                x = src.rearrange("p (u m n) -> p u m n", m=2, n=32)
                dst = stage[:, g % 2, :].rearrange("p (u m n) -> p u m n", m=2, n=32)
                cos, sin = (cst[:, k + 32 * b:k + 32 * b + 32].unsqueeze(1).broadcast_to([P, 8, 32]) for k in (C_COS, C_SIN))
                V.tensor_tensor(tmp[:, 0], x[:, :, 0, :], cos, ALU.mult)
                V.tensor_tensor(tmp[:, 1], x[:, :, 1, :], sin, ALU.mult)
                V.tensor_tensor(tmp[:, 2], x[:, :, 1, :], cos, ALU.mult)
                link(V.tensor_tensor(tmp[:, 3], x[:, :, 0, :], sin, ALU.mult))
                V.tensor_tensor(dst[:, :, 0, :], tmp[:, 0], tmp[:, 1], ALU.subtract)
                link(V.tensor_tensor(dst[:, :, 1, :], tmp[:, 2], tmp[:, 3], ALU.add))
                dve.sem_inc(s_st, 1)
            else:
                V.tensor_copy(v[:, b, (c - 4) * W:(c - 3) * W], src).then_inc(s_st, 1)
            if b == NB - 1:
                split()

        NA = NH * NB

        def maxima(n, w):
            link(V.tensor_reduce(att[:, n % 2, 0:2], at_s[:, n % 2, :, 0:w], AX.X, ALU.max, negate=True))
            dve.sem_inc(at_sm, 1)

        for n in range(NA + 3):
            if n < NA:
                b = n % NB
                w = P * (b + 1)
                dve.wait_ge(at_S, n + 1)
                if n >= 2:
                    dve.wait_ge(at_e, n - 1)
                link(V.scalar_tensor_tensor(at_s[:, n % 2, :, 0:w],
                                            score_banks(n)[:, :, 0:w], 0.125,
                                            causal[:, SEQ - w:SEQ].unsqueeze(1).broadcast_to([P, 2, w]), ALU.mult, ALU.add))
                maxima(n, w)
            if 1 <= n <= NA:
                m = n - 1
                w = P * (m % NB + 1)
                dve.wait_ge(at_e, m + 1)
                if m >= 2:
                    dve.wait_ge(at_T, m - 1)
                a = att[:, m % 2, :]
                link(V.reciprocal(a[:, 4:6], a[:, 2:4]))
                link(V.tensor_scalar(a[:, 5:6], a[:, 5:6], nlam, None, ALU.mult))
                st = stage[:, m % 2, 0:w]
                link(V.tensor_scalar(st, at_p[:, m % 2, 0, 0:w], a[:, 4:5], None, ALU.mult))
                link(V.scalar_tensor_tensor(st, at_p[:, m % 2, 1, 0:w], a[:, 5:6], st, ALU.mult, ALU.add))
                dve.sem_inc(at_w, 1)
            if 3 <= n:
                m = n - 3
                j, b = m // NB, m % NB
                dve.wait_ge(at_sq, m + 1)
                V.tensor_tensor(o[:, b, j * P:(j + 1) * P], acc[:, m % 2, 0:P], gn[:, :], ALU.mult).then_inc(at_og, 1)
        dve.wait_ge(at_og, NA)
        head_norms(3)
        to_channels(T_dao)
        split(2)
        layer_norm(accb, A_DA)
        to_channels(T_moe)

        dve.wait_ge(s_rl, 1)
        L, one1, one2, w1, w2, tot, G = (rt[:, i] for i in range(7))
        d21 = rt[:, 7, :, 0:1]
        m1, m2, r1, r2 = (rt[:, 8 + i, :, 0:1] for i in range(4))
        key = cst[:, C_KEY:C_KEY + NE].unsqueeze(1).broadcast_to([P, NB, NE])
        wide = lambda a: a.broadcast_to([P, NB, NE])
        link(V.tensor_copy(L, up[:, 0, 0:NB * NE].rearrange("p (b n) -> p b n", b=NB)))
        for mx, r, oh, wk, src in ((m1, r1, one1, w1, L), (m2, r2, one2, w2, w1)):
            link(V.tensor_reduce(mx, src, AX.X, ALU.max))
            link(V.tensor_tensor(oh, src, wide(mx), ALU.is_equal))
            link(V.tensor_tensor(oh, oh, key, ALU.mult))
            link(V.tensor_reduce(r, oh, AX.X, ALU.max))
            link(V.tensor_tensor(oh, oh, wide(r), ALU.is_equal))
            if oh is one1:
                link(V.tensor_scalar(wk, oh, NEG, None, ALU.mult))
                link(V.tensor_tensor(wk, wk, src, ALU.add))
        link(V.tensor_tensor(d21, m1, m2, ALU.subtract))
        link(V.tensor_tensor(tot, one1, one2, ALU.add))
        dve.sem_inc(s_ra, 1)
        dve.wait_ge(s_rp, 1)
        link(V.tensor_tensor(G, one1, wide(d21), ALU.mult))
        link(V.tensor_scalar(d21, d21, -1.0, 1.0, ALU.mult, ALU.add))
        link(V.tensor_tensor(w1, one2, wide(d21), ALU.mult))
        link(V.tensor_tensor(gate[:, :, 0:NE], G, w1, ALU.add))
        dve.wait_ge(s_rl, 2)
        link(V.tensor_tensor(w2, tot, up[:, 1, 0:NB * NE].rearrange("p (b n) -> p b n", b=NB), ALU.mult))
        link(V.tensor_scalar(slot[:, :, 0:NE], w2, -1.0, None, ALU.add))
        over, rank = ex[:, 0, :], ex[:, 1, :]
        link(V.tensor_scalar(over, up[:, 1, NB * NE:(NB + 1) * NE], float(P), None, ALU.is_gt))
        link(V.tensor_copy(rank, over))
        for e in range(1, NE):
            link(V.tensor_tensor(rank[:, e:e + 1], rank[:, e - 1:e], over[:, e:e + 1], ALU.add))
        link(V.tensor_copy(extra[:, 0:1], rank[:, NE - 1:NE]))
        for j in range(MAX_EXTRA):
            oh, wk = ex[:, 2, :], rt[:, 12]
            ohw = oh.unsqueeze(1).broadcast_to([P, NB, NE])
            link(V.tensor_scalar(oh, rank, float(j + 1), None, ALU.is_equal))
            link(V.tensor_tensor(oh, oh, over, ALU.mult))
            link(V.tensor_tensor(ex[:, 3, :], oh, cst[:, C_EVAL:C_EVAL + NE], ALU.mult))
            link(V.tensor_reduce(extra[:, 1 + j:2 + j], ex[:, 3, :], AX.X, ALU.add))
            link(V.tensor_tensor(wk, w2, ohw, ALU.mult))
            link(V.tensor_reduce(slot[:, :, NE + j:NE + j + 1], wk, AX.X, ALU.add))
            link(V.tensor_scalar(slot[:, :, NE + j], slot[:, :, NE + j], -1.0 - P, None, ALU.add))
            link(V.tensor_tensor(wk, gate[:, :, 0:NE], ohw, ALU.mult))
            link(V.tensor_reduce(gate[:, :, NE + j:NE + j + 1], wk, AX.X, ALU.add))
        link(V.tensor_copy(extra_i[:, :], extra[:, :]))
        for b in range(NB):
            ins = V.tensor_scalar(y[:, b, :], h[:, b, :], ALPHA, None, ALU.mult)
        link(ins)
        dve.sem_inc(s_rd, 1)

        def expert(m, i, first):
            dve.wait_ge(m["gath"], i * 2 + 1)
            dve.wait_ge(m["turned"], i + 1)
            for b in range(NB):
                V.tensor_scalar(pick[:, b, :], iota, slot[:, b, bass.ds(i + first, 1)], None, ALU.is_equal)
            for b in range(NB):
                ins = V.tensor_scalar(give[:, b, :], iota, slot[:, b, bass.ds(i + first, 1)],
                                      gate[:, b, bass.ds(i + first, 1)], ALU.is_equal, ALU.mult)
            ins.then_inc(m["picked"], 1)

            def split_half(x):
                dve.wait_ge(m["hi"], i * NHALF + (x + 1))
                V.tensor_tensor(wl[:, x % SPLITS, :], raw[:, x % RAW, :],
                                wh[:, x % SPLITS, :].bitcast(F32), ALU.subtract).then_inc(m["lo"], 1)

            split_half(0)
            split_half(1)
            for q in range(2):
                dve.wait_ge(m["xgh"], i * 2 + (q + 1))
                V.tensor_tensor(xgl[:, 4 * q:4 * q + 4, :], tp[:, q, :].rearrange("p (k n) -> p k n", k=4),
                                xgh[:, 4 * q:4 * q + 4, :].bitcast(F32), ALU.subtract).then_inc(m["xg"], 1)
            split_half(2)
            for s in range(EU + 1):
                if s > 0:
                    dve.wait_ge(m["Th"], i * EU + s)
                    V.tensor_tensor(hTl[:, (s - 1) % 2, 0:HALF], tp[:, (s - 1) % 2, 0:HALF],
                                    hTh[:, (s - 1) % 2, 0:HALF].bitcast(F32), ALU.subtract).then_inc(m["Te"], 1)
                if 1 <= s < EU - 1:
                    split_half(gate_half(s + 1, 0))
                if s == EU:
                    break
                dve.wait_ge(m["act"], i * EU + (s + 1))
                if s >= 2:
                    dve.wait_ge(m["T"], i * EU + (s - 1))
                V.tensor_tensor(stage[:, s % 2, 0:HALF], half[:, s % 2, 0:HALF], up[:, s % 2, HALF:W],
                                ALU.mult).then_inc(m["st"], 1)
                if s < EU - 1:
                    split_half(gate_half(s + 1, 1))
                split_half(down_half(s))
            for n in range(4):
                dve.wait_ge(m["give"], i * 4 + (n + 1))
                dve.wait_ge(m["added"], i * 4 + 1)
                yb = y[:, n // 2, (n % 2) * W:(n % 2 + 1) * W]
                V.tensor_tensor(yb, yb, acc[:, 2 + n % 2, :], ALU.add).then_inc(m["added"], 1)

        for m in moe:
            dve.sem_inc(m["added"], 1)
            dve.sem_inc(m["Te"], 1)
            dve.sem_inc(m["lo"], RAW)
        with dve.Fori(0, NE) as i:
            expert(moe[0], i, 0)
        dve.wait_ge(moe[0]["added"], 4 * NE + 1)
        n_extra = dve.value_load(extra_i[0:1, 0:1], min_val=0, max_val=MAX_EXTRA)
        with dve.If(n_extra > 0):
            with dve.Fori(0, n_extra) as j:
                expert(moe[1], j, NE)
            dve.wait_ge(moe[1]["added"], n_extra * 4 + 1)
            dve.sem_inc(s_xdone, 1)
        layer_norm(y)
        last_split = len(pl.halves)
        split(1)

        def rms(dst, src_ready):
            for b in range(NB):
                if src_ready:
                    dve.sem_inc(s_nD, 1)
                    nst[0] += 1
                nst[1] += 1
                dve.wait_ge(s_nA, nst[1])
                r = root(b, sc[:, b, 2:3], 1.0 / D, RMS_EPS)
                V.tensor_scalar(dst[:, b, :], h[:, b, :], r, None, ALU.mult).then_inc(s_norm, 1)

        hn = o

        link(V.memset(uT[:, :, 0:PADC], 0.0))

        def tap(j, tiles):
            for k in tiles:
                src = uT[:, k, j:j + SEQ]
                if j == 0:
                    ins = V.tensor_scalar(cT[:, k, :], src, wdw[:, k, 0:1], rowcols[:, 0, k:k + 1], ALU.mult, ALU.add)
                else:
                    ins = V.scalar_tensor_tensor(cT[:, k, :], src, wdw[:, k, j:j + 1], cT[:, k, :], ALU.mult, ALU.add)
            link(ins)

        rms(hn, True)
        to_channels(T_cv, 0)
        split(2)
        nrows[0] += 32
        dve.wait_ge(s_rows, nrows[0])
        r2 = rows[:, :].rearrange("p (m n) -> p m n", m=2)
        for s in range(8):
            g, c, b = g_cv + s, s // NB, s % NB
            if b == 0:
                split()
            dve.wait_ge(s_up, g + 1)
            hf = half[:, g % 2, :]
            link(V.tensor_tensor(hf.rearrange("p (m n) -> p m n", m=2), up[:, g % 2, :].rearrange("p (m n) -> p m n", m=2),
                                 r2[:, :, c * HALF:(c + 1) * HALF], ALU.add))
            dve.sem_inc(cv_n, 1)
            wait_act()
            if s >= 2:
                dve.wait_ge(s_T, t_cv[s - 2] + 1)
            V.tensor_tensor(stage[:, g % 2, 0:HALF], hf[:, 0:HALF], hf[:, HALF:W], ALU.mult).then_inc(s_st, 1)
            if b == NB - 1:
                split()
                if c >= 2:
                    dve.wait_ge(s_Te, t_cv[1] + 1)
                    for j in range(EARLY * (c - 2), EARLY * (c - 1)):
                        tap(j, CV_DVE[0:2])
        dve.sem_inc(s_rows_free, 1)
        dve.wait_ge(s_Te, T_cback)
        for j in range(CONV):
            tap(j, CV_DVE[2:] if j < 2 * EARLY else CV_DVE)
        dve.sem_inc(cv_dw, 1)
        for b in range(NB):
            dve.wait_ge(s_Te, T_cback + 2 * b + 2)
            r = root(b, stats(b, ctm[:, b, :]), 1.0, RMS_EPS)
            V.tensor_scalar(ctm[:, b, :], ctm[:, b, :], mv[:, b, 0:1], r, ALU.subtract, ALU.mult).then_inc(s_norm, 1)
        to_channels(T_cn, None, stage)
        split(2)
        nrows[0] += 32
        dve.wait_ge(s_rows, nrows[0])
        for b in range(NB):
            dve.wait_ge(s_acc, A_PW2 + b + 1)
            ins = V.tensor_tensor(h[:, b, :], accb[:, b, :], rows[:, 0:D], ALU.add)
        link(ins)

        for i, d in enumerate(after):
            if i == 1:
                rms(hn, True)
                to_channels(d["T_q"], 2)
                for s in range(8):
                    g, c, b = d["g_kv"] + s, s // NB, s % NB
                    if b == 0:
                        split()
                    dve.wait_ge(s_up, g + 1)
                    if c < 2:
                        if s >= 2:
                            dve.wait_ge(s_T, d["t_kv"][s - 2] + 1)
                        dst = stage[:, g % 2, :]
                    else:
                        dst = v[:, b, (c - 2) * W:(c - 1) * W]
                    V.tensor_copy(dst, up[:, g % 2, :]).then_inc(s_st, 1)
                    if b == NB - 1:
                        split()
                for b in range(NB):
                    g = d["g_f"] + b
                    dve.wait_ge(s_up, g + 1)
                    V.tensor_tensor(fx[:, 0, b, :], up[:, g % 2, 0:NH2], bf[:, :], ALU.add).then_inc(s_st, 1)
                dve.wait_ge(s_st, d["g_f"] + NB)
                dve.sem_inc(f_D, 1)
                link(V.tensor_scalar(fx[:, 3], fx[:, 0], 0.0, None, ALU.min))
                to_channels(d["T_q2"], 1)
                dve.wait_ge(f_A, 1)
                link(V.tensor_tensor(fx[:, 4], fx[:, 3], fx[:, 2], ALU.subtract))
                dve.sem_inc(f_D, 1)
                for s in range(4):
                    g = d["g_q"] + s
                    if s % NB == 0:
                        split()
                    dve.wait_ge(s_up, g + 1)
                    if s >= 2:
                        dve.wait_ge(s_T, d["t_q"][s - 2] + 1)
                    V.tensor_scalar(stage[:, g % 2, :], up[:, g % 2, :], HD2 ** -0.5, None, ALU.mult).then_inc(s_st, 1)
                    if s % NB == NB - 1:
                        split()
                dve.wait_ge(f_C, 1)
                cb = fx[:, 5]
                link(V.tensor_copy(cb, up[:, 0, 0:NB * NH2].rearrange("p (b n) -> p b n", b=NB)))
                dve.sem_inc(f_D, 1)
                for n in range(NA + 3):
                    if n < NA:
                        j, b = n // NB, n % NB
                        w = P * (b + 1)
                        dve.wait_ge(at_S, NA + n + 1)
                        if n >= 2:
                            dve.wait_ge(at_e, NA + n - 1)
                        for c in range(2):
                            ins = V.scalar_tensor_tensor(at_s[:, n % 2, c, 0:w], score_banks(n)[:, c, 0:w],
                                                         cb[:, b, 2 * j + c:2 * j + c + 1], causal[:, SEQ - w:SEQ],
                                                         ALU.add, ALU.add)
                        link(ins)
                        maxima(n, w)
                    if 3 <= n:
                        m = n - 3
                        j, b = m // NB, m % NB
                        dve.wait_ge(at_O, NA + m + 1)
                        a = fx[:, 6, 0, 2 * (m % 4):2 * (m % 4) + 2]
                        V.tensor_tensor(o[:, b, j * P:(j + 1) * P].rearrange("p (c n) -> p c n", c=2),
                                        acc[:, m % 2, 0:P].rearrange("p (c n) -> p c n", c=2),
                                        a.unsqueeze(2).broadcast_to([P, 2, HD2]), ALU.mult).then_inc(at_og, 1)
                    if 1 <= n <= NA:
                        m = n - 1
                        dve.wait_ge(at_e, NA + m + 1)
                        link(V.reciprocal(fx[:, 6, 0, 2 * (m % 4):2 * (m % 4) + 2], att[:, m % 2, 2:4]))
                        dve.sem_inc(at_w, 1)
                dve.wait_ge(at_og, 2 * NA)
                dve.sem_inc(s_norm, NB)
                to_channels(d["T_o"])
                split(2)
                rms(hn, False)
            else:
                rms(hn, True)
            to_channels(d["T_f"], 3 + i)
            split(2)
            mlp(d["g_ff"], d["t_ff"], W, 0, 2)
            rms(hn, False)
            turn_lo(hTl[:, 0, :], hTh[:, 0, :], tp[:, d["T_p"] % 2, :])
            to_channels(d["T_g"], 5)
            split(2)
            split()
            for s in range(4):
                g, c, b = d["g_p"] + s, s // NB, s % NB
                if b == 0:
                    split()
                wait_act()
                link(V.tensor_tensor(stage[:, g % 2, :], half[:, g % 2, :], acc[:, s, :], ALU.mult))
                hb = h[:, b, c * W:(c + 1) * W]
                link(V.tensor_tensor(hb, hb, stage[:, g % 2, :], ALU.add))
                dve.sem_inc(s_st, 1)
                if b == NB - 1:
                    split()
            dve.sem_inc(s_norm, NB)
        for b in range(NB):
            dve.sem_inc(s_nD, 1)
            nst[0] += 1
            nst[1] += 1
            dve.wait_ge(s_nA, nst[1])
            r = root(b, sc[:, b, 2:3], 1.0 / D, RMS_EPS)
            V.scalar_tensor_tensor(o[:, b, :], h[:, b, :], r, rows[:, D:2 * D], ALU.mult, ALU.mult).then_inc(s_norm, 1)

    @block.tensor
    def _(pe):
        mm = nc.tensor.matmul

        def turn_bank(tt):
            if tt >= 2:
                pe.wait_ge(s_Te, tt - 1)

        def turn_rows(t0, src, ready):
            for b in range(NB):
                ready(b)
                for q in range(2):
                    tt = t0 + 2 * b + q
                    turn_bank(tt)
                    for k in range(4):
                        ins = nc.tensor.transpose(tp[:, tt % 2, k * P:(k + 1) * P],
                                                  src[:, b, (4 * q + k) * P:(4 * q + k + 1) * P], ident)
                    ins.then_inc(s_T, 1)

        def normed(n):
            return lambda b: pe.wait_ge(s_norm, n + b + 1)

        def split_product(out, x_hi, x_lo, w_hi, w_lo, start, stop):
            mm(out, x_hi, w_hi, start=start, stop=False)
            mm(out, x_hi, w_lo, start=False, stop=False)
            return mm(out, x_lo, w_hi, start=False, stop=stop)

        uses = 0

        def next_half(n):
            nonlocal uses
            q = uses
            uses += 1
            return q, [w[:, q % SPLITS, :].rearrange("p (k n) -> p k n", k=n) for w in (wh, wl)]

        def half_products(out, b, w, part, start=True):
            for k in range(4):
                x = 4 * part + k, slice(b * P, (b + 1) * P)
                ins = split_product(out, xTh[:, x[0], x[1]], xTl[:, x[0], x[1]], w[0][:, k, :], w[1][:, k, :],
                                    start and x[0] == 0, x[0] == KT - 1)
            return ins

        def turn_step(g, tt, nk):
            pe.wait_ge(s_st, g + 1)
            turn_bank(tt)
            for k in range(nk):
                ins = nc.tensor.transpose(tp[:, tt % 2, k * P:(k + 1) * P], stage[:, g % 2, k * P:(k + 1) * P], ident)
            ins.then_inc(s_T, 1)

        def xT_ready(b, t0):
            pe.wait_ge(s_Te, t0 + 2 * b + 2)

        def unit(g0, c, t0, behind=None):
            q, w = next_half(4)
            pe.wait_ge(s_lo, q + 1)
            for b in range(NB):
                g = g0 + NB * c + b
                if c == 0 and t0 is not None:
                    xT_ready(b, t0)
                if g >= 2:
                    pe.wait_ge(s_st, g - 1)
                ins = half_products(up[:, g % 2, :], b, w, 0)
            ins.then_inc(s_used, 1)
            if behind is not None:
                behind(c - 1)
            q, w = next_half(4)
            pe.wait_ge(s_lo, q + 1)
            for b in range(NB):
                half_products(up[:, (g0 + b) % 2, :], b, w, 1).then_inc(s_up, 1)

        def project(g0, ts, chunks, t0, nk):
            def behind(c):
                for b in range(NB):
                    s = NB * c + b
                    if s >= 0 and ts[s] is not None:
                        turn_step(g0 + s, ts[s], nk)

            for c in range(chunks):
                unit(g0, c, t0, behind)
            behind(chunks - 1)

        def residual(scale):
            for b in range(NB):
                for n in range(2):
                    mm(acc[:, 2 * b + n, :], scale, h[:, b, n * W:(n + 1) * W], start=True, stop=False)

        def out_product(t0, scale):
            residual(scale)
            for part in range(2):
                q, w = next_half(4)
                pe.wait_ge(s_lo, q + 1)
                for b in range(NB):
                    if part == 0:
                        xT_ready(b, t0)
                    ins = half_products(acc[:, 2 * b, :], b, w, part, False)
                ins.then_inc(s_used, 1)
            halves = [next_half(4) for _ in range(2)]
            for b in range(NB):
                for part, (q, w) in enumerate(halves):
                    pe.wait_ge(s_lo, q + 1)
                    ins = half_products(acc[:, 2 * b + 1, :], b, w, part, False)
                    if part == 1:
                        ins.then_inc(s_acc, 1)
                    elif b == NB - 1:
                        ins.then_inc(s_used, 1)

        def mlp(g0, ts, t0, tiles, down_halves):
            units = len(ts) // NB

            def down(u, b, w, x, ready):
                if ready:
                    pe.wait_ge(s_Te, ts[NB * u + b] + 1)
                for k in range(2):
                    t_ = slice((2 * x + k) * P, (2 * x + k + 1) * P)
                    for n in range(2):
                        c_ = slice(n * W, (n + 1) * W)
                        ins = split_product(acc[:, 2 * b + n, :], hTh[:, b, t_], hTl[:, b, t_], w[0][:, k, c_], w[1][:, k, c_],
                                            False, u == units - 1 and x == down_halves - 1 and k == 1)
                return ins

            for u in range(units + 1):
                if u < units:
                    unit(g0, u, t0)
                if 1 <= u < units:
                    for x in range(down_halves):
                        q, w = next_half(2)
                        pe.wait_ge(s_lo, q + 1)
                        for b in range(NB):
                            ins = down(u - 1, b, w, x, x == 0)
                        ins.then_inc(s_used, 1)
                if u < units:
                    for b in range(NB):
                        turn_step(g0 + NB * u + b, ts[NB * u + b], tiles)
            halves = [next_half(2) for _ in range(down_halves)]
            for b in range(NB):
                for x, (q, w) in enumerate(halves):
                    pe.wait_ge(s_lo, q + 1)
                    ins = down(units - 1, b, w, x, x == 0)
                    if x == down_halves - 1:
                        ins.then_inc(s_acc, 1)
                    elif b == NB - 1:
                        ins.then_inc(s_used, 1)

        pe.wait_ge(s_cst, 16)
        turn_rows(T_x, h, lambda b: pe.wait_ge(s_x, 16))
        project(g_hg, t_hg, 8, T_x, 4)
        pe.wait_ge(s_lbA, 1 + 2 * NB)
        pe.wait_ge(s_big, 16)
        lev = big[:, H_LEV:H_END]
        for n in range(NH * NB + 2):
            if n < NH * NB:
                j, b = n // NB, n % NB
                if n >= 1:
                    pe.wait_ge(hg_ab, n)
                for q in range(2):
                    ins = mm(acc[:, q, :], lf[:, b, j * P:(j + 1) * P], lev[:, b * P + q * W:b * P + (q + 1) * W],
                             start=True, stop=True)
                ins.then_inc(hg_m, 1)
            if 1 <= n <= NH * NB:
                m = n - 1
                j, b = m // NB, m % NB
                first = 1 - b
                pe.wait_ge(hg_ab, m + 1)
                if m >= 1:
                    pe.wait_ge(hg_sm, m)
                A, B = hgA[:, m % 2], hgB[:, m % 2]
                if b == 1:
                    if m >= 4:
                        pe.wait_ge(hg_sm, m - 3)
                    mm(tp[:, j % 2, 0:P], hgB[:, 0, 0, :], A[:, 7, :], start=True, stop=True)
                for l in range(7):
                    mm(acc[:, 2 + l // 4, (l % 4) * P:(l % 4 + 1) * P], B[:, first + l, :], A[:, first + l, :],
                       start=True, stop=True)
                qk = slice(b * P, (b + 1) * P)
                mm(acc[:, 3, 3 * P:4 * P], kT[:, j, qk], qT[:, j, qk], start=True, stop=True).then_inc(hg_s, 1)
            if 2 <= n:
                m = n - 2
                j, b = m // NB, m % NB
                pe.wait_ge(hg_sm, m + 1)
                if m >= 2:
                    pe.wait_ge(hg_og, m - 1)
                if b == 1:
                    mm(up[:, m % 2, 0:P], hgX, v[:, 0, j * P:(j + 1) * P], start=True, stop=False)
                for l in range(8):
                    ins = mm(up[:, m % 2, 0:P], hgS[:, l, :], v[:, b, j * P:(j + 1) * P], start=(l == 0 and b == 0),
                             stop=(l == 7))
                ins.then_inc(hg_o, 1)
        turn_rows(T_hgo, o, normed(N_HGO))
        out_product(T_hgo, aident)

        turn_rows(T_ff, h, normed(N_LN0))
        residual(aident)
        mlp(g_ff, t_ff, T_ff, 2, 1)

        turn_rows(T_da, h, normed(N_LN1))
        project(g_da, t_da, 6, T_da, 4)
        NA = NH * NB

        def attention(base, scores, turns, outs):
            for n in range(-1, NA + 2):
                if n + 1 < NA:
                    if n >= 1:
                        pe.wait_ge(at_sm, base + n)
                    scores(n + 1, (n + 1) // NB, (n + 1) % NB).then_inc(at_S, 1)
                if 1 <= n <= NA:
                    m = n - 1
                    pe.wait_ge(at_w, base + m + 1)
                    if m >= 2:
                        pe.wait_ge(at_Te, base + m - 1)
                    turns(m, m % NB).then_inc(at_T, 1)
                if 2 <= n:
                    m = n - 2
                    pe.wait_ge(at_Te, base + m + 1)
                    if m >= 2:
                        pe.wait_ge(at_og, base + m - 1)
                    outs(m, m // NB, m % NB).then_inc(at_O, 1)

        def da_scores(n, j, b):
            for c in range(2):
                r = slice(64 * c, 64 * c + 64)
                ins = mm(score_banks(n)[:, c, 0:P * (b + 1)], qT[r, j, b * P:(b + 1) * P], kT[r, j, 0:P * (b + 1)],
                         start=True, stop=True)
            return ins

        def da_turns(m, b):
            for kb in range(b + 1):
                ins = nc.tensor.transpose(tp[:, m % 2, kb * P:(kb + 1) * P], stage[:, m % 2, kb * P:(kb + 1) * P], ident)
            return ins

        def da_outs(m, j, b):
            for kb in range(b + 1):
                ins = mm(acc[:, m % 2, 0:P], half[:, m % 2, kb * P:(kb + 1) * P], v[:, kb, j * P:(j + 1) * P],
                         start=(kb == 0), stop=(kb == b))
            return ins

        pe.wait_ge(s_Te, T_dao)
        pe.wait_ge(s_st, g_da + 12)
        attention(0, da_scores, da_turns, da_outs)
        turn_rows(T_dao, o, normed(N_DAO))
        out_product(T_dao, aident)

        turn_rows(T_moe, h, normed(N_LN2))
        pe.wait_ge(s_small, SMALL)
        for b in range(NB):
            xT_ready(b, T_moe)
            for k in range(KT):
                for x in (xTh, xTl):
                    ins = mm(up[:, 0, b * NE:(b + 1) * NE], x[:, k, b * P:(b + 1) * P].bitcast(F32), wr[:, k, :],
                             start=(k == 0 and x is xTh), stop=(k == KT - 1 and x is xTl))
        ins.then_inc(s_rl, 1)
        pe.wait_ge(s_ra, 1)
        tot = rt[:, 5]
        mm(up[:, 1, 0:NE], tri, tot[:, 0, :], start=True, stop=True)
        mm(up[:, 1, NE:2 * NE], ones, tot[:, 0, :], start=True, stop=False)
        mm(up[:, 1, NE:2 * NE], tri, tot[:, 1, :], start=False, stop=True)
        mm(up[:, 1, 2 * NE:3 * NE], ones, tot[:, 0, :], start=True, stop=False)
        mm(up[:, 1, 2 * NE:3 * NE], ones, tot[:, 1, :], start=False, stop=True).then_inc(s_rl, 1)

        def expert(m, i):
            pe.wait_ge(m["picked"], i + 1)
            pe.wait_ge(m["Te"], i * EU + 1)
            for q in range(2):
                for k in range(4 * q, 4 * q + 4):
                    for b in range(NB):
                        ins = mm(tp[:, q, (k % 4) * P:(k % 4 + 1) * P], h[:, b, k * P:(k + 1) * P], pick[:, b, :],
                                 start=(b == 0), stop=(b == NB - 1))
                ins.then_inc(m["gath"], 1)
            pe.wait_ge(m["added"], i * 4 + 1)
            for b in range(NB):
                ins = nc.tensor.transpose(acc[:, 2, b * P:(b + 1) * P], give[:, b, :], ident)
            ins.then_inc(m["turned"], 1)
            def split_ready(x):
                pe.wait_ge(m["lo"], i * NHALF + (RAW + x + 1))

            def gate_up(s, part):
                x = gate_half(s, part)
                split_ready(x)
                w_hi, w_lo = (w[:, x % SPLITS, :].rearrange("p (k n) -> p k n", k=4) for w in (wh, wl))
                for k in range(4):
                    kk = 4 * part + k
                    ins = split_product(up[:, s % 2, :], xgh[:, kk, :], xgl[:, kk, :], w_hi[:, k, :], w_lo[:, k, :],
                                        kk == 0, kk == KT - 1)
                return ins

            for s in range(EU + 1):
                if s < EU:
                    if s >= 2:
                        pe.wait_ge(m["st"], i * EU + (s - 1))
                    if s == 0:
                        pe.wait_ge(m["xg"], i * 2 + 1)
                    gate_up(s, 0).then_inc(m["used"], 1)
                if s >= 1:
                    pe.wait_ge(m["st"], i * EU + s)
                    if s >= 3:
                        pe.wait_ge(m["Te"], i * EU + (s - 1))
                    for k in range(2):
                        ins = nc.tensor.transpose(tp[:, (s - 1) % 2, k * P:(k + 1) * P],
                                                  stage[:, (s - 1) % 2, k * P:(k + 1) * P], ident)
                    ins.then_inc(m["T"], 1)
                if s < EU:
                    if s == 0:
                        pe.wait_ge(m["xg"], i * 2 + 2)
                    gate_up(s, 1).then_inc(m["up"], 1)
                if s >= 1:
                    u = s - 1
                    x = down_half(u)
                    split_ready(x)
                    w_hi, w_lo = (w[:, x % SPLITS, :].rearrange("p (k n) -> p k n", k=2) for w in (wh, wl))
                    pe.wait_ge(m["Te"], i * EU + (s + 1))
                    if u == 0:
                        pe.wait_ge(m["ye"], i + 1)
                    for n in range(2):
                        for k in range(2):
                            t_, c_ = slice(k * P, (k + 1) * P), slice(n * W, (n + 1) * W)
                            ins = split_product(acc[:, n, :], hTh[:, u % 2, t_], hTl[:, u % 2, t_], w_hi[:, k, c_],
                                                w_lo[:, k, c_], u == 0 and k == 0, u == EU - 1 and k == 1)
                    ins.then_inc(m["down"] if u == EU - 1 else m["used"], 1)
            pe.wait_ge(m["ye"], i + 2)
            pe.wait_ge(m["giveT"], i + 1)
            for n in range(4):
                if n >= 2:
                    pe.wait_ge(m["added"], i * 4 + n)
                mm(acc[:, 2 + n % 2, :], giveT[:, n // 2, :], ye[:, (n % 2) * W:(n % 2 + 1) * W],
                   start=True, stop=True).then_inc(m["give"], 1)

        for m in moe:
            pe.sem_inc(m["gath"], 1)
            pe.sem_inc(m["turned"], 1)
        with pe.Fori(0, NE) as i:
            expert(moe[0], i)
        pe.wait_ge(s_rd, 1)
        n_extra = pe.value_load(extra_i[0:1, 0:1], min_val=0, max_val=MAX_EXTRA)
        with pe.If(n_extra > 0):
            with pe.Fori(0, n_extra) as j:
                expert(moe[1], j)

        turn_rows(T_cv, o, normed(N_RC))
        project(g_cv, t_cv, 4, T_cv, 2)
        pe.wait_ge(s_Te, T_cback)
        pe.wait_ge(s_st, g_cv + 8)
        for i, k in enumerate(CV_PE):
            if i >= 2:
                pe.wait_ge(cv_sum, i - 1)
            for j in range(CONV):
                x = CONV * i + j
                pe.wait_ge(cv_diag, x + 1)
                mm(up[:, k % 2, 0:SEQ], diag[:, x % DIAGS, :], uT[:, k, j:j + SEQ], start=(j == 0),
                   stop=(j == CONV - 1)).then_inc(cv_tap, 1)
        pe.wait_ge(cv_dw, 1)
        pe.wait_ge(cv_sum, len(CV_PE))
        for b in range(NB):
            for q in range(2):
                tt = T_cback + 2 * b + q
                turn_bank(tt)
                for k in range(4):
                    ins = nc.tensor.transpose(tp[:, tt % 2, k * P:(k + 1) * P], cT[:, 4 * q + k, b * P:(b + 1) * P], ident)
                ins.then_inc(s_T, 1)
        turn_rows(T_cn, ctm, normed(N_CB))
        out_product(T_cn, ident)

        for i, d in enumerate(after):
            if i == 1:
                turn_rows(d["T_q"], o, normed(N_AFTER[i]["q"]))
                project(d["g_kv"], d["t_kv"], 4, d["T_q"], 4)
                for b in range(NB):
                    g = d["g_f"] + b
                    pe.wait_ge(s_st, g - 1)
                    for k in range(KT):
                        for x in (xTh, xTl):
                            ins = mm(up[:, g % 2, 0:NH2], x[:, k, b * P:(b + 1) * P].bitcast(F32), wf[:, k, :],
                                     start=(k == 0 and x is xTh), stop=(k == KT - 1 and x is xTl))
                    ins.then_inc(s_up, 1)
                turn_rows(d["T_q2"], o, lambda b: None)
                project(d["g_q"], d["t_q"], 2, d["T_q2"], 4)
                pe.wait_ge(f_D, 2)
                pe.wait_ge(s_Te, d["T_o"])
                lg = fx[:, 4]
                mm(up[:, 0, 0:NH2], tri, lg[:, 0, :], start=True, stop=True)
                mm(up[:, 0, NH2:2 * NH2], ones, lg[:, 0, :], start=True, stop=False)
                mm(up[:, 0, NH2:2 * NH2], tri, lg[:, 1, :], start=False, stop=True).then_inc(f_C, 1)
                pe.wait_ge(f_D, 3)
                for b in range(NB):
                    ins = nc.tensor.transpose(tp[0:NH2, 0, b * P:(b + 1) * P], fx[:, 5, b, :], ident)
                ins.then_inc(f_CT, 1)
                pe.wait_ge(f_ct, 1)
                pe.wait_ge(s_headrow, 16)

                def fox_scores(n, j, b):
                    w = P * (b + 1)
                    for c in range(2):
                        r = slice(64 * c, 64 * c + 64)
                        out = score_banks(n)[:, c, 0:w]
                        mm(out, qT[r, j, b * P:(b + 1) * P], kT[r, j, 0:w], start=True, stop=False)
                        ins = mm(out, headrow[:, 2 * j + c, :], ncT[:, 0:w], start=False, stop=True)
                    return ins

                def fox_turns(m, b):
                    for c in range(2):
                        for kb in range(b + 1):
                            at = (c * (b + 1) + kb) * P
                            ins = nc.tensor.transpose(tp[:, m % 2, at:at + P], at_p[:, m % 2, c, kb * P:(kb + 1) * P], ident)
                    return ins

                def fox_outs(m, j, b):
                    for c in range(2):
                        for kb in range(b + 1):
                            at = (c * (b + 1) + kb) * P
                            ins = mm(acc[:, m % 2, c * HD2:(c + 1) * HD2], half[:, m % 2, at:at + P],
                                     v[:, kb, (2 * j + c) * HD2:(2 * j + c + 1) * HD2], start=(kb == 0), stop=(kb == b))
                    return ins

                attention(NA, fox_scores, fox_turns, fox_outs)
                turn_rows(d["T_o"], o, normed(N_AFTER[i]["o"]))
                out_product(d["T_o"], ident)
            turn_rows(d["T_f"], o, normed(N_AFTER[i]["f"]))
            residual(ident)
            mlp(d["g_ff"], d["t_ff"], d["T_f"], 4, 2)
            pe.wait_ge(s_pe, 16 if i == 0 else 48)
            turn_bank(d["T_p"])
            for k in range(2):
                for b in range(NB):
                    ins = nc.tensor.transpose(tp[:, d["T_p"] % 2, (2 * k + b) * P:(2 * k + b + 1) * P],
                                              pe_tm[:, b, k * P:(k + 1) * P], ident)
            ins.then_inc(s_T, 1)
            turn_rows(d["T_g"], o, normed(N_AFTER[i]["g"]))
            q, w = next_half(2)
            pe.wait_ge(s_lo, q + 1)
            pe.wait_ge(s_Te, d["T_p"] + 1)
            for s in range(4):
                c, b = s // NB, s % NB
                for k in range(2):
                    ins = split_product(acc[:, s, :], pe_Th[:, k, b * P:(b + 1) * P], pe_Tl[:, k, b * P:(b + 1) * P],
                                        w[0][:, k, c * W:(c + 1) * W], w[1][:, k, c * W:(c + 1) * W], k == 0, k == 1)
            ins.then_inc(s_used, 1)
            project(d["g_p"], [None] * 4, 2, d["T_g"], 4)


USED = ["x", "hg_w_in", "hg_lb", "hg_norm_g", "hg_w_out", "da_w_in", "da_lam", "da_norm_g", "da_w_out",
        "ffn_w_gate", "ffn_w_up", "ffn_w_down", "moe_w_router", "moe_w_gate", "moe_w_up", "moe_w_down",
        "ln_g", "ln_b", "p_2", "mix_norm_2", "conv_w_pw1_2", "conv_b_pw1_2", "conv_w_dw_2", "conv_b_dw_2",
        "conv_ln_g_2", "conv_ln_b_2", "conv_w_pw2_2", "conv_b_pw2_2", "kv_norm_2", "w_kvf_2", "b_f_2",
        "attn_w_q_2", "attn_w_o_2", "ffn_norm_2", "ffn_w1_2", "ffn_w2_2", "ple_norm_2", "ple_w_gate_2",
        "ple_w_proj_2", "final_norm_2"]


def declare(nc, inputs):
    arrays, t = {}, {}
    consts, hg_tables = constant_table()
    given = {n: inputs[n] for n in USED} | {"consts": consts, "hg_tables": hg_tables, "headrow": head_rows()}
    for name, a in given.items():
        a = np.ascontiguousarray(a)
        arrays[f"in_{name}"] = a
        t[name] = nc.dram_tensor(f"in_{name}", a.shape, mybir.dt.from_np(a.dtype), kind="ExternalInput").ap()
    t["out"] = nc.dram_tensor("out", (1, SEQ, D), F32, kind="ExternalOutput").ap()
    build(nc, t)
    return arrays


def kernel(**inputs):
    import concourse.bacc as _bacc
    from concourse.bass_utils import run_bass_kernel_spmd as _run

    nc = _bacc.Bacc("TRN2", target_bir_lowering=False, num_devices=1)
    arrays = declare(nc, inputs)
    return _run(nc, [arrays], core_ids=[0]).results[0]["out"]
```

```python
import math
from contextlib import ExitStack

import numpy as np

import concourse.bass as bass
from concourse import mybir

P = 128
D = 1024
SEQ = 256
NB = SEQ // P
KT = D // P
NH = 8
DEPTH = 2
W = 512
HALF = W // 2
D_FF, D_FFE = 2816, 3584
NE = 8
NH2, HD2 = 16, 64
D_PLE = 256
CONV = 31
LN_EPS, RMS_EPS = 1e-5, 1e-6
ALPHA = (2 * DEPTH) ** 0.25
LAM_INIT = 0.8 - 0.6 * math.exp(-0.3)
NEG = -1e30
RING = 3
RAW = 7
SPLITS = 3
CH = KT * W
MAX_EXTRA = SEQ * 2 // (P + 1)

F32 = mybir.dt.float32
F32R = mybir.dt.float32r
I32 = mybir.dt.int32
ALU = mybir.AluOpType
ACT = mybir.ActivationFunctionType
AX = mybir.AxisListType

C_ID, C_AID, C_CAUS = 0, P, 2 * P
C_COS = C_CAUS + 2 * P
C_SIN = C_COS + NB * 32
C_IOTA = C_SIN + NB * 32
C_KEY = C_IOTA + P
C_EVAL = C_KEY + NE
C_ONES = C_EVAL + NE
C_END = C_ONES + P
H_MASK, H_LEV, H_TRI, H_END = 0, 8 * P, 16 * P, 17 * P
LEVELS = [64, 32, 16, 8, 4, 2, 1]


def constant_table():
    c = np.zeros((P, C_END), np.float32)
    i = np.arange(P)
    c[:, C_ID:C_ID + P] = np.eye(P)
    c[:, C_AID:C_AID + P] = ALPHA * np.eye(P)
    u, t = i[:, None], i[None, :]
    lev = [(u > t)]
    mask = []
    for h in LEVELS:
        right = t % (2 * h) >= h
        mid = t // (2 * h) * (2 * h) + h
        lev.append(np.where(right, (u >= mid) & (u <= t), (u > t) & (u < mid)))
        mask.append((u // (2 * h) == t // (2 * h)) & right & (u % (2 * h) < h))
    lev.append(u <= t)
    mask.append(u == t)
    hg = np.concatenate(mask + lev, 1).astype(np.float32)
    c[:, C_CAUS + P:C_CAUS + 2 * P] = np.where(t <= u, 0.0, NEG)
    inv = (10000.0 ** (-np.arange(32, dtype=np.float32) / 32)).astype(np.float32)
    ang = (np.arange(SEQ, dtype=np.float32)[:, None] * inv[None, :]).astype(np.float32)
    for b in range(NB):
        c[:, C_COS + 32 * b:C_COS + 32 * b + 32] = np.cos(ang[b * P:b * P + P])
        c[:, C_SIN + 32 * b:C_SIN + 32 * b + 32] = np.sin(ang[b * P:b * P + P])
    c[:, C_IOTA:C_IOTA + P] = t
    c[:, C_KEY:C_KEY + NE] = NE - np.arange(NE)
    c[:, C_EVAL:C_EVAL + NE] = np.arange(NE)
    c[:, C_ONES:C_ONES + P] = 1.0
    return c, hg


def head_rows():
    return np.repeat(np.eye(NH2, dtype=np.float32)[:, :, None], P, 2)


class Plan:

    def __init__(self):
        self.steps = self.turns = self.chunk = 0
        self.ready = [0] * RING
        self.chunk_ready = {}
        self.last_half = {}
        self.halves = []
        self.told = []
        self.used = self.sums = 0

    def new_chunks(self, n, loads):
        first = self.chunk
        for c in range(first, first + n):
            self.ready[c % RING] += loads[c - first]
            self.chunk_ready[c] = 16 * self.ready[c % RING]
        self.chunk += n
        return first

    def use(self, chunk, part, told=None):
        if told is None:
            self.used += 1
            told = "used", self.used
        self.last_half[chunk] = len(self.halves)
        self.halves.append((chunk, part))
        self.told.append(told)

    def use_project(self, chunks, g0):
        for i, c in enumerate(chunks):
            self.use(c, 0)
            self.use(c, 1, ("up", g0 + NB * (i + 1)))

    def use_mlp(self, chunks, down, g0):
        self.sums += NB
        for u in range(len(chunks) + 1):
            if u < len(chunks):
                self.use(chunks[u], 0)
                self.use(chunks[u], 1, ("up", g0 + NB * (u + 1)))
            if u >= 1:
                for x in down[u - 1]:
                    last = u == len(chunks) and x is down[u - 1][-1]
                    self.use(*x, ("acc", self.sums) if last else None)

    def use_out(self, c0):
        self.sums += NB
        for x in range(4):
            self.use(c0 + x // 2, x % 2, ("acc", self.sums) if x == 3 else None)

    def take_turns(self, n):
        t = self.turns
        self.turns += n
        return t

    def take_steps(self, turned):
        g, t = self.steps, []
        for x in turned:
            t.append(self.turns if x else None)
            self.turns += bool(x)
        self.steps += len(turned)
        return g, t


def build(nc, t):
    ctx = ExitStack()
    with ctx:
        _program(nc, t, ctx)


def _program(nc, t, ctx):
    def sb(name, shape, dt=F32):
        return ctx.enter_context(nc.sbuf_tensor(name, shape, dt))

    def sem(name):
        return ctx.enter_context(nc.semaphore(name))

    acc = ctx.enter_context(nc.psum_tensor("acc", [P, 4, W], F32))
    up = ctx.enter_context(nc.psum_tensor("up", [P, 2, W], F32))
    tp = ctx.enter_context(nc.psum_tensor("tp", [P, 2, W], F32))

    raw = sb("raw", [P, RAW, CH // 2])
    ring = raw[:, 0:2 * RING, :].rearrange("p (c a) n -> p c (a n)", a=2)
    cst = sb("cst", [P, C_END])
    h = sb("h", [P, NB, D])
    xTh = sb("xTh", [P, KT, SEQ], F32R)
    xTl = sb("xTl", [P, KT, SEQ], F32R)
    big = sb("big", [P, H_END])
    rows = big[:, 0:2 * D]
    stage = sb("stage", [P, 2, W])
    half = sb("half", [P, 2, W])
    spare = raw[:, 2 * RING, :]
    wh = sb("wh", [P, SPLITS, CH // 2], F32R)
    wl = sb("wl", [P, SPLITS, CH // 2], F32R)
    hTh = sb("hTh", [P, 2, W], F32R)
    hTl = sb("hTl", [P, 2, W], F32R)
    arena = sb("arena", [P, 5, 2 * D])
    cols = sb("cols", [P, 6, KT])
    rowcols = sb("rowcols", [P, 3, KT])
    wdw = sb("wdw", [P, KT, CONV])
    wr = sb("wr", [P, KT, NE])
    wf = sb("wf", [P, KT, NH2])
    wrh, wrl = (sb(n, [P, KT, NE], F32R) for n in ("wrh", "wrl"))
    wfh, wfl = (sb(n, [P, KT, NH2], F32R) for n in ("wfh", "wfl"))
    bnd = sb("bnd", [P, 2, 6])
    mv = sb("mv", [P, NB, 2])
    sc = sb("sc", [P, NB, 8])
    ss = sb("ss", [P, NB, NH])
    rs = sb("rs", [P, NB, NH])
    lam = sb("lam", [P, 4 * 64 + 8])
    gn = sb("gn", [P, P])
    att = sb("att", [P, 2, 8])
    rt = sb("rt", [P, 16, NB, NE])
    ex = sb("ex", [P, 8, NE])
    slot = sb("slot", [P, NB, NE + MAX_EXTRA])
    gate = sb("gate", [P, NB, NE + MAX_EXTRA])
    extra = sb("extra", [P, 1 + MAX_EXTRA])
    extra_i = sb("extra_i", [P, 1 + MAX_EXTRA], I32)
    fx = sb("fx", [P, 8, NB, NH2])
    ncT = sb("ncT", [NH2, SEQ])
    few = ncT
    bf = sb("bf", [P, NH2])

    ident = cst[:, C_ID:C_ID + P]
    aident = cst[:, C_AID:C_AID + P]
    ones = cst[:, C_ONES:C_ONES + P]
    tri = big[:, H_TRI:H_TRI + P]
    iota = cst[:, C_IOTA:C_IOTA + P]
    causal = cst[:, C_CAUS:C_CAUS + 2 * P]
    accb = acc[:, :, :].rearrange("p (b n) w -> p b (n w)", b=NB)

    lf, kT_, qT_, v_, o_ = (arena[:, i, :] for i in range(5))
    as_tm = lambda a: a.rearrange("p (b n) -> p b n", b=NB)
    as_cm = lambda a: a.rearrange("p (k n) -> p k n", k=KT)
    lf, v, o = as_tm(lf), as_tm(v_), as_tm(o_)
    qT, kT = as_cm(qT_), as_cm(kT_)
    flat = lambda a: a.rearrange("p a b -> p (a b)")
    hg_raw = flat(arena[:, 0:2, :])[:, 0:3 * D].rearrange("p (r n) -> p r n", r=3)
    lb, omlb = spare[:, 0:D], spare[:, D:2 * D]
    HG_SLOT = 7 % RING
    hgA, hgB = (ring[:, HG_SLOT, i * 2 * D:(i + 1) * 2 * D].rearrange("p (i s n) -> p i s n", i=2, s=8) for i in range(2))
    hgS = flat(half[:, :, :]).rearrange("p (s n) -> p s n", s=8)
    hgX = stage[:, 0, 0:P]
    hg_far = stage[:, 1, 0:2 * P].rearrange("p (i n) -> p i n", i=2)
    lev = hTh, hTl
    lfh, lfl = (a[:, :, :].rearrange("p k n -> p (k n)").rearrange("p (b n) -> p b n", b=NB) for a in (xTh, xTl))
    at_s = arena[:, 0, 0:D].rearrange("p (i c n) -> p i c n", i=2, c=2)
    at_p = arena[:, 0, D:2 * D].rearrange("p (i c n) -> p i c n", i=2, c=2)
    headrow = spare[0:NH2, :].rearrange("p (h q) -> p h q", h=NH2)
    give_banks = [acc[:, 2, :], acc[:, 3, :], up[:, 0, :], up[:, 1, :]]
    xgh, xgl = xTh[:, :, 0:P], xTl[:, :, 0:P]
    y = as_tm(arena[:, 0, :])
    ye = arena[:, 1, D:2 * D]
    pick = arena[:, 2, 0:2 * P].rearrange("p (b n) -> p b n", b=NB)
    give = arena[:, 2, 2 * P:4 * P].rearrange("p (b n) -> p b n", b=NB)
    giveT = arena[:, 2, 4 * P:6 * P].rearrange("p (b n) -> p b n", b=NB)
    PADC = CONV - 1
    uT = flat(arena[:, 0:2, :])[:, 0:KT * (SEQ + PADC)].rearrange("p (k n) -> p k n", k=KT)
    cT = as_cm(arena[:, 2, :])
    ctm = as_tm(arena[:, 3, :])
    CV_DVE, CV_PE = range(4), range(4, KT)
    DIAGS = 2 * D // P
    diag = arena[:, 3, :].rearrange("p (i n) -> p i n", i=DIAGS)
    EARLY = 6
    squares = arena[:, 3, D:2 * D]
    pe_tm = arena[:, 3, 0:2 * D_PLE].rearrange("p (b n) -> p b n", b=NB)
    pe_Th, pe_Tl = (a[:, 0, :].rearrange("p (k n) -> p k n", k=2) for a in (hTh, hTl))

    def level_banks(n):
        return acc[:, 0:2, :] if n % 2 == 0 else tp[:, :, :]

    hg_cross = tp[:, 0, 0:P]

    def score_banks(n):
        return up if n % 2 == 0 else acc[:, 2:4, :]

    def ring_k(c, n=KT):
        return ring[:, c % RING, :].rearrange("p (k n) -> p k n", k=n)

    def ring_gu(c):
        return ring[:, c % RING, :].rearrange("p (k m n) -> p k m n", k=KT, m=2)

    pl = Plan()
    one = lambda n: [1] * n
    T_x = pl.take_turns(4)
    HG_CHUNKS = [0, 1, 4, 5, 2, 3, 6, 7]
    c_hg = pl.new_chunks(8, one(8))
    g_hg, t_hg = pl.take_steps([c < 4 for c in HG_CHUNKS for _ in range(NB)])
    pl.use_project([c_hg + i for i in range(8)], g_hg)
    T_hgo = pl.take_turns(4)
    c_hgo = pl.new_chunks(2, one(2))
    pl.use_out(c_hgo)
    T_ff = pl.take_turns(4)
    FF_UNITS = D_FF // HALF
    c_ff = pl.new_chunks(17, [1 if i % 3 == 2 or i == 16 else 2 for i in range(17)])
    ff_gu = [c_ff + 3 * (u // 2) + u % 2 for u in range(FF_UNITS)]
    ff_d = [c_ff + 3 * (u // 2) + (2 if u // 2 < FF_UNITS // 2 else 1) for u in range(FF_UNITS)]
    g_ff, t_ff = pl.take_steps([1] * (FF_UNITS * NB))
    pl.use_mlp(ff_gu, [[(ff_d[u], u % 2)] for u in range(FF_UNITS)], g_ff)
    T_da = pl.take_turns(4)
    c_da = pl.new_chunks(6, one(6))
    g_da, t_da = pl.take_steps([c < 4 for c in range(6) for _ in range(NB)])
    pl.use_project([c_da + i for i in range(6)], g_da)
    T_dao = pl.take_turns(4)
    c_dao = pl.new_chunks(2, one(2))
    pl.use_out(c_dao)
    T_moe = pl.take_turns(4)
    pl.chunk += -pl.chunk % RING
    EU = D_FFE // HALF
    before_moe = len(pl.halves)
    assert before_moe % SPLITS == 0
    c_after = pl.chunk
    G, DN = 0, 1
    HALVES = [(G, 0, 0), (G, 0, 1)]
    for u in range(1, EU):
        HALVES += [(G, u, 0), (G, u, 1), (DN, u - 1, 0)]
    HALVES.append((DN, EU - 1, 0))
    NHALF = len(HALVES)
    half_at = {x: m for m, x in enumerate(HALVES)}
    gate_half = lambda u, part: half_at[G, u, part]
    down_half = lambda u: half_at[DN, u, 0]
    assert NHALF % RAW == 0 and NHALF % SPLITS == 0
    half_loads = [2 if x[0] == G else 1 for x in HALVES]
    slot_loads = [sum(half_loads[r::RAW]) for r in range(RAW)]
    tells_used = lambda m: m < NHALF - 1 and not (HALVES[m][0] == G and HALVES[m][2] == 1)
    used_until = lambda m: sum(map(tells_used, range(m + 1)))
    NUSED = used_until(NHALF - 1)
    T_cv = pl.take_turns(4)
    c_pw1 = pl.new_chunks(4, [2] * 4)
    g_cv, t_cv = pl.take_steps([1] * 8)
    pl.use_project([c_pw1 + i for i in range(4)], g_cv)
    T_cback = pl.take_turns(4)
    T_cn = pl.take_turns(4)
    c_pw2 = pl.new_chunks(2, one(2))
    pl.use_out(c_pw2)
    after = []
    for i in range(DEPTH):
        d = {}
        if i == 1:
            d["T_q"] = pl.take_turns(4)
            d["c_k"] = pl.new_chunks(4, one(4))
            d["g_kv"], d["t_kv"] = pl.take_steps([1] * 4 + [0] * 4)
            d["g_f"], _ = pl.take_steps([0] * 2)
            pl.use_project([d["c_k"] + c for c in range(4)], d["g_kv"])
            d["T_q2"] = pl.take_turns(4)
            d["c_q"] = pl.new_chunks(2, one(2))
            d["g_q"], d["t_q"] = pl.take_steps([1] * 4)
            pl.use_project([d["c_q"] + c for c in range(2)], d["g_q"])
            d["T_o"] = pl.take_turns(4)
            d["c_o"] = pl.new_chunks(2, one(2))
            pl.use_out(d["c_o"])
        d["T_f"] = pl.take_turns(4)
        d["c_f"] = pl.new_chunks(16, one(16))
        d["g_ff"], d["t_ff"] = pl.take_steps([1] * 16)
        pl.use_mlp([d["c_f"] + 2 * u for u in range(8)],
                   [[(d["c_f"] + 2 * u + 1, x) for x in range(2)] for u in range(8)], d["g_ff"])
        d["T_p"] = pl.take_turns(1)
        d["T_g"] = pl.take_turns(4)
        d["c_p"] = pl.new_chunks(3, one(3))
        d["g_p"], _ = pl.take_steps([0] * 4)
        pl.use(d["c_p"], 0)
        pl.use_project([d["c_p"] + 1, d["c_p"] + 2], d["g_p"])
        after.append(d)

    def half_ready(eng, m, i, x):
        eng.wait_ge(m["ready"][x % RAW], i * (16 * slot_loads[x % RAW]) + 16 * sum(half_loads[x % RAW:x + 1:RAW]))

    w_ready = [sem(f"w_ready{s}") for s in range(RING)]
    s_hi = sem("s_hi")
    s_lo = sem("s_lo")
    s_used = sem("s_used")
    s_Th = sem("s_Th")
    s_cst = sem("s_cst")
    s_first = sem("s_first")
    s_big = sem("s_big")
    s_x = sem("s_x")
    s_small = sem("s_small")
    s_gn = sem("s_gn")
    s_lb = sem("s_lb")
    s_rows = sem("s_rows")
    s_rows_free = sem("s_rows_free")
    s_pe = sem("s_pe")
    s_headrow = sem("s_headrow")
    s_up = sem("s_up")
    s_act = sem("s_act")
    s_st = sem("s_st")
    s_T = sem("s_T")
    s_Te = sem("s_Te")
    s_acc = sem("s_acc")
    s_norm = sem("s_norm")
    s_nA = sem("s_nA")
    s_nD = sem("s_nD")
    d_ch = sem("d_ch")
    a_ch = sem("a_ch")
    s_lbA, s_lbD = sem("s_lbA"), sem("s_lbD")
    hg_m, hg_e, hg_ab, hg_s, hg_sm, hg_o, hg_sq, hg_og = (
        sem(n) for n in ("hg_decay", "hg_exp", "hg_scaled", "hg_scores", "hg_masked", "hg_out", "hg_square", "hg_gated"))
    at_S, at_sm, at_e, at_w, at_T, at_Te, at_O, at_sq, at_og = (
        sem(n) for n in ("at_scores", "at_masked", "at_exp", "at_weights", "at_turned", "at_copied", "at_out",
                         "at_square", "at_kept"))
    s_hn = sem("s_hn")
    s_rl, s_rp, s_ra, s_rd = sem("router_logits"), sem("router_places"), sem("router_act"), sem("router_done")
    moe = [{n: sem(f"{p}{n}") for n in ("picked", "gath", "xg", "turned", "giveT", "up", "act", "st", "T", "Te",
                                        "hi", "lo", "used", "xgh", "Th", "down", "ye", "give", "added")} for p in ("m_", "x_")]
    for m, p_ in zip(moe, ("m_", "x_")):
        m["ready"] = [sem(f"{p_}ready{r}") for r in range(RAW)]
    cv_dw, cv_n = sem("conv_done"), sem("conv_normed")
    cv_diag, cv_tap, cv_sum = sem("conv_diagonals"), sem("conv_taps"), sem("conv_sums")
    f_L, f_A, f_D, f_C, f_CT, f_ct = (sem(n) for n in ("f_logits", "f_act", "f_vec", "f_sum", "f_sumT", "f_sumT_sb"))
    s_wh, s_wl = sem("s_wh"), sem("s_wl")
    hg_lev = sem("hg_lev")
    hg_x = sem("hg_x")
    hg_fh, hg_fl = sem("hg_fh"), sem("hg_fl")
    s_few = sem("s_few")
    s_y = sem("s_y")
    s_over = sem("s_over")
    p_ch = sem("p_ch")
    s_xdone = sem("s_xdone")
    s_out = sem("s_out")

    told_by = {"used": s_used, "up": s_up, "acc": s_acc}

    def raw_half(q):
        c, part = pl.halves[q]
        return ring[:, c % RING, part * (CH // 2):(part + 1) * (CH // 2)]

    block = ctx.enter_context(nc.Block())

    N_HGO, N_LN0, N_LN1, N_DAO, N_LN2 = (NB * i for i in range(5))
    N_RC = 6 * NB
    N_AFTER = []
    n = N_RC + NB
    N_CB = n
    n += NB
    for i in range(DEPTH):
        d = {}
        if i == 1:
            d["q"] = n
            n += NB
            d["o"] = n
            n += NB
        d["f"] = n
        n += NB
        d["g"] = n
        n += NB
        d["h"] = n
        n += NB
        N_AFTER.append(d)
    N_FIN = n
    A_HG, A_FF, A_DA = 0, NB, 2 * NB
    A_PW2 = 3 * NB
    A_F0, A_O1, A_F1 = 4 * NB, 5 * NB, 6 * NB

    @block.sync
    def _(sp):
        ld = lambda out, in_, s: sp.dma_start(out, in_).then_inc(s, 16)
        kp = lambda w: w.rearrange("(k p) n -> p k n", p=P)

        def wait_slot(c):
            if RING <= c < c_after or c >= c_after + RING:
                sp.wait_ge(s_lo, pl.last_half[c - RING] + 1)

        def cols_chunk(c, w, col):
            wait_slot(c)
            ld(ring_k(c), kp(w[:, col:col + W]), w_ready[c % RING])

        def pair_chunk(c, wa, wb, col):
            wait_slot(c)
            ld(ring_gu(c)[:, :, 0, :], kp(wa[:, col:col + HALF]), w_ready[c % RING])
            ld(ring_gu(c)[:, :, 1, :], kp(wb[:, col:col + HALF]), w_ready[c % RING])

        def rows_chunk(c, w, row, n):
            wait_slot(c)
            ld(ring_k(c, 4)[:, 0:n, :], kp(w[row:row + n * P, :]), w_ready[c % RING])

        ld(h[:, :, :], t["x"][0].rearrange("(b p) n -> p b n", p=P), s_x)
        ld(cst[:, :], t["consts"], s_cst)
        for i, c in enumerate(HG_CHUNKS):
            if i == 0:
                for part, ready in enumerate((s_first, w_ready[0])):
                    ld(ring_k(c_hg)[:, 4 * part:4 * part + 4, :],
                       kp(t["hg_w_in"][part * (D // 2):(part + 1) * (D // 2), c * W:(c + 1) * W]), ready)
            else:
                cols_chunk(c_hg + i, t["hg_w_in"], c * W)
            if i == 2:
                ld(big[:, :], t["hg_tables"], s_big)
        for i in range(2):
            cols_chunk(c_hgo + i, t["hg_w_out"], i * W)
        sp.wait_ge(hg_o, NH * NB)
        for u in range(FF_UNITS):
            pair_chunk(ff_gu[u], t["ffn_w_gate"][0], t["ffn_w_up"][0], u * HALF)
            if u % 2 == 1:
                rows_chunk(ff_d[u], t["ffn_w_down"][0], (u - 1) * HALF, 4)
            elif u == FF_UNITS - 1:
                rows_chunk(ff_d[u], t["ffn_w_down"][0], u * HALF, 2)
        for i in range(6):
            cols_chunk(c_da + i, t["da_w_in"], i * W)
        for i in range(2):
            cols_chunk(c_dao + i, t["da_w_out"], i * W)

        def expert(m, e, i):
            gw, uw, dw = (t[n][0, bass.ds(e, 1), :, :].rearrange("a k n -> (a k) n")
                          for n in ("moe_w_gate", "moe_w_up", "moe_w_down"))
            for x, (kind, u, part) in enumerate(HALVES):
                sp.wait_ge(m["lo"], i * NHALF + (x + 1))
                dst, ready = raw[:, x % RAW, :], m["ready"][x % RAW]
                if kind == G:
                    dst = dst.rearrange("p (k m n) -> p k m n", k=KT // 2, m=2)
                    for j, w in enumerate((gw, uw)):
                        ld(dst[:, :, j, :], kp(w[part * (D // 2):(part + 1) * (D // 2), u * HALF:(u + 1) * HALF]), ready)
                else:
                    ld(dst.rearrange("p (k n) -> p k n", k=2), kp(dw[u * HALF:(u + 1) * HALF, :]), ready)

        sp.wait_ge(s_lo, before_moe)
        with sp.Fori(0, NE) as e:
            expert(moe[0], e, e)

        sp.wait_ge(s_rd, 1)
        sp.wait_ge(moe[0]["lo"], NE * NHALF + RAW)
        n_extra = sp.value_load(extra_i[0:1, 0:1], min_val=0, max_val=MAX_EXTRA)
        with sp.If(n_extra > 0):
            with sp.Fori(0, n_extra) as j:
                e = sp.value_load(extra_i[0:1, bass.ds(j + 1, 1)], min_val=0, max_val=NE - 1)
                expert(moe[1], e, j)
            sp.wait_ge(moe[1]["lo"], n_extra * NHALF + RAW)
            sp.sem_inc(s_xdone, 1)

        for i in range(4):
            pair_chunk(c_pw1 + i, t["conv_w_pw1_2"][0][:, 0:D], t["conv_w_pw1_2"][0][:, D:2 * D], i * HALF)
        for i in range(2):
            cols_chunk(c_pw2 + i, t["conv_w_pw2_2"][0], i * W)
        for i, d in enumerate(after):
            if i == 1:
                for c in range(4):
                    cols_chunk(d["c_k"] + c, t["w_kvf_2"], c * W)
                for c in range(2):
                    cols_chunk(d["c_q"] + c, t["attn_w_q_2"][0], c * W)
                for c in range(2):
                    cols_chunk(d["c_o"] + c, t["attn_w_o_2"][0], c * W)
            for u in range(8):
                cols_chunk(d["c_f"] + 2 * u, t["ffn_w1_2"][i], u * W)
                rows_chunk(d["c_f"] + 2 * u + 1, t["ffn_w2_2"][i], u * W, 4)
            wait_slot(d["c_p"])
            rows_chunk(d["c_p"], t["ple_w_proj_2"][i], 0, 2)
            for c in range(2):
                cols_chunk(d["c_p"] + 1 + c, t["ple_w_gate_2"][i], c * W)

        for b in range(NB):
            sp.wait_ge(s_norm, N_FIN + b + 1)
            ld(t["out"][0, b * P:(b + 1) * P, :], o[:, b, :], s_out)
        sp.wait_ge(s_out, 16 * NB)

    SMALL = 0

    @block.gpsimd
    def _(pool):
        nonlocal SMALL

        def small(out, in_):
            nonlocal SMALL
            pool.dma_start(out, in_).then_inc(s_small, 16)
            SMALL += 16

        bc = lambda row: row.partition_broadcast(P)
        pool.wait_ge(s_first, 16)
        pool.dma_start(hg_raw, t["hg_lb"].rearrange("r n -> (r n)").partition_broadcast(P)
                       .rearrange("p (r n) -> p r n", r=3)).then_inc(s_lb, 16)

        def load_rows(*srcs):
            for i, s in enumerate(srcs):
                pool.dma_start(rows[:, i * D:(i + 1) * D], bc(s)).then_inc(s_rows, 16)

        with nc.allow_non_contiguous_dma(reason="small parameters"):
            pool.dma_start(gn[:, :], bc(t["hg_norm_g"])).then_inc(s_gn, 16)
            small(lam[:, 0:256], bc(t["da_lam"].rearrange("a n -> (a n)")))
            small(wr[:, :, :], t["moe_w_router"][0].rearrange("(k p) n -> p k n", p=P))
            small(wf[:, :, :], t["w_kvf_2"][:, 2 * D:2 * D + NH2].rearrange("(k p) n -> p k n", p=P))
            small(bf[:, :], bc(t["b_f_2"]))
            for i, a in enumerate((t["mix_norm_2"][0], t["mix_norm_2"][1], t["kv_norm_2"],
                                   t["ffn_norm_2"][0], t["ffn_norm_2"][1], t["ple_norm_2"][0])):
                small(cols[:, i, :], a.rearrange("(k p) -> p k", p=P))
            for i, a in enumerate((t["conv_b_dw_2"][0], t["conv_ln_g_2"][0], t["conv_ln_b_2"][0])):
                small(rowcols[:, i, :], a.rearrange("(k p) -> p k", p=P))
            for k in range(KT):
                small(wdw[:, k, :], t["conv_w_dw_2"][0][:, k * P:(k + 1) * P].rearrange("j p -> p j"))
            pool.wait_ge(hg_o, NH * NB)
            load_rows(t["ln_g"][0, 0], t["ln_b"][0, 0])
            for i, s in enumerate(((t["ln_g"][0, 1], t["ln_b"][0, 1]), (t["ln_g"][1, 0], t["ln_b"][1, 0]),
                                   (t["ln_g"][1, 1], t["ln_b"][1, 1]))):
                pool.wait_ge(s_rows_free, i + 1)
                load_rows(*s)
                if i == 0:
                    pool.dma_start(gn[:, :], bc(t["da_norm_g"])).then_inc(s_gn, 16)
            chain = 0

            def link(ins):
                nonlocal chain
                chain += 1
                ins.then_inc(p_ch, 1)
                pool.wait_ge(p_ch, chain)

            def total(out, a):
                for n in (4, 2):
                    link(nc.gpsimd.tensor_tensor(a[..., 0:n], a[..., 0:n], a[..., n:2 * n], ALU.add))
                link(nc.gpsimd.tensor_tensor(out, a[..., 0:1], a[..., 1:2], ALU.add))

            over, rank = ex[:, 0, :], ex[:, 1, :]
            w2 = rt[:, 4]
            pool.wait_ge(s_over, 1)
            link(nc.gpsimd.tensor_copy(rank, over))
            for e in range(1, NE):
                link(nc.gpsimd.tensor_tensor(rank[:, e:e + 1], rank[:, e - 1:e], over[:, e:e + 1], ALU.add))
            link(nc.gpsimd.tensor_copy(extra[:, 0:1], rank[:, NE - 1:NE]))
            for j in range(MAX_EXTRA):
                oh, wk = ex[:, 2, :], rt[:, 12]
                ohw = oh.unsqueeze(1).broadcast_to([P, NB, NE])
                link(nc.gpsimd.tensor_scalar(oh, rank, float(j + 1), None, ALU.is_equal))
                link(nc.gpsimd.tensor_tensor(oh, oh, over, ALU.mult))
                link(nc.gpsimd.tensor_tensor(ex[:, 3, :], oh, cst[:, C_EVAL:C_EVAL + NE], ALU.mult))
                total(extra[:, 1 + j:2 + j], ex[:, 3, :])
                link(nc.gpsimd.tensor_tensor(wk, w2, ohw, ALU.mult))
                total(slot[:, :, NE + j:NE + j + 1], wk)
                link(nc.gpsimd.tensor_scalar(slot[:, :, NE + j], slot[:, :, NE + j], -1.0 - P, None, ALU.add))
                link(nc.gpsimd.tensor_tensor(wk, gate[:, :, 0:NE], ohw, ALU.mult))
                total(gate[:, :, NE + j:NE + j + 1], wk)
            link(nc.gpsimd.tensor_copy(extra_i[:, :], extra[:, :]))
            pool.sem_inc(s_rd, 1)
            pool.wait_ge(s_rows_free, 4)
            load_rows(t["conv_b_pw1_2"][0][0:D], t["conv_b_pw1_2"][0][D:2 * D])
            pool.wait_ge(s_rows_free, 5)
            load_rows(t["conv_b_pw2_2"][0], t["final_norm_2"])
            pool.wait_ge(s_T, T_cn + 4)
            pool.dma_start(pe_tm, t["p_2"][0, 0].rearrange("(b p) n -> p b n", p=P)).then_inc(s_pe, 16)
            pool.wait_ge(s_norm, N_AFTER[0]["h"] + NB)
            pool.dma_start(cols[:, 5, :], t["ple_norm_2"][1].rearrange("(k p) -> p k", p=P)).then_inc(s_pe, 16)
            pool.wait_ge(s_up, after[1]["g_f"] + NB)
            pool.dma_start(headrow, t["headrow"]).then_inc(s_headrow, 16)
            pool.wait_ge(s_T, after[1]["T_o"] + 4)
            pool.dma_start(pe_tm, t["p_2"][1, 0].rearrange("(b p) n -> p b n", p=P)).then_inc(s_pe, 16)

    @block.scalar
    def _(act):
        f = nc.scalar.activation
        chain = 0

        def link(ins):
            nonlocal chain
            chain += 1
            ins.then_inc(a_ch, 1)
            act.wait_ge(a_ch, chain)

        def copy_turn(t_, out, in_):
            act.wait_ge(s_T, t_ + 1)
            f(out, in_, ACT.Copy).then_inc(s_Te, 1)

        nsplit, last_split = 0, before_moe

        def split(n=1):
            nonlocal nsplit
            for _ in range(n):
                q = nsplit
                if q == last_split:
                    return
                c, part = pl.halves[q]
                if q == 0:
                    act.wait_ge(s_first, 16)
                else:
                    act.wait_ge(w_ready[c % RING], pl.chunk_ready[c])
                if q >= SPLITS and not before_moe <= q < before_moe + SPLITS:
                    told, count = pl.told[q - SPLITS]
                    act.wait_ge(told_by[told], count)
                f(wh[:, q % SPLITS, :], raw_half(q), ACT.Copy).then_inc(s_hi, 1)
                nsplit += 1

        def turn_hi(tt, out, in_, **kw):
            act.wait_ge(s_T, tt + 1)
            f(out, in_, ACT.Copy, **kw).then_inc(s_Th, 1)

        def to_channels(t0, gain=None):
            for b in range(NB):
                for q in range(2):
                    tt = t0 + 2 * b + q
                    dst = xTh[:, 4 * q:4 * q + 4, b * P:(b + 1) * P]
                    src = tp[:, tt % 2, :].rearrange("p (k n) -> p k n", k=4)
                    if gain is None:
                        turn_hi(tt, dst, src)
                    else:
                        act.wait_ge(s_T, tt + 1)
                        for k in range(4):
                            ins = f(dst[:, k, :], src[:, k, :], ACT.Copy, scale=cols[:, gain, 4 * q + k:4 * q + k + 1])
                        ins.then_inc(s_Th, 1)

        def step_copy(tt, dst, chunk, b, nk=4):
            copy_turn(tt, dst[:, nk * chunk:nk * chunk + nk, b * P:(b + 1) * P],
                      tp[:, tt % 2, 0:nk * P].rearrange("p (k n) -> p k n", k=nk))

        acts = [0]

        def step_act(g, out, in_, func, **kw):
            act.wait_ge(s_up, g + 1)
            f(out, in_, func, **kw).then_inc(s_act, 1)
            acts[0] += 1

        nsq = [0]
        roots = [0]

        def norm_root(out, in_):
            nsq[0] += 1
            act.wait_ge(s_nD, nsq[0])
            roots[0] += 1
            f(out, in_, ACT.Sqrt).then_inc(s_nA, 1)

        def layer_norms():
            for b in range(NB):
                norm_root(sc[:, b, 1:2], sc[:, b, 0:1])

        def square(b):
            if roots[0] > 0:
                act.wait_ge(s_nA, roots[0])
            roots[0] += 1
            f(squares, h[:, b, :], ACT.Square, accum_out=sc[:, b, 2:3]).then_inc(s_nA, 1)

        to_channels(T_x)
        split(SPLITS)
        for i, c in enumerate(HG_CHUNKS):
            split()
            if i > 0 and HG_CHUNKS[i - 1] < 4:
                for b in range(NB):
                    pc = HG_CHUNKS[i - 1]
                    step_copy(t_hg[NB * (i - 1) + b], kT if pc >= 2 else qT, pc % 2, b)
            if i > 0 and HG_CHUNKS[i - 1] in (2, 3):
                act.wait_ge(s_lbA, 1 + NB * (HG_CHUNKS[i - 1] - 1))
            for b in range(NB):
                g = g_hg + NB * i + b
                func = ACT.Sigmoid if c in (2, 3, 6, 7) else ACT.Silu if c < 2 else ACT.Copy
                step_act(g, half[:, g % 2, :], up[:, g % 2, :], func)
            if c in (2, 3):
                for b in range(NB):
                    act.wait_ge(s_lbD, 2 + (NB * (c - 2) + b) + 1)
                    f(lf[:, b, (c - 2) * W:(c - 1) * W], half[:, (g_hg + b) % 2, :], ACT.Ln).then_inc(s_lbA, 1)
            split()
            if i == 1:
                act.wait_ge(s_lbD, 1)
                for r in range(3):
                    ins = f(hg_raw[:, r, :], hg_raw[:, r, :], ACT.Exp)
                ins.then_inc(s_lbA, 1)
            elif i == 3:
                act.wait_ge(s_big, 16)
                for b in range(NB):
                    f(lev[b][:, :, :], big[:, H_LEV + b * P:H_LEV + b * P + 2 * W].rearrange("p (a n) -> p a n", a=2),
                      ACT.Copy).then_inc(hg_lev, 1)
        act.wait_ge(s_lbA, 1 + 2 * NB)
        for x in range(2 * NB):
            at = slice((x // NB) * W, (x // NB + 1) * W)
            f(lfh[:, x % NB, at], lf[:, x % NB, at], ACT.Copy).then_inc(hg_fh, 1)
        for n in range(NH * NB + 3):
            if n < NH * NB:
                act.wait_ge(hg_m, n + 1)
                f(level_banks(n), level_banks(n), ACT.Exp).then_inc(hg_e, 1)
            if 2 <= n < NH * NB + 2:
                m = n - 2
                j, b = m // NB, m % NB
                act.wait_ge(hg_o, m + 1)
                f(up[:, m % 2, P:2 * P], up[:, m % 2, 0:P], ACT.Square, accum_out=ss[:, b, j:j + 1]).then_inc(hg_sq, 1)
        act.wait_ge(s_hn, 1)
        f(rs[:, :, :], rs[:, :, :], ACT.Sqrt).then_inc(s_hn, 1)
        to_channels(T_hgo)
        split(2)
        layer_norms()

        def mlp(g0, ts, gate, width, down_halves):
            for u in range(len(ts) // NB):
                split()
                for b in range(NB):
                    step_act(g0 + NB * u + b, half[:, b, 0:width], up[:, b, 0:width], gate)
                split()
                if u >= 1:
                    split(down_halves)
                for b in range(NB):
                    tt = ts[NB * u + b]
                    turn_hi(tt, hTh[:, b, 0:width], tp[:, tt % 2, 0:width])

        to_channels(T_ff)
        split(2)
        act.wait_ge(s_lbD, 2 + 2 * NB + 1)
        f(lam[:, 256:258], lam[:, 256:258], ACT.Exp).then_inc(s_lbA, 1)
        for w, w_hi in ((wr, wrh), (wf, wfh)):
            f(w_hi[:, :, :], w[:, :, :], ACT.Copy).then_inc(s_wh, 1)
        mlp(g_ff, t_ff, ACT.Silu, HALF, 1)
        layer_norms()

        to_channels(T_da)
        split(1)
        for c in range(6):
            split()
            if 1 <= c <= 4:
                for b in range(NB):
                    step_copy(t_da[NB * (c - 1) + b], qT if c <= 2 else kT, (c - 1) % 2, b)
            split()

        def exps(n, b, base):
            w = P * (b + 1)
            act.wait_ge(at_sm, base + n + 1)
            for c in range(2):
                ins = f(at_p[:, n % 2, c, 0:w], at_s[:, n % 2, c, 0:w], ACT.Exp, bias=att[:, n % 2, c:c + 1],
                        accum_out=att[:, n % 2, 2 + c:3 + c])
            ins.then_inc(at_e, 1)

        NA = NH * NB
        for n in range(NA + 3):
            if n < NA:
                exps(n, n % NB, 0)
            if 1 <= n <= NA:
                m = n - 1
                w = P * (m % NB + 1)
                act.wait_ge(at_T, m + 1)
                f(half[:, m % 2, 0:w], tp[:, m % 2, 0:w], ACT.Copy).then_inc(at_Te, 1)
            if 2 <= n < NA + 2:
                m = n - 2
                act.wait_ge(at_O, m + 1)
                f(acc[:, m % 2, P:2 * P], acc[:, m % 2, 0:P], ACT.Square,
                  accum_out=ss[:, m % NB, m // NB:m // NB + 1]).then_inc(at_sq, 1)
        act.wait_ge(s_hn, 4)
        f(rs[:, :, :], rs[:, :, :], ACT.Sqrt).then_inc(s_hn, 1)
        to_channels(T_dao)
        split(2)
        layer_norms()

        to_channels(T_moe)
        act.wait_ge(s_rl, 1)
        f(few[0:NE, :], up[0:NE, 0, 0:SEQ], ACT.Copy).then_inc(s_few, 1)
        act.wait_ge(s_ra, 1)
        f(rt[:, 7, :, 0:1], rt[:, 7, :, 0:1], ACT.Sigmoid).then_inc(s_rp, 1)
        f(y, h[:, :, :], ACT.Copy, scale=ALPHA).then_inc(s_y, 1)

        def split_half(m, i, x):
            half_ready(act, m, i, x)
            if x >= SPLITS:
                split_free(m, i, x - SPLITS)
            f(wh[:, x % SPLITS, :], raw[:, x % RAW, :], ACT.Copy).then_inc(m["hi"], 1)

        def split_free(m, i, x):
            if tells_used(x):
                act.wait_ge(m["used"], i * NUSED + used_until(x))
            else:
                act.wait_ge(m["up"], i * EU + (HALVES[x][1] + 1))

        def split_ahead(m, i):
            for x in range(2):
                split_half(m, i, x)

        def expert(m, i, ahead):
            for q in range(2):
                act.wait_ge(m["gath"], i * 2 + (q + 2))
                f(xgh[:, 4 * q:4 * q + 4, :], tp[:, q, :].rearrange("p (k n) -> p k n", k=4), ACT.Copy).then_inc(m["xgh"], 1)
            act.wait_ge(m["turned"], i + 2)
            f(giveT, acc[:, 2, 0:2 * P].rearrange("p (b n) -> p b n", b=NB), ACT.Copy).then_inc(m["giveT"], 1)
            split_half(m, i, 2)
            for s in range(EU + 1):
                if s > 0:
                    act.wait_ge(m["T"], i * EU + s)
                    f(hTh[:, (s - 1) % 2, 0:HALF], tp[:, (s - 1) % 2, 0:HALF], ACT.Copy).then_inc(m["Th"], 1)
                if 1 <= s < EU - 1:
                    split_half(m, i, gate_half(s + 1, 0))
                if s < EU:
                    act.wait_ge(m["up"], i * EU + (s + 1))
                    f(half[:, s % 2, 0:HALF], up[:, s % 2, 0:HALF], ACT.Silu).then_inc(m["act"], 1)
                if s < EU - 1:
                    split_half(m, i, gate_half(s + 1, 1))
                if s < EU:
                    split_half(m, i, down_half(s))
            if ahead:
                for x in range(2):
                    split_free(m, i, NHALF - SPLITS + x)
                    split_half(m, i + 1, x)
            act.wait_ge(m["down"], i + 1)
            f(ye.rearrange("p (a n) -> p a n", a=2), acc[:, 0:2, :], ACT.Copy).then_inc(m["ye"], 1)

        for m in moe:
            act.sem_inc(m["ye"], 1)
        split_ahead(moe[0], 0)
        with act.Fori(0, NE - 1) as i:
            expert(moe[0], i, True)
        expert(moe[0], NE - 1, False)
        act.wait_ge(s_rd, 1)
        n_extra = act.value_load(extra_i[0:1, 0:1], min_val=0, max_val=MAX_EXTRA)
        with act.If(n_extra > 0):
            with act.Fori(0, n_extra) as j:
                split_ahead(moe[1], j)
                expert(moe[1], j, False)
        def rms(from_acc, a0=None):
            if not from_acc:
                for b in range(NB):
                    nsq[0] += 1
                    act.wait_ge(s_nD, nsq[0])
                    square(b)
                layer_norms()
                return
            for b in range(NB):
                act.wait_ge(s_acc, a0 + b + 1)
                link(f(h[:, b, :], accb[:, b, :], ACT.Copy))
                square(b)
                nsq[0] += 1
                act.wait_ge(s_nD, nsq[0])
                roots[0] += 1
                f(sc[:, b, 1:2], sc[:, b, 0:1], ACT.Sqrt).then_inc(s_nA, 1)

        last_split = len(pl.halves)
        for b in range(NB):
            norm_root(sc[:, b, 1:2], sc[:, b, 0:1])
            if b == 0:
                split(1)
            nsq[0] += 1
            act.wait_ge(s_nD, nsq[0])
            square(b)
        layer_norms()

        to_channels(T_cv, 0)
        split(2)
        for c in range(4):
            split()
            if c > 0:
                for b in range(NB):
                    step_copy(t_cv[NB * (c - 1) + b], uT[:, :, PADC:], c - 1, b, 2)
            for b in range(NB):
                act.wait_ge(cv_n, NB * c + b + 1)
                f(half[:, b, HALF:W], half[:, b, HALF:W], ACT.Sigmoid).then_inc(s_act, 1)
            split()
        for b in range(NB):
            step_copy(t_cv[NB * 3 + b], uT[:, :, PADC:], 3, b, 2)

        def conv_sum(i):
            k = CV_PE[i]
            act.wait_ge(cv_tap, CONV * (i + 1))
            f(cT[:, k, :], up[:, k % 2, 0:SEQ], ACT.Identity, bias=rowcols[:, 0, k:k + 1]).then_inc(cv_sum, 1)

        for x in range(CONV * len(CV_PE)):
            if x >= DIAGS:
                act.wait_ge(cv_tap, x - DIAGS + 1)
            if x % CONV == DIAGS and x > CONV:
                conv_sum(x // CONV - 1)
            f(diag[:, x % DIAGS, :], ident, ACT.Copy, scale=wdw[:, CV_PE[x // CONV], x % CONV:x % CONV + 1]).then_inc(cv_diag, 1)
        conv_sum(len(CV_PE) - 1)
        for b in range(NB):
            for q in range(2):
                tt = T_cback + 2 * b + q
                copy_turn(tt, ctm[:, b, q * W:(q + 1) * W], tp[:, tt % 2, :])
        layer_norms()
        for b in range(NB):
            for q in range(2):
                tt = T_cn + 2 * b + q
                act.wait_ge(s_T, tt + 1)
                for k in range(4 * q, 4 * q + 4):
                    kk = slice((k % 4) * P, (k % 4 + 1) * P)
                    ins = f(stage[:, tt % 2, kk], tp[:, tt % 2, kk], ACT.Silu,
                            scale=rowcols[:, 1, k:k + 1], bias=rowcols[:, 2, k:k + 1])
                link(ins)
                f(xTh[:, 4 * q:4 * q + 4, b * P:(b + 1) * P], stage[:, tt % 2, :].rearrange("p (k n) -> p k n", k=4),
                  ACT.Copy).then_inc(s_Th, 1)
        split(2)

        for i, d in enumerate(after):
            if i == 1:
                rms(False)
                to_channels(d["T_q"], 2)
                split(1)
                for c in range(4):
                    split()
                    if 1 <= c <= 2:
                        for b in range(NB):
                            step_copy(d["t_kv"][NB * (c - 1) + b], kT, c - 1, b)
                    split()
                act.wait_ge(f_L, 1)
                f(few[:, :], up[0:NH2, 0, 0:SEQ], ACT.Copy).then_inc(s_few, 1)
                to_channels(d["T_q2"], 1)
                act.wait_ge(f_D, 1)
                link(f(fx[:, 1], fx[:, 0], ACT.Abs))
                link(f(fx[:, 1], fx[:, 1], ACT.Exp, scale=-1.0))
                f(fx[:, 2], fx[:, 1], ACT.Ln, bias=1.0).then_inc(f_A, 1)
                for c in range(2):
                    split()
                    if c == 1:
                        for b in range(NB):
                            step_copy(d["t_q"][b], qT, 0, b)
                    split()
                for b in range(NB):
                    step_copy(d["t_q"][NB + b], qT, 1, b)
                act.wait_ge(f_CT, 1)
                f(ncT[:, :], tp[0:NH2, 0, 0:SEQ], ACT.Copy, scale=-1.0).then_inc(f_ct, 1)
                for n in range(NA + 2):
                    if n < NA:
                        exps(n, n % NB, NA)
                    if 1 <= n <= NA:
                        m = n - 1
                        w = 2 * P * (m % NB + 1)
                        act.wait_ge(at_T, NA + m + 1)
                        f(half[:, m % 2, 0:w], tp[:, m % 2, 0:w], ACT.Copy).then_inc(at_Te, 1)
                to_channels(d["T_o"])
                split(2)
                rms(True, A_O1)
            else:
                rms(False)
            to_channels(d["T_f"], 3 + i)
            split(2)
            mlp(d["g_ff"], d["t_ff"], ACT.Relu, W, 2)
            rms(True, A_F1 if i else A_F0)
            turn_hi(d["T_p"], hTh[:, 0, :], tp[:, d["T_p"] % 2, :])
            act.wait_ge(s_pe, 16 if i == 0 else 48)
            to_channels(d["T_g"], 5)
            split(2)
            split()
            for c in range(2):
                split()
                for b in range(NB):
                    step_act(d["g_p"] + NB * c + b, half[:, b, :], up[:, b, :], ACT.Sigmoid)
                if c == 0:
                    split()
        rms(False)

    @block.vector
    def _(dve):
        V = nc.vector
        chain = 0

        def link(ins):
            nonlocal chain
            chain += 1
            ins.then_inc(d_ch, 1)
            dve.wait_ge(d_ch, chain)

        acts = [0]

        def wait_act():
            acts[0] += 1
            dve.wait_ge(s_act, acts[0])

        def stage_free(g, last_turn):
            if last_turn is not None:
                dve.wait_ge(s_T, last_turn + 1)

        nst = [0, 0]

        def stats(b, src):
            for q in range(2):
                ins = V.bn_stats(bnd[:, q, :], src[:, q * W:(q + 1) * W])
            link(ins)
            link(V.bn_aggr(mv[:, b, :], bnd[:, :, :]))
            return mv[:, b, 1:2]

        def root(b, var, scale, eps):
            V.tensor_scalar(sc[:, b, 0:1], var, scale, eps, ALU.mult, ALU.add).then_inc(s_nD, 1)
            nst[0] += 1
            nst[1] += 1
            dve.wait_ge(s_nA, nst[1])
            link(V.reciprocal(sc[:, b, 3:4], sc[:, b, 1:2]))
            return sc[:, b, 3:4]

        def tell():
            dve.sem_inc(s_nD, 1)
            nst[0] += 1
            nst[1] += 1

        nrows = [0]

        def layer_norm(src, a0=None, squares=False):
            nrows[0] += 32
            for b in range(NB):
                if a0 is not None:
                    dve.wait_ge(s_acc, a0 + b + 1)
                r = root(b, stats(b, src[:, b, :]), 1.0, LN_EPS)
                if b == 0:
                    dve.wait_ge(s_rows, nrows[0])
                link(V.scalar_tensor_tensor(h[:, b, :], src[:, b, :], mv[:, b, 0:1], rows[:, 0:D], ALU.subtract, ALU.mult))
                ins = V.scalar_tensor_tensor(h[:, b, :], h[:, b, :], r, rows[:, D:2 * D], ALU.mult, ALU.add)
                chain_ins(ins)
                dve.sem_inc(s_norm, 1)
                if squares:
                    tell()
            dve.sem_inc(s_rows_free, 1)

        chain_ins = link
        nsplit, last_split = 0, before_moe

        def split(n=1):
            nonlocal nsplit
            for _ in range(n):
                q = nsplit
                if q == last_split:
                    return
                dve.wait_ge(s_hi, q + 1)
                V.tensor_tensor(wl[:, q % SPLITS, :], raw_half(q), wh[:, q % SPLITS, :].bitcast(F32),
                                ALU.subtract).then_inc(s_lo, 1)
                nsplit += 1

        turned = 0

        def wait_turn():
            nonlocal turned
            turned += 1
            dve.wait_ge(s_Th, turned)

        def turn_lo(out, hi, in_):
            wait_turn()
            V.tensor_tensor(out, in_, hi.bitcast(F32), ALU.subtract).then_inc(s_Te, 1)

        def to_channels(t0, gain=None, src=None):
            for b in range(NB):
                for q in range(2):
                    tt = t0 + 2 * b + q
                    at = slice(4 * q, 4 * q + 4), slice(b * P, (b + 1) * P)
                    lo, hi = xTl[:, at[0], at[1]], xTh[:, at[0], at[1]]
                    x = (tp if src is None else src)[:, tt % 2, :].rearrange("p (k n) -> p k n", k=4)
                    if gain is None:
                        turn_lo(lo, hi, x)
                    else:
                        wait_turn()
                        for k in range(4):
                            ins = V.scalar_tensor_tensor(lo[:, k, :], x[:, k, :], cols[:, gain, 4 * q + k:4 * q + k + 1],
                                                         hi[:, k, :].bitcast(F32), ALU.mult, ALU.subtract)
                        ins.then_inc(s_Te, 1)

        for m in moe:
            dve.sem_inc(m["lo"], RAW)
        last_turn = [None, None]
        to_channels(T_x)
        split(SPLITS)
        for i, c in enumerate(HG_CHUNKS):
            split()
            for b in range(NB):
                s = NB * i + b
                g = g_hg + s
                hf = half[:, g % 2, :]
                st = stage[:, g % 2, :]
                wait_act()
                stage_free(g, last_turn[g % 2])
                if c in (2, 3):
                    cc = slice((c - 2) * W, (c - 1) * W)
                    link(V.tensor_tensor(hf, hf, omlb[:, cc], ALU.mult))
                    link(V.tensor_tensor(hf, hf, lb[:, cc], ALU.add))
                    link(V.tensor_scalar(st, hf, -1.0, 1.0, ALU.mult, ALU.add))
                    link(V.tensor_scalar(hf, hf, 2.0 ** -63, None, ALU.max))
                    dve.sem_inc(s_lbD, 1)
                    dve.sem_inc(s_st, 1)
                elif c < 2:
                    V.tensor_copy(st, hf).then_inc(s_st, 1)
                elif c < 6:
                    V.tensor_copy(v[:, b, (c - 4) * W:(c - 3) * W], hf).then_inc(s_st, 1)
                else:
                    V.tensor_tensor(o[:, b, (c - 6) * W:(c - 5) * W].rearrange("p (j n) -> p j n", n=P),
                                    hf.rearrange("p (j n) -> p j n", n=P),
                                    gn[:, :].unsqueeze(1).broadcast_to([P, 4, P]), ALU.mult).then_inc(s_st, 1)
                last_turn[g % 2] = t_hg[s] if t_hg[s] is not None else last_turn[g % 2]
            split()
            e3 = hg_raw
            if i == 0:
                dve.wait_ge(s_lb, 16)
                link(V.tensor_tensor(lb, e3[:, 0, :], e3[:, 1, :], ALU.max))
                link(V.tensor_tensor(lb, lb, e3[:, 2, :], ALU.max))
            elif i == 1:
                for r in range(3):
                    ins = V.tensor_tensor(e3[:, r, :], e3[:, r, :], lb, ALU.subtract)
                ins.then_inc(s_lbD, 1)
            elif i == 2:
                dve.wait_ge(s_lbA, 1)
                link(V.tensor_tensor(lb, e3[:, 0, :], e3[:, 1, :], ALU.add))
                link(V.tensor_tensor(lb, lb, e3[:, 2, :], ALU.add))
                link(V.reciprocal(omlb[:, 0:W], lb[:, 0:W]))
            elif i == 3:
                link(V.reciprocal(omlb[:, W:D], lb[:, W:D]))
                link(V.tensor_tensor(lb, e3[:, 0, :], omlb, ALU.mult))
                link(V.tensor_scalar(omlb, lb, -1.0, 1.0, ALU.mult, ALU.add))
                dve.sem_inc(s_lbD, 1)
                dve.wait_ge(s_gn, 16)
        for x in range(2 * NB):
            at = slice((x // NB) * W, (x // NB + 1) * W)
            dve.wait_ge(hg_fh, x + 1)
            V.tensor_tensor(lfl[:, x % NB, at], lf[:, x % NB, at], lfh[:, x % NB, at].bitcast(F32),
                            ALU.subtract).then_inc(hg_fl, 1)
        for n in range(NH * NB + 3):
            if n < NH * NB:
                j, b = n // NB, n % NB
                dve.wait_ge(hg_e, n + 1)
                if n == 0:
                    dve.wait_ge(s_Te, T_hgo)
                if n >= 2:
                    dve.wait_ge(hg_s, n - 1)
                ev = level_banks(n).rearrange("p a w -> p (a w)").rearrange("p (s n) -> p s n", s=8)
                at = slice(b * P, (b + 1) * P)
                over = lambda x, levels: x[:, j, at].unsqueeze(1).broadcast_to([P, levels, P])
                V.tensor_tensor(hgA[:, n % 2], ev, over(qT, 8), ALU.mult)
                if b == 0:
                    V.tensor_tensor(hg_far[:, j % 2, :], ev[:, 0, :], kT[:, j, at], ALU.mult)
                    ins = V.tensor_tensor(hgB[:, n % 2, 1:8], ev[:, 1:8], over(kT, 7), ALU.mult)
                else:
                    ins = V.tensor_tensor(hgB[:, n % 2], ev, over(kT, 8), ALU.mult)
                ins.then_inc(hg_ab, 1)
            if 1 <= n <= NH * NB:
                m = n - 1
                dve.wait_ge(hg_s, m + 1)
                if m % NB == 1:
                    V.tensor_copy(hgX, hg_cross).then_inc(hg_x, 1)
                if m >= 1:
                    dve.wait_ge(hg_o, m)
                ins = V.tensor_tensor(hgS, accb[:, 1, :].rearrange("p (s n) -> p s n", s=8),
                                      big[:, H_MASK:H_MASK + 8 * P].rearrange("p (s n) -> p s n", s=8), ALU.mult)
                ins.then_inc(hg_sm, 1)
            if 3 <= n:
                m = n - 3
                j, b = m // NB, m % NB
                dve.wait_ge(hg_sq, m + 1)
                oj = o[:, b, j * P:(j + 1) * P]
                V.tensor_tensor(oj, up[:, m % 2, 0:P], oj, ALU.mult).then_inc(hg_og, 1)

        def head_norms(k):
            link(V.tensor_scalar(rs[:, :, :], ss[:, :, :], 1.0 / P, LN_EPS, ALU.mult, ALU.add))
            dve.sem_inc(s_hn, 1)
            dve.wait_ge(s_hn, k + 2)
            link(V.reciprocal(rs[:, :, :], rs[:, :, :]))
            for b in range(NB):
                ob = o[:, b, :].rearrange("p (j n) -> p j n", n=P)
                V.tensor_tensor(ob, ob, rs[:, b, :].unsqueeze(2).broadcast_to([P, NH, P]), ALU.mult).then_inc(s_norm, 1)

        dve.wait_ge(hg_og, NH * NB)
        head_norms(0)
        dve.sem_inc(s_hn, 1)
        to_channels(T_hgo)
        split(2)
        layer_norm(accb, A_HG)

        def mlp(g0, ts, width, off, down_halves):
            for u in range(len(ts) // NB):
                split()
                for b in range(NB):
                    s = NB * u + b
                    wait_act()
                    if u >= 1:
                        dve.wait_ge(s_T, ts[s - NB] + 1)
                    V.tensor_tensor(stage[:, b, 0:width], half[:, b, 0:width], up[:, b, off:off + width],
                                    ALU.mult).then_inc(s_st, 1)
                split()
                if u >= 1:
                    split(down_halves)
                for b in range(NB):
                    turn_lo(hTl[:, b, 0:width], hTh[:, b, 0:width], tp[:, ts[NB * u + b] % 2, 0:width])

        to_channels(T_ff)
        split(2)
        dve.wait_ge(s_small, SMALL)
        lr = lam[:, 0:256].rearrange("p (a n) -> p a n", a=4)
        link(V.tensor_tensor(lr[:, 0, :], lr[:, 0, :], lr[:, 1, :], ALU.mult))
        link(V.tensor_tensor(lr[:, 2, :], lr[:, 2, :], lr[:, 3, :], ALU.mult))
        link(V.tensor_reduce(lam[:, 256:257], lr[:, 0, :], AX.X, ALU.add))
        link(V.tensor_reduce(lam[:, 257:258], lr[:, 2, :], AX.X, ALU.add))
        dve.sem_inc(s_lbD, 1)
        dve.wait_ge(s_lbA, 1 + 2 * NB + 1)
        link(V.tensor_tensor(lam[:, 258:259], lam[:, 257:258], lam[:, 256:257], ALU.subtract))
        link(V.tensor_scalar(lam[:, 259:260], lam[:, 258:259], -LAM_INIT, None, ALU.add))
        nlam = lam[:, 259:260]
        dve.wait_ge(s_gn, 32)
        link(V.tensor_scalar(gn[:, :], gn[:, :], 1.0 - LAM_INIT, None, ALU.mult))
        dve.wait_ge(s_wh, 2)
        for w, w_hi, w_lo in ((wr, wrh, wrl), (wf, wfh, wfl)):
            V.tensor_tensor(w_lo[:, :, :], w[:, :, :], w_hi[:, :, :].bitcast(F32), ALU.subtract).then_inc(s_wl, 1)
        mlp(g_ff, t_ff, HALF, HALF, 1)
        layer_norm(accb, A_FF)

        tmp = flat(half[:, :, :]).rearrange("p (i u n) -> p i u n", i=4, u=8)
        to_channels(T_da)
        split(1)
        for s in range(12):
            g, c, b = g_da + s, s // NB, s % NB
            if b == 0:
                split()
            dve.wait_ge(s_up, g + 1)
            src = up[:, g % 2, :]
            if c < 4:
                if s >= 2:
                    dve.wait_ge(s_T, t_da[s - 2] + 1)
                x = src.rearrange("p (u m n) -> p u m n", m=2, n=32)
                dst = stage[:, g % 2, :].rearrange("p (u m n) -> p u m n", m=2, n=32)
                cos, sin = (cst[:, k + 32 * b:k + 32 * b + 32].unsqueeze(1).broadcast_to([P, 8, 32]) for k in (C_COS, C_SIN))
                V.tensor_tensor(tmp[:, 0], x[:, :, 0, :], cos, ALU.mult)
                V.tensor_tensor(tmp[:, 1], x[:, :, 1, :], sin, ALU.mult)
                V.tensor_tensor(tmp[:, 2], x[:, :, 1, :], cos, ALU.mult)
                link(V.tensor_tensor(tmp[:, 3], x[:, :, 0, :], sin, ALU.mult))
                V.tensor_tensor(dst[:, :, 0, :], tmp[:, 0], tmp[:, 1], ALU.subtract)
                link(V.tensor_tensor(dst[:, :, 1, :], tmp[:, 2], tmp[:, 3], ALU.add))
                dve.sem_inc(s_st, 1)
            else:
                V.tensor_copy(v[:, b, (c - 4) * W:(c - 3) * W], src).then_inc(s_st, 1)
            if b == NB - 1:
                split()

        NA = NH * NB

        def mark(ins):
            nonlocal chain
            chain += 1
            ins.then_inc(d_ch, 1)
            return chain

        def behind(count):
            dve.wait_ge(d_ch, count)

        def maxima(n, w, masked):
            behind(masked)
            V.tensor_reduce(att[:, n % 2, 0:2], at_s[:, n % 2, :, 0:w], AX.X, ALU.max, negate=True).then_inc(at_sm, 1)

        for n in range(NA + 3):
            if n < NA:
                b = n % NB
                w = P * (b + 1)
                dve.wait_ge(at_S, n + 1)
                if n >= 2:
                    dve.wait_ge(at_e, n - 1)
                masked = mark(V.scalar_tensor_tensor(at_s[:, n % 2, :, 0:w],
                                                     score_banks(n)[:, :, 0:w], 0.125,
                                                     causal[:, SEQ - w:SEQ].unsqueeze(1).broadcast_to([P, 2, w]),
                                                     ALU.mult, ALU.add))
            if 1 <= n <= NA:
                m = n - 1
                a = att[:, m % 2, :]
                dve.wait_ge(at_e, m + 1)
                inverse = mark(V.reciprocal(a[:, 4:6], a[:, 2:4]))
            if n < NA:
                maxima(n, P * (n % NB + 1), masked)
            if 1 <= n <= NA:
                w = P * (m % NB + 1)
                if m >= 2:
                    dve.wait_ge(at_T, m - 1)
                behind(inverse)
                mark(V.tensor_scalar(a[:, 5:6], a[:, 5:6], nlam, None, ALU.mult))
                st = stage[:, m % 2, 0:w]
                behind(mark(V.tensor_scalar(st, at_p[:, m % 2, 0, 0:w], a[:, 4:5], None, ALU.mult)))
                V.scalar_tensor_tensor(st, at_p[:, m % 2, 1, 0:w], a[:, 5:6], st, ALU.mult, ALU.add).then_inc(at_w, 1)
            if 3 <= n:
                m = n - 3
                j, b = m // NB, m % NB
                dve.wait_ge(at_sq, m + 1)
                V.tensor_tensor(o[:, b, j * P:(j + 1) * P], acc[:, m % 2, 0:P], gn[:, :], ALU.mult).then_inc(at_og, 1)
        dve.wait_ge(at_og, NA)
        head_norms(3)
        to_channels(T_dao)
        split(2)
        layer_norm(accb, A_DA)
        to_channels(T_moe)

        dve.wait_ge(s_rl, 2)
        L, one1, one2, w1, w2, tot, G = (rt[:, i] for i in range(7))
        d21 = rt[:, 7, :, 0:1]
        m1, m2, r1, r2 = (rt[:, 8 + i, :, 0:1] for i in range(4))
        key = cst[:, C_KEY:C_KEY + NE].unsqueeze(1).broadcast_to([P, NB, NE])
        wide = lambda a: a.broadcast_to([P, NB, NE])
        link(V.tensor_copy(L, up[:, 0, 0:NB * NE].rearrange("p (b n) -> p b n", b=NB)))
        for mx, r, oh, wk, src in ((m1, r1, one1, w1, L), (m2, r2, one2, w2, w1)):
            link(V.tensor_reduce(mx, src, AX.X, ALU.max))
            link(V.tensor_tensor(oh, src, wide(mx), ALU.is_equal))
            link(V.tensor_tensor(oh, oh, key, ALU.mult))
            link(V.tensor_reduce(r, oh, AX.X, ALU.max))
            link(V.tensor_tensor(oh, oh, wide(r), ALU.is_equal))
            if oh is one1:
                link(V.tensor_scalar(wk, oh, NEG, None, ALU.mult))
                link(V.tensor_tensor(wk, wk, src, ALU.add))
        link(V.tensor_tensor(d21, m1, m2, ALU.subtract))
        link(V.tensor_tensor(tot, one1, one2, ALU.add))
        dve.sem_inc(s_ra, 1)
        dve.wait_ge(s_rp, 1)
        link(V.tensor_tensor(G, one1, wide(d21), ALU.mult))
        link(V.tensor_scalar(d21, d21, -1.0, 1.0, ALU.mult, ALU.add))
        link(V.tensor_tensor(w1, one2, wide(d21), ALU.mult))
        link(V.tensor_tensor(gate[:, :, 0:NE], G, w1, ALU.add))
        dve.wait_ge(s_rl, 3)
        link(V.tensor_tensor(w2, tot, up[:, 1, 0:NB * NE].rearrange("p (b n) -> p b n", b=NB), ALU.mult))
        link(V.tensor_scalar(slot[:, :, 0:NE], w2, -1.0, None, ALU.add))
        over, rank = ex[:, 0, :], ex[:, 1, :]
        link(V.tensor_scalar(over, up[:, 1, NB * NE:(NB + 1) * NE], float(P), None, ALU.is_gt))
        dve.sem_inc(s_over, 1)
        dve.wait_ge(s_y, 1)

        def split_half(m, i, x):
            dve.wait_ge(m["hi"], i * NHALF + (x + 1))
            V.tensor_tensor(wl[:, x % SPLITS, :], raw[:, x % RAW, :], wh[:, x % SPLITS, :].bitcast(F32),
                            ALU.subtract).then_inc(m["lo"], 1)

        def start(m, i, first):
            dve.wait_ge(m["gath"], i * 2 + 1)
            dve.wait_ge(m["turned"], i + 1)
            column = bass.ds(i + first, 1)
            for b in range(NB):
                V.tensor_scalar(pick[:, b, :], iota, slot[:, b, column], None, ALU.is_equal)
            for b in range(NB):
                ins = V.tensor_scalar(give[:, b, :], iota, slot[:, b, column], gate[:, b, column], ALU.is_equal, ALU.mult)
            ins.then_inc(m["picked"], 1)
            for x in range(2):
                split_half(m, i, x)

        def expert(m, i, first, ahead):
            for q in range(2):
                dve.wait_ge(m["xgh"], i * 2 + (q + 1))
                V.tensor_tensor(xgl[:, 4 * q:4 * q + 4, :], tp[:, q, :].rearrange("p (k n) -> p k n", k=4),
                                xgh[:, 4 * q:4 * q + 4, :].bitcast(F32), ALU.subtract).then_inc(m["xg"], 1)
            split_half(m, i, 2)
            for s in range(EU + 1):
                if s > 0:
                    dve.wait_ge(m["Th"], i * EU + s)
                    V.tensor_tensor(hTl[:, (s - 1) % 2, 0:HALF], tp[:, (s - 1) % 2, 0:HALF],
                                    hTh[:, (s - 1) % 2, 0:HALF].bitcast(F32), ALU.subtract).then_inc(m["Te"], 1)
                if 1 <= s < EU - 1:
                    split_half(m, i, gate_half(s + 1, 0))
                if s == EU:
                    break
                dve.wait_ge(m["act"], i * EU + (s + 1))
                if s >= 2:
                    dve.wait_ge(m["T"], i * EU + (s - 1))
                V.tensor_tensor(stage[:, s % 2, 0:HALF], half[:, s % 2, 0:HALF], up[:, s % 2, HALF:W],
                                ALU.mult).then_inc(m["st"], 1)
                if s < EU - 1:
                    split_half(m, i, gate_half(s + 1, 1))
                split_half(m, i, down_half(s))
            if ahead:
                start(m, i + 1, first)
            for n in range(4):
                dve.wait_ge(m["give"], i * 4 + (n + 1))
                dve.wait_ge(m["added"], i * 4 + 1)
                yb = y[:, n // 2, (n % 2) * W:(n % 2 + 1) * W]
                V.tensor_tensor(yb, yb, give_banks[n], ALU.add).then_inc(m["added"], 1)

        for m in moe:
            dve.sem_inc(m["added"], 1)
            dve.sem_inc(m["Te"], 1)
        start(moe[0], 0, 0)
        with dve.Fori(0, NE - 1) as i:
            expert(moe[0], i, 0, True)
        expert(moe[0], NE - 1, 0, False)
        dve.wait_ge(moe[0]["added"], 4 * NE + 1)
        dve.wait_ge(s_rd, 1)
        n_extra = dve.value_load(extra_i[0:1, 0:1], min_val=0, max_val=MAX_EXTRA)
        with dve.If(n_extra > 0):
            with dve.Fori(0, n_extra) as j:
                start(moe[1], j, NE)
                expert(moe[1], j, NE, False)
            dve.wait_ge(moe[1]["added"], n_extra * 4 + 1)
            dve.sem_inc(s_xdone, 1)
        last_split = len(pl.halves)
        layer_norm(y, squares=True)
        def rms(dst, told):
            for b in range(NB):
                if not told:
                    nst[1] += 1
                    dve.wait_ge(s_nA, nst[1])
                elif b == 0:
                    dve.wait_ge(s_nA, nst[1] - 1)
                r = root(b, sc[:, b, 2:3], 1.0 / D, RMS_EPS)
                V.tensor_scalar(dst[:, b, :], h[:, b, :], r, None, ALU.mult).then_inc(s_norm, 1)

        hn = o

        link(V.memset(uT[:, :, 0:PADC], 0.0))

        def tap(j, tiles):
            for k in tiles:
                src = uT[:, k, j:j + SEQ]
                if j == 0:
                    ins = V.tensor_scalar(cT[:, k, :], src, wdw[:, k, 0:1], rowcols[:, 0, k:k + 1], ALU.mult, ALU.add)
                else:
                    ins = V.scalar_tensor_tensor(cT[:, k, :], src, wdw[:, k, j:j + 1], cT[:, k, :], ALU.mult, ALU.add)
            link(ins)

        rms(hn, True)
        split(1)
        to_channels(T_cv, 0)
        split(2)
        nrows[0] += 32
        dve.wait_ge(s_rows, nrows[0])
        r2 = rows[:, :].rearrange("p (m n) -> p m n", m=2)
        for s in range(8):
            g, c, b = g_cv + s, s // NB, s % NB
            if b == 0:
                split()
            dve.wait_ge(s_up, g + 1)
            hf = half[:, g % 2, :]
            link(V.tensor_tensor(hf.rearrange("p (m n) -> p m n", m=2), up[:, g % 2, :].rearrange("p (m n) -> p m n", m=2),
                                 r2[:, :, c * HALF:(c + 1) * HALF], ALU.add))
            dve.sem_inc(cv_n, 1)
            wait_act()
            if s >= 2:
                dve.wait_ge(s_T, t_cv[s - 2] + 1)
            V.tensor_tensor(stage[:, g % 2, 0:HALF], hf[:, 0:HALF], hf[:, HALF:W], ALU.mult).then_inc(s_st, 1)
            if b == NB - 1:
                split()
                if c >= 2:
                    dve.wait_ge(s_Te, t_cv[1] + 1)
                    for j in range(EARLY * (c - 2), EARLY * (c - 1)):
                        tap(j, CV_DVE[0:2])
        dve.sem_inc(s_rows_free, 1)
        dve.wait_ge(s_Te, T_cback)
        for j in range(CONV):
            tap(j, CV_DVE[2:] if j < 2 * EARLY else CV_DVE)
        dve.sem_inc(cv_dw, 1)
        for b in range(NB):
            dve.wait_ge(s_Te, T_cback + 2 * b + 2)
            r = root(b, stats(b, ctm[:, b, :]), 1.0, RMS_EPS)
            V.tensor_scalar(ctm[:, b, :], ctm[:, b, :], mv[:, b, 0:1], r, ALU.subtract, ALU.mult).then_inc(s_norm, 1)
        to_channels(T_cn, None, stage)
        split(2)
        nrows[0] += 32
        dve.wait_ge(s_rows, nrows[0])
        for b in range(NB):
            dve.wait_ge(s_acc, A_PW2 + b + 1)
            link(V.tensor_tensor(h[:, b, :], accb[:, b, :], rows[:, 0:D], ALU.add))
            tell()

        for i, d in enumerate(after):
            if i == 1:
                rms(hn, True)
                to_channels(d["T_q"], 2)
                split(1)
                for s in range(8):
                    g, c, b = d["g_kv"] + s, s // NB, s % NB
                    if b == 0:
                        split()
                    dve.wait_ge(s_up, g + 1)
                    if c < 2:
                        if s >= 2:
                            dve.wait_ge(s_T, d["t_kv"][s - 2] + 1)
                        dst = stage[:, g % 2, :]
                    else:
                        dst = v[:, b, (c - 2) * W:(c - 1) * W]
                    V.tensor_copy(dst, up[:, g % 2, :]).then_inc(s_st, 1)
                    if b == NB - 1:
                        split()
                for b in range(NB):
                    g = d["g_f"] + b
                    dve.wait_ge(s_up, g + 1)
                    V.tensor_tensor(fx[:, 0, b, :], up[:, g % 2, 0:NH2], bf[:, :], ALU.add).then_inc(s_st, 1)
                dve.wait_ge(s_st, d["g_f"] + NB)
                dve.sem_inc(f_D, 1)
                link(V.tensor_scalar(fx[:, 3], fx[:, 0], 0.0, None, ALU.min))
                to_channels(d["T_q2"], 1)
                dve.wait_ge(f_A, 1)
                link(V.tensor_tensor(fx[:, 4], fx[:, 3], fx[:, 2], ALU.subtract))
                dve.sem_inc(f_D, 1)
                for s in range(4):
                    g = d["g_q"] + s
                    if s % NB == 0:
                        split()
                    dve.wait_ge(s_up, g + 1)
                    if s >= 2:
                        dve.wait_ge(s_T, d["t_q"][s - 2] + 1)
                    V.tensor_scalar(stage[:, g % 2, :], up[:, g % 2, :], HD2 ** -0.5, None, ALU.mult).then_inc(s_st, 1)
                    if s % NB == NB - 1:
                        split()
                dve.wait_ge(f_C, 1)
                cb = fx[:, 5]
                link(V.tensor_copy(cb, up[:, 0, 0:NB * NH2].rearrange("p (b n) -> p b n", b=NB)))
                dve.sem_inc(f_D, 1)
                for n in range(NA + 3):
                    if n < NA:
                        j, b = n // NB, n % NB
                        w = P * (b + 1)
                        dve.wait_ge(at_S, NA + n + 1)
                        if n >= 2:
                            dve.wait_ge(at_e, NA + n - 1)
                        for c in range(2):
                            ins = V.scalar_tensor_tensor(at_s[:, n % 2, c, 0:w], score_banks(n)[:, c, 0:w],
                                                         cb[:, b, 2 * j + c:2 * j + c + 1], causal[:, SEQ - w:SEQ],
                                                         ALU.add, ALU.add)
                        masked = mark(ins)
                    if 1 <= n <= NA:
                        m = n - 1
                        dve.wait_ge(at_e, NA + m + 1)
                        V.reciprocal(fx[:, 6, 0, 2 * (m % 4):2 * (m % 4) + 2], att[:, m % 2, 2:4]).then_inc(at_w, 1)
                    if n < NA:
                        maxima(n, w, masked)
                    if 3 <= n:
                        m = n - 3
                        j, b = m // NB, m % NB
                        dve.wait_ge(at_O, NA + m + 1)
                        a = fx[:, 6, 0, 2 * (m % 4):2 * (m % 4) + 2]
                        V.tensor_tensor(o[:, b, j * P:(j + 1) * P].rearrange("p (c n) -> p c n", c=2),
                                        acc[:, m % 2, 0:P].rearrange("p (c n) -> p c n", c=2),
                                        a.unsqueeze(2).broadcast_to([P, 2, HD2]), ALU.mult).then_inc(at_og, 1)
                dve.wait_ge(at_og, 2 * NA)
                dve.sem_inc(s_norm, NB)
                to_channels(d["T_o"])
                split(2)
                rms(hn, False)
            else:
                rms(hn, True)
            to_channels(d["T_f"], 3 + i)
            split(2)
            mlp(d["g_ff"], d["t_ff"], W, 0, 2)
            rms(hn, False)
            turn_lo(hTl[:, 0, :], hTh[:, 0, :], tp[:, d["T_p"] % 2, :])
            to_channels(d["T_g"], 5)
            split(2)
            split()
            for s in range(4):
                g, c, b = d["g_p"] + s, s // NB, s % NB
                if b == 0:
                    split()
                wait_act()
                link(V.tensor_tensor(stage[:, g % 2, :], half[:, g % 2, :], acc[:, s, :], ALU.mult))
                hb = h[:, b, c * W:(c + 1) * W]
                link(V.tensor_tensor(hb, hb, stage[:, g % 2, :], ALU.add))
                dve.sem_inc(s_st, 1)
                if s == 1:
                    split()
                if s >= NB:
                    tell()
            dve.sem_inc(s_norm, NB)
        dve.wait_ge(s_nA, nst[1] - 1)
        for b in range(NB):
            r = root(b, sc[:, b, 2:3], 1.0 / D, RMS_EPS)
            V.scalar_tensor_tensor(o[:, b, :], h[:, b, :], r, rows[:, D:2 * D], ALU.mult, ALU.mult).then_inc(s_norm, 1)

    @block.tensor
    def _(pe):
        mm = nc.tensor.matmul

        def turn_bank(tt):
            if tt >= 2:
                pe.wait_ge(s_Te, tt - 1)

        def turn_rows(t0, src, ready):
            for b in range(NB):
                ready(b)
                for q in range(2):
                    tt = t0 + 2 * b + q
                    turn_bank(tt)
                    for k in range(4):
                        ins = nc.tensor.transpose(tp[:, tt % 2, k * P:(k + 1) * P],
                                                  src[:, b, (4 * q + k) * P:(4 * q + k + 1) * P], ident)
                    ins.then_inc(s_T, 1)

        def normed(n):
            return lambda b: pe.wait_ge(s_norm, n + b + 1)

        def split_product(out, x_hi, x_lo, w_hi, w_lo, start, stop):
            mm(out, x_hi, w_hi, start=start, stop=False)
            mm(out, x_hi, w_lo, start=False, stop=False)
            return mm(out, x_lo, w_hi, start=False, stop=stop)

        def few_columns(n, w_hi, w_lo, done):
            for k in range(KT):
                for i, (w, x) in enumerate(((w_hi, xTh), (w_lo, xTh), (w_hi, xTl))):
                    ins = mm(up[0:n, 0, 0:SEQ], w[:, k, :], x[:, k, :], start=(k == 0 and i == 0),
                             stop=(k == KT - 1 and i == 2))
            ins.then_inc(done, 1)

        uses = 0

        def next_half(n):
            nonlocal uses
            q = uses
            uses += 1
            return q, [w[:, q % SPLITS, :].rearrange("p (k n) -> p k n", k=n) for w in (wh, wl)]

        def half_products(out, b, w, part, start=True):
            for k in range(4):
                x = 4 * part + k, slice(b * P, (b + 1) * P)
                ins = split_product(out, xTh[:, x[0], x[1]], xTl[:, x[0], x[1]], w[0][:, k, :], w[1][:, k, :],
                                    start and x[0] == 0, x[0] == KT - 1)
            return ins

        def turn_step(g, tt, nk):
            pe.wait_ge(s_st, g + 1)
            turn_bank(tt)
            for k in range(nk):
                ins = nc.tensor.transpose(tp[:, tt % 2, k * P:(k + 1) * P], stage[:, g % 2, k * P:(k + 1) * P], ident)
            ins.then_inc(s_T, 1)

        def xT_ready(b, t0):
            pe.wait_ge(s_Te, t0 + 2 * b + 2)

        def unit(g0, c, t0, behind=None):
            q, w = next_half(4)
            pe.wait_ge(s_lo, q + 1)
            for b in range(NB):
                g = g0 + NB * c + b
                if c == 0 and t0 is not None:
                    xT_ready(b, t0)
                if g >= 2:
                    pe.wait_ge(s_st, g - 1)
                ins = half_products(up[:, g % 2, :], b, w, 0)
            ins.then_inc(s_used, 1)
            if behind is not None:
                behind(c - 1)
            q, w = next_half(4)
            pe.wait_ge(s_lo, q + 1)
            for b in range(NB):
                half_products(up[:, (g0 + b) % 2, :], b, w, 1).then_inc(s_up, 1)

        def project(g0, ts, chunks, t0, nk):
            def behind(c):
                for b in range(NB):
                    s = NB * c + b
                    if s >= 0 and ts[s] is not None:
                        turn_step(g0 + s, ts[s], nk)

            for c in range(chunks):
                unit(g0, c, t0, behind)
            behind(chunks - 1)

        def residual(scale, blocks=range(NB)):
            for b in blocks:
                for n in range(2):
                    mm(acc[:, 2 * b + n, :], scale, h[:, b, n * W:(n + 1) * W], start=True, stop=False)

        def out_product(t0):
            for part in range(2):
                q, w = next_half(4)
                pe.wait_ge(s_lo, q + 1)
                for b in range(NB):
                    if part == 0:
                        xT_ready(b, t0)
                    ins = half_products(acc[:, 2 * b, :], b, w, part, False)
                ins.then_inc(s_used, 1)
            halves = [next_half(4) for _ in range(2)]
            for b in range(NB):
                for part, (q, w) in enumerate(halves):
                    pe.wait_ge(s_lo, q + 1)
                    ins = half_products(acc[:, 2 * b + 1, :], b, w, part, False)
                    if part == 1:
                        ins.then_inc(s_acc, 1)
                    elif b == NB - 1:
                        ins.then_inc(s_used, 1)

        def mlp(g0, ts, t0, tiles, down_halves, scale):
            units = len(ts) // NB

            def down(u, b, w, x, ready):
                if ready:
                    pe.wait_ge(s_Te, ts[NB * u + b] + 1)
                for k in range(2):
                    t_ = slice((2 * x + k) * P, (2 * x + k + 1) * P)
                    for n in range(2):
                        c_ = slice(n * W, (n + 1) * W)
                        ins = split_product(acc[:, 2 * b + n, :], hTh[:, b, t_], hTl[:, b, t_], w[0][:, k, c_], w[1][:, k, c_],
                                            False, u == units - 1 and x == down_halves - 1 and k == 1)
                return ins

            for u in range(units + 1):
                if u < units:
                    unit(g0, u, t0)
                if u == 0:
                    residual(scale)
                if 1 <= u < units:
                    for x in range(down_halves):
                        q, w = next_half(2)
                        pe.wait_ge(s_lo, q + 1)
                        for b in range(NB):
                            ins = down(u - 1, b, w, x, x == 0)
                        ins.then_inc(s_used, 1)
                if u < units:
                    for b in range(NB):
                        turn_step(g0 + NB * u + b, ts[NB * u + b], tiles)
            halves = [next_half(2) for _ in range(down_halves)]
            for b in range(NB):
                for x, (q, w) in enumerate(halves):
                    pe.wait_ge(s_lo, q + 1)
                    ins = down(units - 1, b, w, x, x == 0)
                    if x == down_halves - 1:
                        ins.then_inc(s_acc, 1)
                    elif b == NB - 1:
                        ins.then_inc(s_used, 1)

        pe.wait_ge(s_cst, 16)
        turn_rows(T_x, h, lambda b: pe.wait_ge(s_x, 16))
        project(g_hg, t_hg, 8, T_x, 4)
        pe.wait_ge(hg_lev, NB)
        for n in range(NH * NB + 2):
            if n < NH * NB:
                j, b = n // NB, n % NB
                pe.wait_ge(hg_fl, NB * (j // 4) + b + 1)
                if n == 1:
                    pe.wait_ge(s_Te, T_hgo)
                if n >= 2:
                    pe.wait_ge(hg_ab, n - 1)
                    if b == 1:
                        pe.wait_ge(hg_x, n // NB)
                for q in range(2):
                    for part in (lfh, lfl):
                        ins = mm(level_banks(n)[:, q, :], part[:, b, j * P:(j + 1) * P],
                                 lev[b][:, q, :], start=part is lfh, stop=part is lfl)
                ins.then_inc(hg_m, 1)
            if 1 <= n <= NH * NB:
                m = n - 1
                j, b = m // NB, m % NB
                first = 1 - b
                pe.wait_ge(hg_ab, m + 1)
                if m >= 1:
                    pe.wait_ge(hg_sm, m)
                A, B = hgA[:, m % 2], hgB[:, m % 2]
                if b == 1:
                    mm(hg_cross, hg_far[:, j % 2, :], A[:, 7, :], start=True, stop=True)
                for l in range(7):
                    mm(acc[:, 2 + l // 4, (l % 4) * P:(l % 4 + 1) * P], B[:, first + l, :], A[:, first + l, :],
                       start=True, stop=True)
                qk = slice(b * P, (b + 1) * P)
                mm(acc[:, 3, 3 * P:4 * P], kT[:, j, qk], qT[:, j, qk], start=True, stop=True).then_inc(hg_s, 1)
            if 2 <= n:
                m = n - 2
                j, b = m // NB, m % NB
                pe.wait_ge(hg_sm, m + 1)
                if m >= 2:
                    pe.wait_ge(hg_og, m - 1)
                if b == 1:
                    pe.wait_ge(hg_x, j + 1)
                    mm(up[:, m % 2, 0:P], hgX, v[:, 0, j * P:(j + 1) * P], start=True, stop=False)
                for l in range(8):
                    ins = mm(up[:, m % 2, 0:P], hgS[:, l, :], v[:, b, j * P:(j + 1) * P], start=(l == 0 and b == 0),
                             stop=(l == 7))
                ins.then_inc(hg_o, 1)
        residual(aident)
        turn_rows(T_hgo, o, normed(N_HGO))
        out_product(T_hgo)

        turn_rows(T_ff, h, normed(N_LN0))
        mlp(g_ff, t_ff, T_ff, 2, 1, aident)

        turn_rows(T_da, h, normed(N_LN1))
        project(g_da, t_da, 6, T_da, 4)
        NA = NH * NB

        def attention(base, scores, turns, outs):
            for n in range(-1, NA + 2):
                if n + 1 < NA:
                    if n >= 1:
                        pe.wait_ge(at_sm, base + n)
                    scores(n + 1, (n + 1) // NB, (n + 1) % NB).then_inc(at_S, 1)
                if 1 <= n <= NA:
                    m = n - 1
                    pe.wait_ge(at_w, base + m + 1)
                    if m >= 2:
                        pe.wait_ge(at_Te, base + m - 1)
                    turns(m, m % NB).then_inc(at_T, 1)
                if 2 <= n:
                    m = n - 2
                    pe.wait_ge(at_Te, base + m + 1)
                    if m >= 2:
                        pe.wait_ge(at_og, base + m - 1)
                    outs(m, m // NB, m % NB).then_inc(at_O, 1)

        def da_scores(n, j, b):
            for c in range(2):
                r = slice(64 * c, 64 * c + 64)
                ins = mm(score_banks(n)[:, c, 0:P * (b + 1)], qT[r, j, b * P:(b + 1) * P], kT[r, j, 0:P * (b + 1)],
                         start=True, stop=True)
            return ins

        def da_turns(m, b):
            for kb in range(b + 1):
                ins = nc.tensor.transpose(tp[:, m % 2, kb * P:(kb + 1) * P], stage[:, m % 2, kb * P:(kb + 1) * P], ident)
            return ins

        def da_outs(m, j, b):
            for kb in range(b + 1):
                ins = mm(acc[:, m % 2, 0:P], half[:, m % 2, kb * P:(kb + 1) * P], v[:, kb, j * P:(j + 1) * P],
                         start=(kb == 0), stop=(kb == b))
            return ins

        pe.wait_ge(s_Te, T_dao)
        pe.wait_ge(s_st, g_da + 12)
        attention(0, da_scores, da_turns, da_outs)
        residual(aident, [1])
        turn_rows(T_dao, o, normed(N_DAO))
        residual(aident, [0])
        out_product(T_dao)

        turn_rows(T_moe, h, normed(N_LN2))
        pe.wait_ge(s_wl, 2)
        xT_ready(NB - 1, T_moe)
        few_columns(NE, wrh, wrl, s_rl)
        pe.wait_ge(s_few, 1)
        for b in range(NB):
            ins = nc.tensor.transpose(up[:, 0, b * NE:(b + 1) * NE], few[0:NE, b * P:(b + 1) * P], ident[0:NE, 0:NE])
        ins.then_inc(s_rl, 1)
        pe.wait_ge(s_ra, 1)
        tot = rt[:, 5]
        mm(up[:, 1, 0:NE], tri, tot[:, 0, :], start=True, stop=True)
        mm(up[:, 1, NE:2 * NE], ones, tot[:, 0, :], start=True, stop=False)
        mm(up[:, 1, NE:2 * NE], tri, tot[:, 1, :], start=False, stop=True)
        mm(up[:, 1, 2 * NE:3 * NE], ones, tot[:, 0, :], start=True, stop=False)
        mm(up[:, 1, 2 * NE:3 * NE], ones, tot[:, 1, :], start=False, stop=True).then_inc(s_rl, 1)

        def gather(m, i):
            pe.wait_ge(m["picked"], i + 1)
            pe.wait_ge(m["Te"], i * EU + 1)
            for q in range(2):
                for k in range(4 * q, 4 * q + 4):
                    for b in range(NB):
                        ins = mm(tp[:, q, (k % 4) * P:(k % 4 + 1) * P], h[:, b, k * P:(k + 1) * P], pick[:, b, :],
                                 start=(b == 0), stop=(b == NB - 1))
                ins.then_inc(m["gath"], 1)

        def expert(m, i, ahead):
            pe.wait_ge(m["added"], i * 4 + 1)
            for b in range(NB):
                ins = nc.tensor.transpose(acc[:, 2, b * P:(b + 1) * P], give[:, b, :], ident)
            ins.then_inc(m["turned"], 1)
            def split_ready(x):
                pe.wait_ge(m["lo"], i * NHALF + (RAW + x + 1))

            def gate_up(s, part):
                x = gate_half(s, part)
                split_ready(x)
                w_hi, w_lo = (w[:, x % SPLITS, :].rearrange("p (k n) -> p k n", k=4) for w in (wh, wl))
                for k in range(4):
                    kk = 4 * part + k
                    ins = split_product(up[:, s % 2, :], xgh[:, kk, :], xgl[:, kk, :], w_hi[:, k, :], w_lo[:, k, :],
                                        kk == 0, kk == KT - 1)
                return ins

            for s in range(EU + 1):
                if s < EU:
                    if s >= 2:
                        pe.wait_ge(m["st"], i * EU + (s - 1))
                    if s == 0:
                        pe.wait_ge(m["xg"], i * 2 + 1)
                    gate_up(s, 0).then_inc(m["used"], 1)
                if s >= 1:
                    pe.wait_ge(m["st"], i * EU + s)
                    if s >= 3:
                        pe.wait_ge(m["Te"], i * EU + (s - 1))
                    for k in range(2):
                        ins = nc.tensor.transpose(tp[:, (s - 1) % 2, k * P:(k + 1) * P],
                                                  stage[:, (s - 1) % 2, k * P:(k + 1) * P], ident)
                    ins.then_inc(m["T"], 1)
                if s < EU:
                    if s == 0:
                        pe.wait_ge(m["xg"], i * 2 + 2)
                    gate_up(s, 1).then_inc(m["up"], 1)
                if s >= 1:
                    u = s - 1
                    x = down_half(u)
                    split_ready(x)
                    w_hi, w_lo = (w[:, x % SPLITS, :].rearrange("p (k n) -> p k n", k=2) for w in (wh, wl))
                    pe.wait_ge(m["Te"], i * EU + (s + 1))
                    if u == 0:
                        pe.wait_ge(m["ye"], i + 1)
                    for n in range(2):
                        for k in range(2):
                            t_, c_ = slice(k * P, (k + 1) * P), slice(n * W, (n + 1) * W)
                            ins = split_product(acc[:, n, :], hTh[:, u % 2, t_], hTl[:, u % 2, t_], w_hi[:, k, c_],
                                                w_lo[:, k, c_], u == 0 and k == 0, u == EU - 1 and k == 1)
                    ins.then_inc(m["down"] if u == EU - 1 else m["used"], 1)
            if ahead:
                gather(m, i + 1)
            pe.wait_ge(m["ye"], i + 2)
            pe.wait_ge(m["giveT"], i + 1)
            for n in range(4):
                mm(give_banks[n], giveT[:, n // 2, :], ye[:, (n % 2) * W:(n % 2 + 1) * W],
                   start=True, stop=True).then_inc(m["give"], 1)

        for m in moe:
            pe.sem_inc(m["gath"], 1)
            pe.sem_inc(m["turned"], 1)
        gather(moe[0], 0)
        with pe.Fori(0, NE - 1) as i:
            expert(moe[0], i, True)
        expert(moe[0], NE - 1, False)
        pe.wait_ge(s_rd, 1)
        n_extra = pe.value_load(extra_i[0:1, 0:1], min_val=0, max_val=MAX_EXTRA)
        with pe.If(n_extra > 0):
            with pe.Fori(0, n_extra) as j:
                gather(moe[1], j)
                expert(moe[1], j, False)

        turn_rows(T_cv, o, normed(N_RC))
        project(g_cv, t_cv, 4, T_cv, 2)
        pe.wait_ge(s_Te, T_cback)
        pe.wait_ge(s_st, g_cv + 8)
        for i, k in enumerate(CV_PE):
            if i >= 2:
                pe.wait_ge(cv_sum, i - 1)
            for j in range(CONV):
                x = CONV * i + j
                pe.wait_ge(cv_diag, x + 1)
                mm(up[:, k % 2, 0:SEQ], diag[:, x % DIAGS, :], uT[:, k, j:j + SEQ], start=(j == 0),
                   stop=(j == CONV - 1)).then_inc(cv_tap, 1)
        pe.wait_ge(cv_dw, 1)
        pe.wait_ge(cv_sum, len(CV_PE))
        for b in range(NB):
            for q in range(2):
                tt = T_cback + 2 * b + q
                turn_bank(tt)
                for k in range(4):
                    ins = nc.tensor.transpose(tp[:, tt % 2, k * P:(k + 1) * P], cT[:, 4 * q + k, b * P:(b + 1) * P], ident)
                ins.then_inc(s_T, 1)
        residual(ident)
        turn_rows(T_cn, ctm, normed(N_CB))
        out_product(T_cn)

        for i, d in enumerate(after):
            if i == 1:
                turn_rows(d["T_q"], o, normed(N_AFTER[i]["q"]))
                project(d["g_kv"], d["t_kv"], 4, d["T_q"], 4)
                pe.wait_ge(s_st, d["g_f"])
                few_columns(NH2, wfh, wfl, f_L)
                pe.wait_ge(s_few, 2)
                for b in range(NB):
                    nc.tensor.transpose(up[:, (d["g_f"] + b) % 2, 0:NH2], few[:, b * P:(b + 1) * P],
                                        ident[0:NH2, 0:NH2]).then_inc(s_up, 1)
                turn_rows(d["T_q2"], o, lambda b: None)
                project(d["g_q"], d["t_q"], 2, d["T_q2"], 4)
                pe.wait_ge(f_D, 2)
                pe.wait_ge(s_Te, d["T_o"])
                lg = fx[:, 4]
                mm(up[:, 0, 0:NH2], tri, lg[:, 0, :], start=True, stop=True)
                mm(up[:, 0, NH2:2 * NH2], ones, lg[:, 0, :], start=True, stop=False)
                mm(up[:, 0, NH2:2 * NH2], tri, lg[:, 1, :], start=False, stop=True).then_inc(f_C, 1)
                pe.wait_ge(f_D, 3)
                for b in range(NB):
                    ins = nc.tensor.transpose(tp[0:NH2, 0, b * P:(b + 1) * P], fx[:, 5, b, :], ident)
                ins.then_inc(f_CT, 1)
                pe.wait_ge(f_ct, 1)
                pe.wait_ge(s_headrow, 16)

                def fox_scores(n, j, b):
                    w = P * (b + 1)
                    for c in range(2):
                        r = slice(64 * c, 64 * c + 64)
                        out = score_banks(n)[:, c, 0:w]
                        mm(out, qT[r, j, b * P:(b + 1) * P], kT[r, j, 0:w], start=True, stop=False)
                        ins = mm(out, headrow[:, 2 * j + c, :], ncT[:, 0:w], start=False, stop=True)
                    return ins

                def fox_turns(m, b):
                    for c in range(2):
                        for kb in range(b + 1):
                            at = (c * (b + 1) + kb) * P
                            ins = nc.tensor.transpose(tp[:, m % 2, at:at + P], at_p[:, m % 2, c, kb * P:(kb + 1) * P], ident)
                    return ins

                def fox_outs(m, j, b):
                    for c in range(2):
                        for kb in range(b + 1):
                            at = (c * (b + 1) + kb) * P
                            ins = mm(acc[:, m % 2, c * HD2:(c + 1) * HD2], half[:, m % 2, at:at + P],
                                     v[:, kb, (2 * j + c) * HD2:(2 * j + c + 1) * HD2], start=(kb == 0), stop=(kb == b))
                    return ins

                attention(NA, fox_scores, fox_turns, fox_outs)
                residual(ident, [1])
                turn_rows(d["T_o"], o, normed(N_AFTER[i]["o"]))
                residual(ident, [0])
                out_product(d["T_o"])
            turn_rows(d["T_f"], o, normed(N_AFTER[i]["f"]))
            mlp(d["g_ff"], d["t_ff"], d["T_f"], 4, 2, ident)
            pe.wait_ge(s_pe, 16 if i == 0 else 48)
            turn_bank(d["T_p"])
            for k in range(2):
                for b in range(NB):
                    ins = nc.tensor.transpose(tp[:, d["T_p"] % 2, (2 * k + b) * P:(2 * k + b + 1) * P],
                                              pe_tm[:, b, k * P:(k + 1) * P], ident)
            ins.then_inc(s_T, 1)
            turn_rows(d["T_g"], o, normed(N_AFTER[i]["g"]))
            q, w = next_half(2)
            pe.wait_ge(s_lo, q + 1)
            pe.wait_ge(s_Te, d["T_p"] + 1)
            for s in range(4):
                c, b = s // NB, s % NB
                for k in range(2):
                    ins = split_product(acc[:, s, :], pe_Th[:, k, b * P:(b + 1) * P], pe_Tl[:, k, b * P:(b + 1) * P],
                                        w[0][:, k, c * W:(c + 1) * W], w[1][:, k, c * W:(c + 1) * W], k == 0, k == 1)
            ins.then_inc(s_used, 1)
            project(d["g_p"], [None] * 4, 2, d["T_g"], 4)


USED = ["x", "hg_w_in", "hg_lb", "hg_norm_g", "hg_w_out", "da_w_in", "da_lam", "da_norm_g", "da_w_out",
        "ffn_w_gate", "ffn_w_up", "ffn_w_down", "moe_w_router", "moe_w_gate", "moe_w_up", "moe_w_down",
        "ln_g", "ln_b", "p_2", "mix_norm_2", "conv_w_pw1_2", "conv_b_pw1_2", "conv_w_dw_2", "conv_b_dw_2",
        "conv_ln_g_2", "conv_ln_b_2", "conv_w_pw2_2", "conv_b_pw2_2", "kv_norm_2", "w_kvf_2", "b_f_2",
        "attn_w_q_2", "attn_w_o_2", "ffn_norm_2", "ffn_w1_2", "ffn_w2_2", "ple_norm_2", "ple_w_gate_2",
        "ple_w_proj_2", "final_norm_2"]


def declare(nc, inputs):
    arrays, t = {}, {}
    consts, hg_tables = constant_table()
    given = {n: inputs[n] for n in USED} | {"consts": consts, "hg_tables": hg_tables, "headrow": head_rows()}
    for name, a in given.items():
        a = np.ascontiguousarray(a)
        arrays[f"in_{name}"] = a
        t[name] = nc.dram_tensor(f"in_{name}", a.shape, mybir.dt.from_np(a.dtype), kind="ExternalInput").ap()
    t["out"] = nc.dram_tensor("out", (1, SEQ, D), F32, kind="ExternalOutput").ap()
    build(nc, t)
    return arrays


def kernel(**inputs):
    import concourse.bacc as _bacc
    from concourse.bass_utils import run_bass_kernel_spmd as _run

    nc = _bacc.Bacc("TRN2", target_bir_lowering=False, num_devices=1)
    arrays = declare(nc, inputs)
    return _run(nc, [arrays], core_ids=[0]).results[0]["out"]
```
